# Optimizing a Trainium2 kernel written in Bass

```python
import jax, jax.numpy as jnp
from jax import lax
import numpy as np
import math
import jax
import jax.numpy as jnp

D_MODEL = 2048
BATCH = 1
SEQ = 256
DEPTH = 2

CTX_LEN = 256
GRID_W = 64
D_MIX = D_MODEL
D_CONV = D_MIX // 2
D_RET = D_MIX - D_CONV
RET_HEADS = 8
RET_HEAD_DIM = D_RET // RET_HEADS
CONV_WIDTH = 3
CHUNK = 128
D_IN = 4 * D_CONV + 4 * D_RET
ROPE_BASE = 10000.0
RET_DECAY_OFFSET = 5.0
EPS = 1e-6


def _rmsnorm(x, w):
    xf = x.astype(jnp.float32)
    y = xf * lax.rsqrt(jnp.mean(xf * xf, axis=-1, keepdims=True) + EPS)
    return (y * w.astype(jnp.float32)).astype(x.dtype)

def _split_in(u):
    idx = [D_CONV, 2 * D_CONV, 3 * D_CONV, 4 * D_CONV,
           4 * D_CONV + D_RET, 4 * D_CONV + 2 * D_RET, 4 * D_CONV + 3 * D_RET]
    return jnp.split(u, idx, axis=-1)

def _short_conv(u, w):
    up = jnp.pad(u, ((0, 0), (1, 1), (0, 0)))
    return up[:, :-2] * w[0] + up[:, 1:-1] * w[1] + up[:, 2:] * w[2]

def _conv_branch(h, b, c, z, conv_w, norm_w):
    y = b * _short_conv(c * h, conv_w)
    return jax.nn.silu(z) * _rmsnorm(y, norm_w)

def _heads(t):
    b, l, _ = t.shape
    return t.reshape(b, l, RET_HEADS, RET_HEAD_DIM).transpose(0, 2, 1, 3)

def _rope_1d(x, pos):
    f = x.shape[-1] // 2
    inv = ROPE_BASE ** (-jnp.arange(f, dtype=jnp.float32) / f)
    ang = pos.astype(jnp.float32)[:, None] * inv[None, :]
    cos, sin = jnp.cos(ang), jnp.sin(ang)
    x1, x2 = x[..., :f], x[..., f:]
    return jnp.concatenate([x1 * cos - x2 * sin, x1 * sin + x2 * cos], axis=-1).astype(x.dtype)

def _axial_rope(x, row_pos, col_pos):
    half = x.shape[-1] // 2
    return jnp.concatenate([_rope_1d(x[..., :half], row_pos),
                            _rope_1d(x[..., half:], col_pos)], axis=-1)

def _chunk_retention(q, k, v, lg, s0):
    b, h, l, dk = q.shape
    n = l // CHUNK
    qc = q.reshape(b, h, n, CHUNK, dk)
    kc = k.reshape(b, h, n, CHUNK, dk)
    vc = v.reshape(b, h, n, CHUNK, v.shape[-1])
    pos = jnp.arange(CHUNK, dtype=jnp.float32)
    diff = pos[:, None] - pos[None, :]
    dmask = jnp.where(diff >= 0, jnp.exp(lg[:, None, None] * jnp.maximum(diff, 0.0)[None]), 0.0)
    scores = jnp.einsum('bhnid,bhnjd->bhnij', qc, kc) * dmask[None, :, None]
    intra = jnp.einsum('bhnij,bhnje->bhnie', scores, vc)
    k_decay = jnp.exp(lg[:, None] * (CHUNK - 1 - pos)[None])
    q_decay = jnp.exp(lg[:, None] * (pos + 1.0)[None])
    chunk_decay = jnp.exp(lg * CHUNK)
    chunk_kv = jnp.einsum('bhnjd,hj,bhnje->nbhde', kc, k_decay, vc)

    def step(s, kv):
        return chunk_decay[None, :, None, None] * s + kv, s

    _, s_prev = lax.scan(step, s0, chunk_kv)
    inter = jnp.einsum('bhnid,hi,nbhde->bhnie', qc, q_decay, s_prev)
    return (intra + inter).reshape(b, h, l, -1)

def _bidir_retention(q, k, v, lg_f, lg_b, s0_f, s0_b):
    o_f = _chunk_retention(q, k, v, lg_f, s0_f)
    flip = lambda t: jnp.flip(t, axis=2)
    o_b = _chunk_retention(flip(q), flip(k), flip(v), lg_b, s0_b)
    return o_f + flip(o_b)

def _context_states(k, v, lg_f, lg_b):
    lc = k.shape[2]
    t = jnp.arange(lc, dtype=jnp.float32)
    w_f = jnp.exp(lg_f[:, None] * (lc - 1.0 - t)[None])
    w_b = jnp.exp(lg_b[:, None] * t[None])
    s_f = jnp.einsum('bhtd,ht,bhte->bhde', k, w_f, v)
    s_b = jnp.einsum('bhtd,ht,bhte->bhde', k, w_b, v)
    return s_f, s_b

def _ret_out(o, z, gn_w):
    of = o.astype(jnp.float32)
    mu = jnp.mean(of, axis=-1, keepdims=True)
    var = jnp.mean(jnp.square(of - mu), axis=-1, keepdims=True)
    on = (of - mu) * lax.rsqrt(var + EPS)
    b, h, l, d = on.shape
    on = on.transpose(0, 2, 1, 3).reshape(b, l, h * d) * gn_w.astype(jnp.float32)
    return jax.nn.silu(z) * on.astype(z.dtype)

def _layer(x, ctx, c, c_ctx, norm_w, w_mod, b_mod, w_in, conv_w, conv_norm_w, ret_norm_w,
           decay_f, decay_b, w_out, row_pos, col_pos, update_ctx):
    d = D_MODEL
    lg_f = -jnp.exp(decay_f.astype(jnp.float32))
    lg_b = -jnp.exp(decay_b.astype(jnp.float32))
    k_scale = RET_HEAD_DIM ** -0.5

    shift, scale, gate = jnp.split(jax.nn.silu(c) @ w_mod + b_mod, 3, axis=-1)
    hx = _rmsnorm(x, norm_w) * (1 + scale[:, None]) + shift[:, None]
    a_h, a_b, a_c, a_z, q, k, v, r_z = _split_in(hx @ w_in)

    n_mod = 3 if update_ctx else 2
    mod_c = jax.nn.silu(c_ctx) @ w_mod[:, :n_mod * d] + b_mod[:n_mod * d]
    hc = _rmsnorm(ctx, norm_w) * (1 + mod_c[d:2 * d]) + mod_c[:d]
    if update_ctx:
        ca_h, ca_b, ca_c, ca_z, cq, ck, cv, cr_z = _split_in(hc @ w_in)
    else:
        kv0 = 4 * D_CONV + D_RET
        ck, cv = jnp.split(hc @ w_in[:, kv0:kv0 + 2 * D_RET], 2, axis=-1)
    ck_h = _heads(ck) * k_scale
    cv_h = _heads(cv)
    s_f, s_b = _context_states(ck_h, cv_h, lg_f, lg_b)

    q_h = _axial_rope(_heads(q), row_pos, col_pos)
    k_h = _axial_rope(_heads(k), row_pos, col_pos) * k_scale
    o = _bidir_retention(q_h, k_h, _heads(v), lg_f, lg_b, s_f, s_b)
    y_ret = _ret_out(o, r_z, ret_norm_w)
    y_conv = _conv_branch(a_h, a_b, a_c, a_z, conv_w, conv_norm_w)
    x = x + gate[:, None] * (jnp.concatenate([y_conv, y_ret], axis=-1) @ w_out)

    if update_ctx:
        zeros = jnp.zeros_like(s_f)
        oc = _bidir_retention(_heads(cq), ck_h, cv_h, lg_f, lg_b, zeros, zeros)
        yc_ret = _ret_out(oc, cr_z, ret_norm_w)
        yc_conv = _conv_branch(ca_h, ca_b, ca_c, ca_z, conv_w, conv_norm_w)
        ctx = ctx + mod_c[2 * d:] * (jnp.concatenate([yc_conv, yc_ret], axis=-1) @ w_out)
    return x, ctx

def first_inputs(seed: int = 0) -> dict:
    key = jax.random.key(seed)
    ks = jax.random.split(key, 16)
    f32 = jnp.float32
    nrm = lambda k, s: jax.random.normal(k, s, f32)
    base = jnp.log(-jnp.log1p(-(2.0 ** -(RET_DECAY_OFFSET + jnp.arange(RET_HEADS, dtype=f32)))))
    return {
        "x": nrm(ks[0], (BATCH, SEQ, D_MODEL)),
        "c": nrm(ks[1], (BATCH, D_MODEL)),
        "ctx": nrm(ks[2], (BATCH, CTX_LEN, D_MODEL)),
        "c_ctx": nrm(ks[3], (D_MODEL,)),
        "norm_w": 1.0 + 0.05 * nrm(ks[4], (DEPTH, D_MODEL)),
        "w_mod": nrm(ks[5], (DEPTH, D_MODEL, 3 * D_MODEL)) * (0.5 * D_MODEL ** -0.5),
        "b_mod": 0.02 * nrm(ks[6], (DEPTH, 3 * D_MODEL)),
        "w_in": nrm(ks[7], (DEPTH, D_MODEL, D_IN)) * D_MODEL ** -0.5,
        "conv_w": nrm(ks[8], (DEPTH, CONV_WIDTH, D_CONV)) * CONV_WIDTH ** -0.5,
        "conv_norm_w": 1.0 + 0.05 * nrm(ks[9], (DEPTH, D_CONV)),
        "ret_norm_w": 1.0 + 0.05 * nrm(ks[10], (DEPTH, D_RET)),
        "ret_decay_f": base[None] + 0.05 * nrm(ks[11], (DEPTH, RET_HEADS)),
        "ret_decay_b": base[None] + 0.05 * nrm(ks[12], (DEPTH, RET_HEADS)),
        "w_out": nrm(ks[13], (DEPTH, D_MIX, D_MODEL)) * D_MIX ** -0.5,
        "final_norm_w": 1.0 + 0.05 * nrm(ks[14], (D_MODEL,)),
    }

def first_block(x, c, ctx, c_ctx, norm_w, w_mod, b_mod, w_in, conv_w, conv_norm_w, ret_norm_w,
              ret_decay_f, ret_decay_b, w_out, final_norm_w):
    seq = x.shape[1]
    rows = seq // GRID_W
    row_pos = jnp.repeat(jnp.arange(rows), GRID_W)
    col_pos = jnp.tile(jnp.arange(GRID_W), rows)
    for layer in range(DEPTH):
        x, ctx = _layer(x, ctx, c, c_ctx, norm_w[layer], w_mod[layer], b_mod[layer], w_in[layer],
                        conv_w[layer], conv_norm_w[layer], ret_norm_w[layer],
                        ret_decay_f[layer], ret_decay_b[layer], w_out[layer],
                        row_pos, col_pos, layer < DEPTH - 1)
    return _rmsnorm(x, final_norm_w)


DEPTH_2 = 1

HEAD_DIM = 128
MIX_WIDTH = D_MODEL
N_HEADS_TOTAL = MIX_WIDTH // HEAD_DIM
N_HEADS_SB = N_HEADS_TOTAL // 2
N_HEADS_DIL = N_HEADS_TOTAL - N_HEADS_SB
SB_WIDTH = N_HEADS_SB * HEAD_DIM
DIL_WIDTH = N_HEADS_DIL * HEAD_DIM
IN_WIDTH = 3 * (SB_WIDTH + DIL_WIDTH)
IN_SPLITS = (SB_WIDTH, 2 * SB_WIDTH, 3 * SB_WIDTH, 3 * SB_WIDTH + DIL_WIDTH, 3 * SB_WIDTH + 2 * DIL_WIDTH)
D_FF = -(-8 * D_MODEL // (3 * 256)) * 256
PLI_DIM = 256
BLOCK = 128
DIL_GROUPS = ((128, 1), (512, 4), (2048, 16))
NUM_BUCKETS = 32
MAX_DISTANCE = 2048
RMS_EPS = 1e-6


def rms_norm(x, gain):
    xf = x.astype(jnp.float32)
    y = xf * lax.rsqrt(jnp.mean(xf * xf, axis=-1, keepdims=True) + RMS_EPS)
    return (y * gain.astype(jnp.float32)).astype(x.dtype)

def t5_bucket(dist):
    max_exact = NUM_BUCKETS // 2
    d = jnp.maximum(dist, 1).astype(jnp.float32)
    large = max_exact + (jnp.log(d / max_exact) / math.log(MAX_DISTANCE / max_exact)
                         * (NUM_BUCKETS - max_exact)).astype(jnp.int32)
    large = jnp.minimum(large, NUM_BUCKETS - 1)
    return jnp.where(dist < max_exact, dist, large)

def stick_breaking_attention(q, k, v):
    b, s, h, e = q.shape
    nblk = s // BLOCK
    scale = 1.0 / math.sqrt(e)
    kt = k.transpose(0, 2, 1, 3)
    vt = v.transpose(0, 2, 1, 3).astype(jnp.float32)
    qb = q.reshape(b, nblk, BLOCK, h, e).transpose(1, 0, 3, 2, 4)
    starts = jnp.arange(nblk, dtype=jnp.int32) * BLOCK
    key_pos = jnp.arange(s, dtype=jnp.int32)

    def one_block(args):
        qi, t0 = args
        z = jnp.einsum('bhqe,bhke->bhqk', qi, kt).astype(jnp.float32) * scale
        q_pos = t0 + jnp.arange(BLOCK, dtype=jnp.int32)
        earlier = key_pos[None, :] < q_pos[:, None]
        log_keep = jnp.where(earlier, jax.nn.log_sigmoid(-z), 0.0)
        later = lax.cumsum(log_keep, axis=3, reverse=True) - log_keep
        a = jnp.where(earlier, jnp.exp(jax.nn.log_sigmoid(z) + later), 0.0)
        return jnp.einsum('bhqk,bhke->bhqe', a, vt)

    o = lax.map(one_block, (qb, starts))
    return o.transpose(1, 0, 3, 2, 4).reshape(b, s, h, e).astype(q.dtype)

def dilated_branch(q, k, v, rel_bias, window, dilation):
    b, s, h, e = q.shape
    span = dilation * BLOCK
    s_pad = -(-s // span) * span
    nb = s_pad // span
    n_back = window // dilation
    scale = 1.0 / math.sqrt(e)

    def to_sub(t):
        t = jnp.pad(t, ((0, 0), (0, s_pad - s), (0, 0), (0, 0)))
        return t.reshape(b, nb, BLOCK, dilation, h, e).transpose(0, 3, 4, 1, 2, 5)

    def with_prev(t):
        prev = jnp.pad(t[:, :, :, :-1], ((0, 0), (0, 0), (0, 0), (1, 0), (0, 0), (0, 0)))
        return jnp.concatenate([prev, t], axis=4)

    qs = to_sub(q)
    kk = with_prev(to_sub(k))
    vv = with_prev(to_sub(v)).astype(jnp.float32)
    logits = jnp.einsum('brhnqe,brhnke->brhnqk', qs, kk).astype(jnp.float32) * scale

    qi = jnp.arange(BLOCK, dtype=jnp.int32)[:, None]
    ki = jnp.arange(2 * BLOCK, dtype=jnp.int32)[None, :]
    rel = BLOCK + qi - ki
    band = (rel >= 0) & (rel <= n_back)
    bias = rel_bias.astype(jnp.float32)[t5_bucket(jnp.maximum(rel, 0) * dilation)]
    bias = bias.transpose(2, 0, 1)[:, None]
    has_prev = (jnp.arange(nb)[:, None, None] > 0) | (ki[None] >= BLOCK)
    valid = band[None] & has_prev

    logits = jnp.where(valid, logits + bias, -jnp.inf)
    m = jnp.max(logits, axis=-1, keepdims=True)
    p = jnp.exp(logits - m)
    denom = jnp.sum(p, axis=-1, keepdims=True)
    o = jnp.einsum('brhnqk,brhnke->brhnqe', p, vv) / denom
    lse = m + jnp.log(denom)

    def from_sub(t):
        return t.transpose(0, 3, 4, 1, 2, 5).reshape(b, s_pad, h, t.shape[-1])[:, :s]

    return from_sub(o), from_sub(lse)[..., 0]

def dilated_mixture(q, k, v, rel_bias):
    outs, lses = [], []
    for window, dilation in DIL_GROUPS:
        o, l = dilated_branch(q, k, v, rel_bias, window, dilation)
        outs.append(o)
        lses.append(l)
    w = jax.nn.softmax(jnp.stack(lses, axis=0), axis=0)
    o = jnp.sum(w[..., None] * jnp.stack(outs, axis=0), axis=0)
    return o.astype(q.dtype)

def second_inputs(seed: int = 0) -> dict:
    key = jax.random.key(seed)
    ks = jax.random.split(key, 15)

    def normal(k, shape, scale):
        return jax.random.normal(k, shape, jnp.float32) * scale

    def gain(k, shape):
        return 1.0 + normal(k, shape, 0.01)

    return {
        "x": normal(ks[0], (BATCH, SEQ, D_MODEL), 1.0),
        "p": normal(ks[1], (DEPTH_2, BATCH, SEQ, PLI_DIM), 1.0),
        "ln_mix_pre": gain(ks[2], (DEPTH_2, D_MODEL)),
        "w_in": normal(ks[3], (DEPTH_2, D_MODEL, IN_WIDTH), D_MODEL ** -0.5),
        "ln_head": gain(ks[4], (DEPTH_2, MIX_WIDTH)),
        "w_out": normal(ks[5], (DEPTH_2, MIX_WIDTH, D_MODEL), MIX_WIDTH ** -0.5),
        "ln_mix_post": gain(ks[6], (DEPTH_2, D_MODEL)),
        "rel_bias": normal(ks[7], (NUM_BUCKETS, N_HEADS_DIL), 0.5),
        "ln_ffn_pre": gain(ks[8], (DEPTH_2, D_MODEL)),
        "w_gate_up": normal(ks[9], (DEPTH_2, D_MODEL, 2 * D_FF), D_MODEL ** -0.5),
        "w_down": normal(ks[10], (DEPTH_2, D_FF, D_MODEL), D_FF ** -0.5),
        "ln_ffn_post": gain(ks[11], (DEPTH_2, D_MODEL)),
        "ln_pli": gain(ks[12], (DEPTH_2, D_MODEL)),
        "w_pli_gate": normal(ks[13], (DEPTH_2, D_MODEL, D_MODEL), D_MODEL ** -0.5),
        "w_pli_proj": normal(ks[14], (DEPTH_2, PLI_DIM, D_MODEL), PLI_DIM ** -0.5),
    }

def second_block(x, p, ln_mix_pre, w_in, ln_head, w_out, ln_mix_post, rel_bias,
              ln_ffn_pre, w_gate_up, w_down, ln_ffn_post, ln_pli, w_pli_gate, w_pli_proj):
    b, s, _ = x.shape
    for i in range(DEPTH_2):
        h = rms_norm(x, ln_mix_pre[i])
        proj = h @ w_in[i]
        q_sb, k_sb, v_sb, q_dl, k_dl, v_dl = jnp.split(proj, list(IN_SPLITS), axis=-1)
        sb_shape = (b, s, N_HEADS_SB, HEAD_DIM)
        dl_shape = (b, s, N_HEADS_DIL, HEAD_DIM)
        o_sb = stick_breaking_attention(q_sb.reshape(sb_shape), k_sb.reshape(sb_shape), v_sb.reshape(sb_shape))
        o_dl = dilated_mixture(q_dl.reshape(dl_shape), k_dl.reshape(dl_shape), v_dl.reshape(dl_shape), rel_bias)
        o = jnp.concatenate([o_sb, o_dl], axis=2)
        o = rms_norm(o, ln_head[i].reshape(N_HEADS_TOTAL, HEAD_DIM)).reshape(b, s, MIX_WIDTH)
        x = x + rms_norm(o @ w_out[i], ln_mix_post[i])
        h = rms_norm(x, ln_ffn_pre[i])
        g, u = jnp.split(h @ w_gate_up[i], 2, axis=-1)
        f = (jax.nn.silu(g) * u) @ w_down[i]
        x = x + rms_norm(f, ln_ffn_post[i])
        gate = jax.nn.sigmoid(rms_norm(x, ln_pli[i]) @ w_pli_gate[i])
        x = x + gate * (p[i] @ w_pli_proj[i])
    return x


_first_inputs = second_inputs


def second_inputs(seed=0):
    import zlib

    import numpy as np

    out = dict(_first_inputs(seed))
    spreads = {}
    factors = {'ln_mix_pre': 4.869,
     'ln_head': 7.251,
     'ln_mix_post': 6.985,
     'ln_ffn_pre': 7.126,
     'ln_ffn_post': 8.0,
     'ln_pli': 8.0}
    for name, (base, spread) in spreads.items():
        noise = np.random.default_rng([zlib.crc32(name.encode()), seed]).standard_normal(out[name].shape)
        drawn = base * np.exp(spread * noise) if base else spread * noise
        out[name] = jnp.asarray(drawn.astype(out[name].dtype))
    for name, factor in factors.items():
        out[name] = (out[name] * factor).astype(out[name].dtype)
    return out


_narrow_inputs = second_inputs


def second_inputs(seed=0):

    out = dict(_narrow_inputs(seed))
    wider = {'ln_head': 5.19,
     'ln_mix_post': 5.03,
     'ln_ffn_pre': 6.04,
     'ln_ffn_post': 8.74,
     'ln_pli': 12.0}
    for name, times in wider.items():
        mean = out[name].mean()
        out[name] = (mean + times * (out[name] - mean)).astype(out[name].dtype)
    return out


def setup_inputs(seed=0):
    out = dict(first_inputs(seed))
    for name, value in second_inputs(seed + 1).items():
        if name != "x":
            out[name + "_2"] = value
    return out


def reference(
    x, c, ctx, c_ctx, norm_w, w_mod, b_mod, w_in, conv_w, conv_norm_w, ret_norm_w, ret_decay_f,
    ret_decay_b, w_out, final_norm_w, p_2, ln_mix_pre_2, w_in_2, ln_head_2, w_out_2,
    ln_mix_post_2, rel_bias_2, ln_ffn_pre_2, w_gate_up_2, w_down_2, ln_ffn_post_2, ln_pli_2,
    w_pli_gate_2, w_pli_proj_2,
):
    x = first_block(
        x, c, ctx, c_ctx, norm_w, w_mod, b_mod, w_in, conv_w, conv_norm_w, ret_norm_w,
        ret_decay_f, ret_decay_b, w_out, final_norm_w,
    )
    return second_block(
        x, p_2, ln_mix_pre_2, w_in_2, ln_head_2, w_out_2, ln_mix_post_2, rel_bias_2,
        ln_ffn_pre_2, w_gate_up_2, w_down_2, ln_ffn_post_2, ln_pli_2, w_pli_gate_2,
        w_pli_proj_2,
    )


_drawn_inputs = setup_inputs


def setup_inputs(seed=0):
    import zlib

    import numpy as np

    out = dict(_drawn_inputs(seed))
    spreads = {}
    factors = {}
    for name, (base, spread) in spreads.items():
        noise = np.random.default_rng([zlib.crc32(name.encode()), seed]).standard_normal(out[name].shape)
        drawn = base * np.exp(spread * noise) if base else spread * noise
        out[name] = jnp.asarray(drawn.astype(out[name].dtype))
    for name, factor in factors.items():
        out[name] = (out[name] * factor).astype(out[name].dtype)
    return out
```

```python
import numpy as np
import concourse.bass as bass
import concourse.mybir as mybir
from contextlib import ExitStack, contextmanager

P = 128
D = 2048
KT = D // P
TOK = 256
HALF = 1024
HEADS = 8
FF = 5632
FKT = FF // P
EPS = 1e-6
SLOTS = 4
LEAD = 3
PHASES = [
    ("mod0", 8, 8, 1024), ("in0_conv", 8, 8, 1024), ("in0_ret", 8, 8, 1024), ("modg0", 4, 8, 1024),
    ("out0", 4, 8, 1024), ("mod1", 8, 8, 1024), ("modg1", 4, 8, 1024), ("in1_conv", 8, 8, 1024),
    ("in1_ret", 8, 8, 1024), ("out1", 4, 8, 1024), ("sb", 8, 8, 768), ("dil", 8, 8, 768),
    ("out2", 4, 8, 1024), ("ffn_up", 22, 8, 1024), ("ffn_down", 4, 22, 1024), ("proj", 4, 1, 1024),
    ("gate", 4, 8, 1024),
]
BASE, SHAPE = {}, {}
_n = 0
for _name, _c, _per, _w in PHASES:
    BASE[_name], SHAPE[_name] = _n, (_c, _per, _w)
    _n += _c * _per
PIECES = _n
LINKS = {'pool_ret': 1, 'act_in0_conv': 0, 'act_in0_ret': 0, 'act_out0': 4, 'act_in1_conv': 0, 'act_in1_ret': 0, 'act_sb': 8, 'act_dil': 8, 'act_ffn_up': 0, 'act_gate': 0, 'dve_mod0': 0, 'dve_in0_conv': 4, 'dve_in0_ret': 6, 'dve_out0': 0, 'dve_mod1': 0, 'dve_in1_conv': 4, 'dve_in1_ret': 6, 'dve_sb': 8, 'dve_dil': 10, 'dve_ffn_up': 0, 'dve_gate': 2, 'pe_mod0': 0, 'pe_in0_conv': 0, 'pe_in0_ret': 0, 'pe_out0': 0, 'pe_mod1': 0, 'pe_in1_conv': 0, 'pe_in1_ret': 0, 'pe_sb': 0, 'pe_dil': 0, 'pe_ffn_up': 0, 'pe_gate': 0}
COLS, _n = {}, 0
for _name, _w in [("norm0", 16), ("norm1", 16), ("bmod0", 32), ("bmod1", 32), ("convw0", 24),
                  ("convw1", 24), ("convn0", 8), ("convn1", 8), ("retn0", 8), ("retn1", 8),
                  ("mixpre", 16), ("head", 16), ("ffnpre", 16), ("pli", 16), ("c", 16),
                  ("cctx", 16), ("eps", 1)]:
    COLS[_name] = _n
    _n += _w
NCOLS = _n
MATS = ["ident", "ones"]
ATTN_MATS = ["later", "flip"]
WIDE = ["cos", "sin", "dpos", "dneg", "dscale", "dctxf", "dctxb"]


def shape_constants():
    i = np.arange(P)
    mats = {
        "ident": np.eye(P), "later": i[:, None] > i[None, :], "ones": np.ones((P, P)),
        "flip": i[:, None] + i[None, :] == P - 1,
    }
    f = 32
    inv = (np.float32(10000.0) ** (-np.arange(f, dtype=np.float32) / np.float32(f))).astype(np.float32)
    pos = np.arange(TOK)
    ang = np.stack([(pos // 64), (pos % 64)], 1).astype(np.float32)[:, :, None] * inv
    cos = np.cos(ang.astype(np.float32)).astype(np.float32)
    sin = np.sin(ang.astype(np.float32)).astype(np.float32)
    cos = np.stack([cos, cos], 2).reshape(TOK, 128)
    sin = np.stack([-sin, sin], 2).reshape(TOK, 128)
    rows = lambda a: np.concatenate([a, a], 1).reshape(2, P, 256).transpose(1, 0, 2).reshape(P, 512)
    key = (np.arange(2)[None, :, None] * P + i[:, None, None])
    q = np.arange(TOK)[None, None, :]
    d = q - key
    wide = {
        "cos": rows(cos), "sin": rows(sin), "dpos": np.maximum(d, 0), "dneg": np.maximum(-d, 0),
        "dscale": (1 + (d == 0)) * np.float32(P ** -0.5), "dctxf": q + TOK - key, "dctxb": TOK - q + key,
    }
    earlier = (key < q).astype(np.float32)
    n = np.arange(384)
    dist = 255 - n
    dd = np.maximum(dist, 0)
    big = 16 + (np.log(np.maximum(dd, 1).astype(np.float32) / np.float32(16)) / np.float32(np.log(128.0))
                * np.float32(16)).astype(np.int32)
    bucket = np.where(dd < 16, dd, np.minimum(big, 31))
    onehot = (np.arange(32)[:, None] == bucket[None, :]) & (dist >= 0)[None, :]
    times = (dist <= 128).astype(int) + (dist % 4 == 0) + (dist % 16 == 0)
    times = np.where(dist >= 0, times, 0)
    add = np.where(times > 0, np.log(np.maximum(times, 1)), -1e30)
    f32 = lambda a: np.ascontiguousarray(a, np.float32)
    return (f32(np.concatenate([mats[m] for m in MATS], 1)),
            f32(np.concatenate([wide[m].reshape(P, 512) for m in WIDE], 1)),
            f32(np.concatenate([-earlier.reshape(P, 512), earlier.reshape(P, 512)] + [mats[m] for m in ATTN_MATS], 1)),
            f32(onehot), f32(np.repeat(add[None], HEADS, 0)))


class Chain:

    def __init__(self, eng, sem):
        self.eng, self.sem, self.total, self.n, self.at = eng, sem, 0, 0, 0

    def link(self, ins):
        self.n += 1
        ins.then_inc(self.sem, 1)
        self.eng.wait_ge(self.sem, self.at + self.total + self.n)

    @contextmanager
    def turn(self, name, i, turns):
        self.total, self.n = self.total + self.n, 0
        self.at = i * LINKS.get(name, 1)
        yield
        if self.n != LINKS.get(name, 1):
            raise ValueError(f"LINKS {name} {self.n}")
        self.at, self.n, self.total = 0, 0, self.total + turns * LINKS.get(name, 1)


def over_chunks(eng, chain, key, chunks, paired, body):
    if not paired:
        with eng.Fori(0, chunks - 1) as i, chain.turn(key, i, chunks - 1):
            body(i + 1, 1)
        return
    pairs = (chunks - 2) // 2
    if pairs > 1:
        with eng.Fori(0, pairs) as i, chain.turn(key, i, pairs):
            body(2 * i + 1, 1)
            body(2 * i + 2, 0)
    else:
        body(1, 1)
        body(2, 0)
    body(chunks - 1, 1)


def build(nc, a, out):
    F32, F32R = mybir.dt.float32, mybir.dt.float32r
    ALU, ACT, AX = mybir.AluOpType, mybir.ActivationFunctionType, mybir.AxisListType
    ds = bass.ds
    top = ExitStack()
    sb = lambda scope, n, shape, dt=F32: scope.enter_context(nc.sbuf_tensor(n, shape, dt))
    scratch = nc.dram_tensor("bias_by_distance", [HEADS, 384], F32, kind="Internal").ap()

    with top:
        X = sb(top, "X", [P, 4 * D])
        raw = sb(top, "raw", [P, SLOTS, 1024])
        w_hi = sb(top, "w_hi", [P, SLOTS, 1024], F32R)
        w_lo = sb(top, "w_lo", [P, SLOTS, 1024], F32R)
        mats = sb(top, "mats", [P, len(MATS) * P])
        cols = sb(top, "cols", [P, NCOLS])
        ssq = sb(top, "ssq", [P, 4, 4])
        rstd = sb(top, "rstd", [P, 4])
        rstd_root = sb(top, "rstd_root", [P, 4])
        scale_h = sb(top, "scale_h", [P, 4])
        layer = ExitStack()
        act_hi = sb(layer, "act_hi", [P, KT * 512], F32R)
        act_lo = sb(layer, "act_lo", [P, KT * 512], F32R)
        gates = sb(layer, "gates", [P, 2, D])
        wide = sb(layer, "wide", [P, len(WIDE) * 512])
        lg = sb(layer, "lg", [P, 32])
        cvec = sb(layer, "cvec", [P, 2 * KT + P])
        c_hi = sb(layer, "c_hi", [P, 2 * KT + P], F32R)
        c_lo = sb(layer, "c_lo", [P, 2 * KT + P], F32R)
        modT = sb(layer, "modT", [P, 2, 32])
        mod_a = sb(layer, "mod_a", [P, 2, KT])
        u = sb(layer, "u", [P, 4, 512])
        qk = sb(layer, "qk", [P, 2, 256])
        qT = sb(layer, "qT", [P, 512])
        kT = sb(layer, "kT", [P, 512])
        sT = sb(layer, "sT", [P, 4, 256])
        rot = sT[:, 2:4, :]
        sTc = qk
        g = sT[:, :, :].rearrange("p b q -> p (b q)")[:, 0:516].rearrange("p (b n) -> p b n", b=2)
        zr = sb(layer, "zr", [P, 4, 128])
        decay = sb(layer, "decay", [P, 4, 256])
        dtmp = sb(layer, "dtmp", [P, 512])
        acc = decay[:, 0:2, :].rearrange("p b q -> p (b q)")
        stats = sb(layer, "stats", [P, 4, 6])
        mv = sb(layer, "mv", [P, 4, 2])
        root = sb(layer, "root", [P, 4])
        msb = sb(layer, "msb", [P, 512])
        layer.close()
        block2 = ExitStack()
        h_hi = sb(block2, "h_hi", [P, KT * 256], F32R)
        h_lo = sb(block2, "h_lo", [P, KT * 256], F32R)
        xs2 = sb(block2, "xs2", [P, 2, 512])
        attn = ExitStack()
        maskd = sb(attn, "maskd", [P, 2 * 512 + len(ATTN_MATS) * P])
        bias = sb(attn, "bias", [P, HEADS, 256])
        hankel = sb(attn, "hankel", [P, HEADS, 256])
        onehot = sb(attn, "onehot", [32, 384])
        relb = sb(attn, "relb", [32, HEADS])
        dadd = sb(attn, "dadd", [HEADS, 384])
        ext = sb(attn, "ext", [HEADS, 384])
        mixrow = sb(attn, "mixrow", [P, D])
        u2 = sb(attn, "u2", [P, 2, 384])
        qkT = sb(attn, "qkT", [P, 512])
        t1 = sb(attn, "t1", [P, 512])
        t2 = sb(attn, "t2", [P, 512])
        t3 = sb(attn, "t3", [P, 512])
        t4 = sb(attn, "t4", [P, 512])
        aT = sb(attn, "aT", [P, 512])
        on = sb(attn, "on", [P, 2, 128])
        rsum = sb(attn, "rsum", [P, 2])
        hsq = sb(attn, "hsq", [P, 2])
        hroot = sb(attn, "hroot", [P, 2])
        hr = sb(attn, "hr", [P, 2])
        rmax = sb(attn, "rmax", [P, 2])
        attn.close()
        ffn = ExitStack()
        f_hi = sb(ffn, "f_hi", [P, FKT * 256], F32R)
        f_lo = sb(ffn, "f_lo", [P, FKT * 256], F32R)
        ffn.close()
        pli = ExitStack()
        sig = sb(pli, "sig", [P, 2, 512])
        pli.close()
        block2.close()
        late = ExitStack()
        frow = sb(late, "frow", [P, D])
        ptok = sb(late, "ptok", [P, 2 * 256])
        p_hi = sb(late, "p_hi", [P, 2 * 256], F32R)
        p_lo = sb(late, "p_lo", [P, 2 * 256], F32R)
        late.close()
        fs = xs2[:, 0, :].rearrange("p (t n) -> p t n", t=2)
        ff = xs2[:, 1, :].rearrange("p (t n) -> p t n", t=2)

        main = [top.enter_context(nc.psum_tensor(f"main{i}", [P, 512], F32)) for i in range(4)]
        aux = [top.enter_context(nc.psum_tensor(f"aux{i}", [P, 512], F32)) for i in range(4)]

        S = {}

        def sem(name):
            if name not in S:
                S[name] = top.enter_context(nc.semaphore(name))
            return S[name]

        raw_in = [sem(f"raw_in{i}") for i in range(SLOTS)]
        hi_split, lo_split = sem("hi_split"), sem("lo_split")
        eaten = sem("eaten")
        free_a, free_d = sem("free_a"), sem("free_d")
        for n in ("loads_c loads_p act_chain dve_chain pool_chain consts lgx lgd cx csplit md_e md_T md_d mg_e "
                  "mg_s mg_d norm_sum norm_root norm_rstd xs_ready xT_ready h_hi_ready h_ready loads_x "
                  "cv_T cv_z cv_y cv_q cv_done cf_s cf_q cf_r y_scaled p_hi_ready p_lo_ready "
                  "rt_dz rt_e rt_ec stats_done msb_read act_pause dve_pause rt_D rt_rope rt_z rt_T rt_qa rt_kd rt_s rt_sT rt_o rt_v rt_sq rt_n rt_yT rt_y "
                  "out_x x_in gate_row fin_x1 fin_sq bT bT2 bT3 bT4 bT5 mix_in fr_in pt_in p_ready px_h "
                  "a_T a_qk a_z s_l s_lk s_lat s_s s_e a_aT a_o a_sq a_n a_yT a_y d_L d_p d_pT d_r "
                  "r_copy res_x f_g f_T f_hi f_lo pj_out gt_sig gt_x stored ssq0 out_sq").split():
            sem(n)
        s = S

        mat = lambda n: mats[:, MATS.index(n) * P:(MATS.index(n) + 1) * P]
        amat = lambda n: maskd[:, 1024 + ATTN_MATS.index(n) * P:1024 + (ATTN_MATS.index(n) + 1) * P]
        wd = lambda n: wide[:, WIDE.index(n) * 512:(WIDE.index(n) + 1) * 512]
        wd3 = lambda n: wd(n).rearrange("p (b q) -> p b q", b=2)
        col = lambda n, j=0: cols[:, ds(COLS[n] + j, 1)]
        colv = lambda n, w: cols[:, COLS[n]:COLS[n] + w]
        x3 = X[:, :].rearrange("p (t d) -> p t d", t=4)
        rr = X[:, 2 * D:4 * D].rearrange("p (t d) -> p t d", t=2)
        y_of = [X[:, :].rearrange("p (k n) -> p k n", n=512),
                X[:, 2 * D:4 * D].rearrange("p (k n) -> p k n", n=256)]
        tokens = [4, 2]

        by_act = {"in0_conv", "in0_ret", "in1_conv", "in1_ret", "sb", "dil", "out2", "ffn_up", "ffn_down", "gate"}
        done_a, done_d, na, nd = {}, {}, 1, 1
        for name, c, per, w in PHASES:
            done_a[name], done_d[name] = na, nd
            if name != "proj":
                nd += c
                na += c if name in by_act else 0
        paired = {n: n not in ("in0_conv", "in0_ret", "in1_conv", "in1_ret", "out0") for n, *_ in PHASES}

        def chunk_end(name, c):
            return BASE[name] + (c + 1) * SHAPE[name][1]

        def squares(W):
            return qk[:].rearrange("p t n -> p (t n)")[:, 0:W]

        def act_hi_scratch():
            return act_hi[:, 0:D]

        def prep_index(n):
            return {0: 0, 1: 1, 3: 2, 5: 3, 7: 4}[n]

        def norm_groups(k):
            return {0: (0, 1), 2: (2,), 4: (3,)}.get(k, ())

        def norm_bank(T, kg, kk):
            if T == 4:
                return aux[kk], 0
            return aux[2 * (kg % 2) + kk // 2], 256 * (kk % 2)

        block = top.enter_context(nc.Block())

        @block.sync
        def _(sp):
            for name, chunks, per, w in PHASES:
                def fetch(group, slot):
                    n = BASE[name] // SLOTS + group
                    if not (isinstance(n, int) and n == 0):
                        sp.wait_ge(lo_split, SLOTS * n + slot - SLOTS + 1)
                    sp.dma_start(raw[:, slot, 0:w], a["w_" + name][SLOTS * group + slot, :, :]).then_inc(raw_in[slot], 16)

                groups = chunks * per // SLOTS
                for slot in range(SLOTS):
                    fetch(0, slot)
                if groups > 1:
                    with sp.Fori(1, groups) as i:
                        for slot in range(SLOTS):
                            fetch(i, slot)

        @block.gpsimd
        def _(pool):
            ch = Chain(pool, s["pool_chain"])
            pool.dma_start(cols[:], a["cols"]).then_inc(s["loads_c"], 16)
            pool.dma_start(mats[:], a["mats"]).then_inc(s["loads_c"], 16)
            pool.dma_start(x3[:, 0:2, :], a["x"].rearrange("(t p) d -> p t d", p=P)).then_inc(s["loads_x"], 16)
            pool.dma_start(x3[:, 2:4, :], a["ctx"].rearrange("(t p) d -> p t d", p=P)).then_inc(s["loads_x"], 16)
            pool.dma_start(wide[:], a["wide"]).then_inc(s["loads_p"], 16)
            pool.dma_start(lg[:], a["decays"].partition_broadcast(P)).then_inc(s["loads_p"], 16)
            for b in range(2):
                pool.dma_start(gates[:, b, :], a["gate_bias"][0, :].partition_broadcast(P)).then_inc(s["gate_row"], 16)
            for L in range(2):
                T = tokens[L]
                W = T * P
                Y = y_of[L]
                if L == 1:
                    pool.wait_ge(s["rt_y"], 9)
                ch.link(nc.gpsimd.memset(g[:, :, 0:1], 0.0))
                ch.link(nc.gpsimd.memset(g[:, :, 257:258], 0.0))
                nc.gpsimd.memset(acc[:], 0.0).then_inc(s["cv_q"], 1)
                pool.wait_ge(s["cv_q"], 9 * L + 1)
                with pool.Fori(0, 8) as e, ch.turn("pool_conv", e, 8):
                    pool.wait_ge(s["cv_y"], 8 * L + e + 1)
                    ch.link(nc.gpsimd.tensor_tensor(out=squares(W), in0=kT[:, 0:W], in1=kT[:, 0:W], op=ALU.mult))
                    nc.gpsimd.tensor_tensor(out=acc[:, 0:W], in0=acc[:, 0:W], in1=squares(W), op=ALU.add).then_inc(s["cv_q"], 1)
                    pool.wait_ge(s["cv_q"], 9 * L + e + 2)
                pool.wait_ge(s["cf_r"], L + 1)
                for j in range(8):
                    nc.gpsimd.tensor_tensor(out=Y[:, j, :], in0=Y[:, j, :], in1=msb[:, 0:W], op=ALU.mult).then_inc(s["y_scaled"], 1)
                if L == 0:
                    pool.wait_ge(s["loads_p"], 32)
                with pool.Fori(0, 8) as e, ch.turn("pool_ret", e, 8):
                    dflat = decay[:].rearrange("p b q -> p (b q)")
                    pool.wait_ge(s["rt_e"], 8 * L + e + 1)
                    nc.gpsimd.tensor_tensor(out=dflat[:, 512:1024], in0=dflat[:, 512:1024], in1=dtmp[:], op=ALU.mult).then_inc(s["rt_dz"], 1)
                    pool.wait_ge(s["rt_dz"], 8 * L + e + 1)
                    ch.link(nc.gpsimd.tensor_tensor(out=dflat[:, 512:1024], in0=dflat[:, 512:1024], in1=wd("dscale"), op=ALU.mult))
                    pool.wait_ge(s["rt_ec"], 8 * L + e + 1)
                    nc.gpsimd.tensor_tensor(out=dflat[:, 0:512], in0=dflat[:, 0:512], in1=dtmp[:], op=ALU.add).then_inc(s["rt_D"], 1)
                    pool.wait_ge(s["rt_D"], 8 * L + e + 1)
                if L == 0:
                    pool.wait_ge(s["p_lo_ready"], 8)
                    pool.wait_ge(s["p_hi_ready"], 8)
                    pool.dma_start(x3[:, 0:2, :], a["x"].rearrange("(t p) d -> p t d", p=P)).then_inc(s["x_in"], 16)
                    pool.dma_start(x3[:, 2:4, :], a["ctx"].rearrange("(t p) d -> p t d", p=P)).then_inc(s["x_in"], 16)
                    pool.wait_ge(s["out_x"], 4)
                    pool.dma_start(gates[:, 0, :], a["gate_bias"][1, :].partition_broadcast(P)).then_inc(s["gate_row"], 16)
                    pool.dma_start(gates[:, 1, :], a["rows"][0, :].partition_broadcast(P)).then_inc(s["gate_row"], 16)
            pool.wait_ge(s["fin_x1"], 1)
            pool.wait_ge(s["eaten"], chunk_end("out1", 3))
            pool.dma_start(maskd[:], a["maskd"]).then_inc(s["bT"], 16)
            pool.dma_start(onehot[:], a["onehot"]).then_inc(s["bT"], 16)
            pool.dma_start(relb[:], a["rel_bias"]).then_inc(s["bT"], 16)
            pool.dma_start(dadd[:], a["dadd"]).then_inc(s["bT"], 16)
            pool.dma_start(mixrow[:], a["rows"][1, :].partition_broadcast(P)).then_inc(s["mix_in"], 16)
            pool.wait_ge(s["bT3"], 1)
            pool.dma_start(scratch, ext[:]).then_inc(s["bT4"], 16)
            pool.wait_ge(s["bT4"], 16)
            pool.dma_start(hankel[:], bass.AP(tensor=scratch.tensor, offset=0, ap=[[1, P], [384, HEADS], [1, 256]])).then_inc(s["bT5"], 16)
            pool.wait_ge(s["eaten"], chunk_end("ffn_up", 21))
            pool.dma_start(frow[:], a["rows"][2, :].partition_broadcast(P)).then_inc(s["fr_in"], 16)
            pool.dma_start(ptok[:], a["pT"]).then_inc(s["pt_in"], 16)
            for c in range(4):
                pool.wait_ge(s["gt_x"], c + 1)
                pool.dma_start(out.rearrange("(t p) d -> p t d", p=P)[:, :, c * 512:(c + 1) * 512], x3[:, 0:2, c * 512:(c + 1) * 512]).then_inc(s["stored"], 16)
            pool.wait_ge(s["stored"], 64)

        @block.scalar
        def _(act):
            ch = Chain(act, s["act_chain"])
            A = nc.scalar.activation

            def pause():
                act.sem_inc(s["act_pause"], 1)

            def split(p, slot):
                if isinstance(p, int) and p >= PIECES:
                    return
                act.wait_ge(raw_in[slot], 16 * ((p - slot) // SLOTS) + 16 if isinstance(p, int) else 4 * (p - slot) + 16)
                if not (isinstance(p, int) and p < SLOTS):
                    act.wait_ge(eaten, p - SLOTS + 1)
                A(w_hi[:, slot, :], raw[:, slot, :], ACT.Copy).then_inc(hi_split, 1)

            def phase(name, head, epi, last=False):
                chunks, per, _ = SHAPE[name]
                base = BASE[name]

                def body(c, cs, step):
                    for k in range(per):
                        step(k)
                        split(base + c * per + LEAD + k, (base + cs * per + LEAD + k) % SLOTS)

                body(0, 0, head)
                if epi and last:
                    for c in range(1, chunks):
                        body(c, c % 2, lambda k: epi(c - 1, (c - 1) % 2, k))
                elif epi:
                    over_chunks(act, ch, "act_" + name, chunks, paired[name],
                                lambda c, par: body(c, par, lambda k: epi(c - 1, 1 - par, k)))
                else:
                    for c in range(1, chunks):
                        body(c, c, lambda k: None)

            nothing = lambda k: None

            def tail(epi, e, par, per=8):
                for k in range(per):
                    epi(e, par, k)

            def norm_root(n, T, scale=1.0 / D):
                act.wait_ge(s["norm_sum"], n + 1)
                A(rstd_root[:, 0:T], rstd[:, 0:T], ACT.Sqrt, bias=col("eps"), scale=scale).then_inc(s["norm_root"], 1)

            def norm_step(n, T, xs, hi, A_cols, B_cols, kg):
                if kg == 0:
                    act.wait_ge(s["norm_rstd"], n + 1)
                m = 4 * prep_index(n) + kg
                if m > 0:
                    act.wait_ge(s["xT_ready"], m)
                for t in range(T):
                    ins = A(xs[:, t, :], x3[:, t, kg * 512:(kg + 1) * 512], ACT.Copy, scale=rstd[:, t:t + 1])
                ins.then_inc(s["xs_ready"], 1)
                act.wait_ge(s["xT_ready"], m + 1)
                for kk in range(4):
                    kt = 4 * kg + kk
                    bank, c0 = norm_bank(T, kg, kk)
                    for b in range(T // 2):
                        ins = A(hi[:, kt * T * P + b * 256:kt * T * P + b * 256 + 256], bank[:, c0 + b * 256:c0 + b * 256 + 256],
                                ACT.Identity, scale=A_cols(b, kt), bias=B_cols(b, kt) if B_cols else 0.0)
                ins.then_inc(s["h_hi_ready"], 1)

            a_layer = lambda b, kt: mod_a[:, b, kt:kt + 1]
            b_layer = lambda b, kt: modT[:, b, kt:kt + 1]

            def conv(L, e, k):
                T = tokens[L]
                if k == 0:
                    act.wait_ge(eaten, chunk_end(f"in{L}_conv", e))
                    act.wait_ge(s["cv_done"], 8 * L + e + 1)
                    for t in range(0, T, 2):
                        ins = A(u[:, t, :], main[t][:, :], ACT.Copy)
                    ins.then_inc(free_a, 1)
                if k == 2:
                    act.wait_ge(s["cv_T"], 8 * L + e + 1)
                    A(zr[:].rearrange("p t n -> p (t n)")[:, 0:T * P], aux[3][:, 0:T * P], ACT.Silu)
                    A(qT[:, 0:T * P], aux[2][:, 0:T * P], ACT.Copy).then_inc(s["cv_z"], 1)

            def conv_root(L):
                act.wait_ge(s["cf_s"], L + 1)
                A(dtmp[:, 0:tokens[L] * P], aux[0][:, 0:tokens[L] * P], ACT.Sqrt, bias=col("eps"), scale=1.0 / HALF).then_inc(s["cf_q"], 1)

            def ret(L, e, k):
                T = tokens[L]
                if k == 0:
                    act.wait_ge(eaten, chunk_end(f"in{L}_ret", e))
                    act.wait_ge(s["rt_y"], 8 * L + e + 1)
                    for t in range(0, 4, 2):
                        lo, n = (128, 256) if t >= T else (0, 512)
                        ins = A(u[:, t, lo:lo + n], main[t][:, lo:lo + n], ACT.Copy)
                    ins.then_inc(free_a, 1)
                if k == 1:
                    act.wait_ge(free_d, done_d[f"in{L}_ret"] + e + 1)
                    act.wait_ge(free_a, done_a[f"in{L}_ret"] + e + 1)
                    A(zr[:, 0:T, :], u[:, 0:T, 384:512], ACT.Silu).then_inc(s["rt_z"], 1)
                    h = 16 * L + e
                    act.wait_ge(s["rt_sT"], 8 * L + e + 1)
                    dflat = decay[:].rearrange("p b q -> p (b q)")
                    pause()
                    A(dflat[:, 512:1024], wd("dpos"), ACT.Exp, scale=lg[:, ds(h, 1)])
                    A(dtmp[:], wd("dneg"), ACT.Exp, scale=lg[:, ds(h + 8, 1)]).then_inc(s["rt_e"], 1)
                    A(dflat[:, 0:512], wd("dctxf"), ACT.Exp, scale=lg[:, ds(h, 1)])
                    act.wait_ge(s["rt_dz"], 8 * L + e + 1)
                    pause()
                    A(dtmp[:], wd("dctxb"), ACT.Exp, scale=lg[:, ds(h + 8, 1)]).then_inc(s["rt_ec"], 1)
                if k == 2:
                    act.wait_ge(s["rt_T"], 8 * L + e + 1)
                    A(qT[:, 0:T * P], aux[0][:, 0:T * P], ACT.Copy).then_inc(s["rt_qa"], 1)
                if k == 6:
                    act.wait_ge(s["rt_v"], 8 * L + e + 1)
                    A(root[:, 0:T], mv[:, 0:T, 1], ACT.Sqrt, bias=col("eps")).then_inc(s["rt_sq"], 1)

            def split_step(n, hi, src, W, k):
                A(hi[:, 2 * k * W:2 * (k + 1) * W], src(k), ACT.Copy).then_inc(s["p_hi_ready"], 1)

            def out_layer(L, e, k):
                T = tokens[L]
                if k == 1:
                    act.wait_ge(s["out_x"], 4 * L + e + 1)
                    for t in range(T):
                        pause()
                        ch.link(A(msb[:], x3[:, t, ds(e * 512, 512)], ACT.Square, accum_out=ssq[:, t, ds(e, 1)]))
                if k == 2:
                    act.sem_inc(s["out_sq"], 1)

            def attn_front(e, par, k, name):
                n = e + (8 if name == "dil" else 0)
                if k == 0:
                    act.wait_ge(eaten, chunk_end(name, e))
                    act.wait_ge(s["a_y"], n + 1)
                    A(u2[:, 0, :], main[2 * par][:, 0:384], ACT.Copy).then_inc(free_a, 1)
                if k == 1:
                    act.wait_ge(s["a_T"], n + 1)
                    A(qkT[:], aux[0][:, :], ACT.Copy).then_inc(s["a_qk"], 1)

            def attn_back(e, k, name):
                n = e + (8 if name == "dil" else 0)
                if k == 6:
                    act.wait_ge(s["a_o"], n + 1)
                    if name == "dil":
                        act.wait_ge(s["d_r"], e + 1)
                    for t in range(2):
                        sc = rsum[:, t:t + 1] if name == "dil" else 1.0
                        ch.link(A(t4[:, t * P:(t + 1) * P], aux[3][:, t * P:(t + 1) * P], ACT.Square, scale=sc, accum_out=hsq[:, t:t + 1]))
                    A(hroot[:], hsq[:], ACT.Sqrt, bias=col("eps"), scale=1.0 / P).then_inc(s["a_sq"], 1)

            def sb_head(e, par, k):
                attn_front(e, par, k, "sb")
                if k == 2:
                    act.wait_ge(s["a_z"], e + 1)
                    ch.link(A(t1[:], aux[1][:, :], ACT.Abs, scale=P ** -0.5))
                    ch.link(A(t1[:], t1[:], ACT.Exp, scale=-1.0))
                    A(t1[:], t1[:], ACT.Ln, bias=1.0).then_inc(s["s_l"], 1)
                if k == 4:
                    act.wait_ge(s["s_s"], e + 1)
                    A(t3[:], t3[:], ACT.Exp).then_inc(s["s_e"], 1)
                attn_back(e, k, "sb")

            def dil_head(e, par, k):
                attn_front(e, par, k, "dil")
                if k == 3:
                    act.wait_ge(s["d_L"], e + 1)
                    ch.link(A(t2[:, 0:256], t1[:, 0:256], ACT.Exp, bias=rmax[:, 0:1], accum_out=rsum[:, 0:1]))
                    ch.link(A(t2[:, 256:384], t1[:, 256:384], ACT.Exp, bias=rmax[:, 1:2], accum_out=rsum[:, 1:2]))
                    act.sem_inc(s["d_p"], 1)
                attn_back(e, k, "dil")

            def plain_out(name, n, e, par, k):
                if k == 0:
                    act.wait_ge(eaten, chunk_end(name, e))
                    pause()
                    A(rr[:, 0, ds(e * 512, 512)], main[2 * par][:, :], ACT.Copy).then_inc(free_a, 1)
                if k == 1:
                    act.wait_ge(free_a, done_a[name] + e + 1)
                    act.wait_ge(free_d, done_d[name] + e + 1)
                    for t in range(2):
                        pause()
                        ch.link(A(xs2[:, 0, :], rr[:, t, ds(e * 512, 512)], ACT.Square, accum_out=ssq[:, t, ds(e, 1)]))
                if k == 2:
                    act.sem_inc(s["out_sq"], 1)

            def residual_sq(n):
                for t in range(2):
                    act.wait_ge(s["res_x"], n + 1)
                    ch.link(A(rr[:, t, :], x3[:, t, :], ACT.Square, accum_out=ssq[:, t, 0:1]))
                act.sem_inc(s["ssq0"], 1)

            def ffn_up(e, par, k):
                if k == 0:
                    act.wait_ge(eaten, chunk_end("ffn_up", e))
                    act.wait_ge(s["f_T"], e + 1)
                    for t in range(2):
                        ins = A(fs[:, t, :], main[2 * par + t][:, 0:256], ACT.Silu)
                    ins.then_inc(free_a, 1)
                if k == 2:
                    act.wait_ge(s["f_T"], e + 2)
                    pause()
                    A(f_hi[:, ds(e * 512, 512)], aux[0][:, :], ACT.Copy).then_inc(s["f_hi"], 1)

            def gate(e, par, k):
                if k == 0:
                    act.wait_ge(eaten, chunk_end("gate", e))
                    if e > 0:
                        act.wait_ge(s["gt_x"], e)
                    for t in range(2):
                        ins = A(sig[:, t, :], main[2 * par + t][:, :], ACT.Sigmoid)
                    ins.then_inc(free_a, 1)

            act.sem_inc(free_a, 1)
            for p in range(LEAD):
                split(p, p)
            act.wait_ge(s["loads_c"], 32)
            act.wait_ge(s["cx"], 1)
            ch.link(A(cvec[:, 0:2 * KT], msb[:, 0:32], ACT.Silu))
            ch.link(A(c_hi[:], cvec[:], ACT.Copy))
            act.sem_inc(s["csplit"], 1)
            act.wait_ge(s["loads_p"], 32)
            A(lg[:], lg[:], ACT.Exp).then_inc(s["lgx"], 1)

            norm = 0
            for L in range(2):
                T = tokens[L]
                xs = u
                phase(f"mod{L}" if L == 0 else "mod1", nothing, None) if L == 0 else phase("mod1", nothing, None)
                if L == 1:
                    phase("modg1", nothing, None)
                else:
                    act.wait_ge(s["loads_x"], 32)
                    act.wait_ge(s["ssq0"], 1)
                    for t in range(4):
                        ch.link(A(act_hi_scratch(), x3[:, t, :], ACT.Square, accum_out=ssq[:, t, 0:1]))
                    act.sem_inc(s["out_sq"], 4)
                norm_root(norm, 4)
                act.wait_ge(s["lgd"], 1)
                act.wait_ge(s["consts"], L + 1)
                phase(f"in{L}_conv", lambda k: [norm_step(norm, 4, xs, act_hi, a_layer, b_layer, kg) for kg in norm_groups(k)],
                      lambda e, par, k: conv(L, e, k))

                def ret_start(k):
                    conv(L, 7, k)
                    if k == 7:
                        conv_root(L)

                phase(f"in{L}_ret", ret_start, lambda e, par, k: ret(L, e, k))
                Y, W = y_of[L], T * P

                def last_head(k):
                    ret(L, 7, k)

                if L == 0:
                    phase("modg0", last_head, None)
                else:
                    for k in range(8):
                        last_head(k)

                def branch(k, L=L, Y=Y, W=W):
                    if k == 0:
                        act.wait_ge(s["rt_y"], 8 * L + 9)
                        act.wait_ge(s["y_scaled"], 8 * L + 8)
                        act.wait_ge(eaten, chunk_end(f"in{L}_ret", 7))
                    split_step(L, act_hi, lambda k: Y[:, 2 * k:2 * k + 2, :].rearrange("p a n -> p (a n)"), W, k)

                phase(f"out{L}", branch, lambda e, par, k: out_layer(L, e, k))
                for k in range(3):
                    out_layer(L, 3, k)
                norm += 1
            norm_root(2, 2)
            for t in range(2):
                act.wait_ge(s["fin_x1"], 1)
                ch.link(A(rr[:, t, :], x3[:, t, :], ACT.Square, accum_out=ssq[:, t, 0:1]))
            act.sem_inc(s["fin_sq"], 1)
            norm_root(3, 2)
            ln = lambda name: (lambda b, kt: col(name, kt))
            phase("sb", lambda k: [norm_step(3, 2, xs2, h_hi, ln("mixpre"), None, kg) for kg in norm_groups(k)], sb_head)
            phase("dil", lambda k: sb_head(7, 1, k), dil_head)
            tail(dil_head, 7, 1)
            O = y_of[1]

            def heads(k):
                if k == 0:
                    act.wait_ge(s["a_y"], 17)
                    act.wait_ge(eaten, chunk_end("dil", 7))
                split_step(2, h_hi, lambda k: O[:, 2 * k:2 * k + 2, :].rearrange("p a n -> p (a n)"), 256, k)

            phase("out2", heads, lambda e, par, k: plain_out("out2", 0, e, par, k))
            for k in range(3):
                plain_out("out2", 0, 3, 1, k)
            norm_root(4, 2)
            residual_sq(0)
            norm_root(5, 2)
            phase("ffn_up", lambda k: [norm_step(5, 2, xs2, h_hi, ln("ffnpre"), None, kg) for kg in norm_groups(k)], ffn_up)
            phase("ffn_down", lambda k: ffn_up(21, 1, k), lambda e, par, k: plain_out("ffn_down", 1, e, par, k))
            for k in range(3):
                plain_out("ffn_down", 1, 3, 1, k)
            norm_root(6, 2)
            act.wait_ge(s["pt_in"], 16)
            A(p_hi[:], ptok[:], ACT.Copy).then_inc(s["px_h"], 1)
            phase("proj", nothing, None)
            residual_sq(1)
            norm_root(7, 2)
            act.wait_ge(eaten, chunk_end("proj", 3))
            for c in range(4):
                ins = A(rr[:, 0, c * 512:(c + 1) * 512], (main if c < 2 else aux)[2 * (c % 2)][:, :], ACT.Copy)
            ins.then_inc(s["pj_out"], 1)
            phase("gate", lambda k: [norm_step(7, 2, xs2, h_hi, ln("pli"), None, kg) for kg in norm_groups(k)], gate, last=True)
            gate(3, 1, 0)

        @block.vector
        def _(dve):
            ch = Chain(dve, s["dve_chain"])
            V = nc.vector

            def split(p, slot):
                if isinstance(p, int) and p >= PIECES:
                    return
                dve.wait_ge(hi_split, p + 1)
                V.tensor_tensor(out=w_lo[:, slot, :], in0=raw[:, slot, :], in1=w_hi[:, slot, :].bitcast(F32), op=ALU.subtract).then_inc(lo_split, 1)

            def phase(name, head, epi, last=False):
                chunks, per, _ = SHAPE[name]
                base = BASE[name]

                def body(c, cs, step):
                    for k in range(per):
                        step(k)
                        split(base + c * per + LEAD + k, (base + cs * per + LEAD + k) % SLOTS)

                body(0, 0, head)
                if epi and last:
                    for c in range(1, chunks):
                        body(c, c % 2, lambda k: epi(c - 1, (c - 1) % 2, k))
                elif epi:
                    over_chunks(dve, ch, "dve_" + name, chunks, paired[name],
                                lambda c, par: body(c, par, lambda k: epi(c - 1, 1 - par, k)))
                else:
                    for c in range(1, chunks):
                        body(c, c, lambda k: None)

            nothing = lambda k: None

            def tail(epi, e, par, per=8):
                for k in range(per):
                    epi(e, par, k)

            def mod(L, e, par, k):
                if k == 0:
                    dve.wait_ge(eaten, chunk_end(f"mod{L}", e))
                    V.tensor_copy(out=msb[0:2, :], in_=main[2 * par][0:2, :]).then_inc(free_d, 1)
                if k == 2:
                    dve.wait_ge(s["md_T"], 8 * L + e + 1)
                    V.tensor_tensor(out=modT[:, :, ds(4 * e, 4)], in0=aux[0][:, 0:8].rearrange("p (k b) -> p b k", b=2),
                                    in1=cols[:, ds(COLS[f"bmod{L}"] + 4 * e, 4)].unsqueeze(1).to_broadcast([P, 2, 4]), op=ALU.add).then_inc(s["md_d"], 1)

            def mod_gate(L, e, par, k):
                if k == 0:
                    dve.wait_ge(eaten, chunk_end(f"modg{L}", e))
                    V.tensor_copy(out=msb[0:2, :], in_=main[2 * par][0:2, :]).then_inc(free_d, 1)
                if k == 2:
                    dve.wait_ge(s["mg_s"], 4 * L + e + 1)
                    for b in range(2 - L):
                        gb = gates[:, b, ds(512 * e, 512)]
                        ins = V.tensor_tensor(out=gb, in0=gb, in1=aux[b][:, :], op=ALU.add)
                    ins.then_inc(s["mg_d"], 1)

            def norm_sum(n, T, nsum):
                if nsum:
                    ch.link(V.tensor_reduce(out=rstd[:, 0:T], in_=ssq[:, 0:T, :], axis=AX.X, op=ALU.add))
                else:
                    ch.link(V.tensor_copy(out=rstd[:, 0:T], in_=ssq[:, 0:T, 0]))
                dve.sem_inc(s["norm_sum"], 1)
                dve.wait_ge(s["norm_root"], n + 1)
                V.reciprocal(out=rstd[:, 0:T], in_=rstd_root[:, 0:T]).then_inc(s["norm_rstd"], 1)
                dve.wait_ge(s["norm_rstd"], n + 1)

            def norm_step(n, T, tmp, hi, lo, A_cols, B_cols, kg):
                m = 4 * prep_index(n) + kg
                dve.wait_ge(s["xT_ready"], m + 1)
                dve.wait_ge(s["h_hi_ready"], m + 1)
                for kk in range(4):
                    kt = 4 * kg + kk
                    bank, c0 = norm_bank(T, kg, kk)
                    for b in range(T // 2):
                        src = bank[:, c0 + b * 256:c0 + b * 256 + 256]
                        sl = slice(kt * T * P + b * 256, kt * T * P + b * 256 + 256)
                        if B_cols:
                            ch.link(V.tensor_scalar(out=tmp[:, b * 256:b * 256 + 256], in0=src, scalar1=A_cols(b, kt), scalar2=B_cols(b, kt), op0=ALU.mult, op1=ALU.add))
                            ins = V.tensor_tensor(out=lo[:, sl], in0=tmp[:, b * 256:b * 256 + 256], in1=hi[:, sl].bitcast(F32), op=ALU.subtract)
                        else:
                            ins = V.scalar_tensor_tensor(out=lo[:, sl], in0=src, scalar=A_cols(b, kt), in1=hi[:, sl].bitcast(F32), op0=ALU.mult, op1=ALU.subtract)
                        if kk < 3 or b < T // 2 - 1:
                            ch.link(ins)
                ins.then_inc(s["h_ready"], 1)
                dve.wait_ge(s["h_ready"], m + 1)

            a_layer = lambda b, kt: mod_a[:, b, kt:kt + 1]
            b_layer = lambda b, kt: modT[:, b, kt:kt + 1]

            def conv(L, e, k):
                T = tokens[L]
                S2, W = T // 2, T * P
                seq = lambda ap: ap.rearrange("p (b n) -> p b n", b=S2)
                if k == 0:
                    dve.wait_ge(eaten, chunk_end(f"in{L}_conv", e))
                    for t in range(1, T, 2):
                        ins = V.tensor_copy(out=u[:, t, :], in_=main[t][:, :])
                    ins.then_inc(free_d, 1)
                if k == 3:
                    dve.wait_ge(s["cv_z"], 8 * L + e + 1)
                    dve.wait_ge(s["cv_T"], 8 * L + e + 1)
                    ch.link(V.tensor_tensor(out=g[:, 0:S2, 1:257], in0=seq(qT[:, 0:W]), in1=seq(aux[0][:, 0:W]), op=ALU.mult))
                    dve.wait_ge(s["cv_q"], 9 * L + e + 1)
                    y = seq(kT[:, 0:W])
                    ch.link(V.tensor_scalar(out=y, in0=g[:, 0:S2, 0:256], scalar1=col(f"convw{L}", e), scalar2=None, op0=ALU.mult))
                if k == 4:
                    y = seq(kT[:, 0:W])
                    for tap in (1, 2):
                        ch.link(V.scalar_tensor_tensor(out=y, in0=g[:, 0:S2, tap:tap + 256], scalar=col(f"convw{L}", e + 8 * tap), in1=y, op0=ALU.mult, op1=ALU.add))
                if k == 5:
                    V.tensor_tensor(out=kT[:, 0:W], in0=kT[:, 0:W], in1=aux[1][:, 0:W], op=ALU.mult).then_inc(s["cv_y"], 1)
                    dve.wait_ge(s["cv_y"], 8 * L + e + 1)
                    V.scalar_tensor_tensor(out=y_of[L][:, ds(e, 1), :].rearrange("p a n -> p (a n)"), in0=kT[:, 0:W], scalar=col(f"convn{L}", e),
                                           in1=zr[:].rearrange("p t n -> p (t n)")[:, 0:W], op0=ALU.mult, op1=ALU.mult).then_inc(s["cv_done"], 1)
                    dve.wait_ge(s["cv_done"], 8 * L + e + 2)

            def conv_rstd(L):
                dve.wait_ge(s["cf_q"], L + 1)
                V.reciprocal(out=msb[:, 0:tokens[L] * P], in_=dtmp[:, 0:tokens[L] * P]).then_inc(s["cf_r"], 1)

            def ret(L, e, k):
                T = tokens[L]
                W = T * P
                n = 8 * L + e
                if k == 0:
                    dve.wait_ge(eaten, chunk_end(f"in{L}_ret", e))
                    for t in (1, 3):
                        lo, w = (128, 256) if t >= T else (0, 512)
                        ins = V.tensor_copy(out=u[:, t, lo:lo + w], in_=main[t][:, lo:lo + w])
                    ins.then_inc(free_d, 1)
                    dve.wait_ge(free_d, done_d[f"in{L}_ret"] + e + 1)
                    dve.wait_ge(free_a, done_a[f"in{L}_ret"] + e + 1)
                    ch.link(V.tensor_tensor(out=qk[:], in0=u[:, 0:2, 0:256], in1=wd3("cos"), op=ALU.mult))
                    halves = lambda ap: ap.rearrange("p t (a h f) -> p t a h f", a=4, h=2)
                    src, dst, sn = halves(u[:, 0:2, 0:256]), halves(rot), halves(wd3("sin"))
                    for h in range(2):
                        ch.link(V.tensor_tensor(out=dst[:, :, :, h, :], in0=src[:, :, :, 1 - h, :], in1=sn[:, :, :, h, :], op=ALU.mult))
                    V.tensor_tensor(out=qk[:], in0=qk[:], in1=rot, op=ALU.add).then_inc(s["rt_rope"], 1)
                if k == 2:
                    dve.wait_ge(s["rt_T"], n + 1)
                    V.tensor_copy(out=kT[:], in_=aux[1][:, :]).then_inc(s["rt_kd"], 1)
                if k == 3:
                    dve.wait_ge(s["rt_s"], n + 1)
                    dve.wait_ge(s["rt_D"], n + 1)
                    two = lambda b: aux[b][:, :].rearrange("p (b q) -> p b q", b=2)
                    V.scalar_tensor_tensor(out=sT[:, 0:2, :], in0=two(2), scalar=P ** -0.5, in1=decay[:, 0:2, :], op0=ALU.mult, op1=ALU.mult)
                    if L == 0:
                        V.tensor_tensor(out=sTc[:], in0=two(0), in1=decay[:, 2:4, :], op=ALU.mult)
                    V.tensor_tensor(out=sT[:, 2:4, :], in0=two(3), in1=decay[:, 2:4, :], op=ALU.mult).then_inc(s["rt_sT"], 1)
                if k == 5:
                    dve.wait_ge(s["rt_o"], n + 1)
                    for t in range(T):
                        ins = V.bn_stats(out=stats[:, t, :], in_=aux[1][:, t * P:(t + 1) * P])
                    ch.link(ins)
                    dve.sem_inc(s["stats_done"], 1)
                    for t in range(T):
                        ins = V.bn_aggr(out=mv[:, t, :], in_=stats[:, t, :])
                    ins.then_inc(s["rt_v"], 1)
                if k == 6:
                    dve.wait_ge(s["rt_v"], n + 1)
                    dve.wait_ge(s["rt_sq"], n + 1)
                    ch.link(V.reciprocal(out=root[:, 0:T], in_=root[:, 0:T]))
                    for t in range(T):
                        ins = V.tensor_scalar(out=kT[:, t * P:(t + 1) * P], in0=aux[1][:, t * P:(t + 1) * P], scalar1=mv[:, t, 0:1],
                                              scalar2=root[:, t:t + 1], op0=ALU.subtract, op1=ALU.mult)
                    ch.link(ins)
                    dve.wait_ge(s["rt_z"], n + 1)
                    V.tensor_tensor(out=kT[:, 0:W], in0=kT[:, 0:W], in1=zr[:].rearrange("p t n -> p (t n)")[:, 0:W], op=ALU.mult).then_inc(s["rt_n"], 1)
                if k == 7:
                    dve.wait_ge(s["rt_yT"], n + 1)
                    V.tensor_scalar(out=y_of[L][:, ds(8 + e, 1), :].rearrange("p a n -> p (a n)"), in0=aux[2][:, 0:W], scalar1=col(f"retn{L}", e),
                                    scalar2=None, op0=ALU.mult).then_inc(s["rt_y"], 1)
                    dve.wait_ge(s["rt_y"], n + 2)

            def split_step(n, hi, lo, src, W, k):
                dve.wait_ge(s["p_hi_ready"], 8 * n + k + 1)
                V.tensor_tensor(out=lo[:, 2 * k * W:2 * (k + 1) * W], in0=src(k), in1=hi[:, 2 * k * W:2 * (k + 1) * W].bitcast(F32), op=ALU.subtract).then_inc(s["p_lo_ready"], 1)

            def out_layer(L, e, par, k):
                T = tokens[L]
                if k == 0:
                    dve.wait_ge(eaten, chunk_end(f"out{L}", e))
                    for t in range(T):
                        gt = gates[:, t // 2, ds(512 * e, 512)]
                        ins = V.tensor_tensor(out=u[:, t, :], in0=main[(2 * par if L else 0) + t][:, :], in1=gt, op=ALU.mult)
                    ins.then_inc(free_d, 1)
                    dve.wait_ge(free_d, done_d[f"out{L}"] + e + 1)
                    dve.wait_ge(s["x_in"], 32)
                    for t in range(T):
                        xt = x3[:, t, ds(512 * e, 512)]
                        ins = V.tensor_tensor(out=xt, in0=xt, in1=u[:, t, :], op=ALU.add)
                    ins.then_inc(s["out_x"], 1)
                    dve.wait_ge(s["out_x"], 4 * L + e + 1)

            def attn_front(e, par, k, name):
                n = e + (8 if name == "dil" else 0)
                if k == 0:
                    dve.wait_ge(eaten, chunk_end(name, e))
                    V.tensor_copy(out=u2[:, 1, :], in_=main[2 * par + 1][:, 0:384]).then_inc(free_d, 1)

            def attn_back(e, k, name):
                n = e + (8 if name == "dil" else 0)
                if k == 6:
                    dve.wait_ge(s["a_sq"], n + 1)
                    ch.link(V.reciprocal(out=hr[:], in_=hroot[:]))
                    if name == "dil":
                        ch.link(V.tensor_tensor(out=hr[:], in0=hr[:], in1=rsum[:], op=ALU.mult))
                    for t in range(2):
                        ins = V.tensor_scalar(out=on[:, t, :], in0=aux[3][:, t * P:(t + 1) * P], scalar1=hr[:, t:t + 1], scalar2=None, op0=ALU.mult)
                    ins.then_inc(s["a_n"], 1)
                if k == 7:
                    dve.wait_ge(s["a_yT"], n + 1)
                    V.tensor_scalar(out=y_of[1][:, ds(n, 1), :].rearrange("p a n -> p (a n)"), in0=aux[0][:, 0:256], scalar1=col("head", n), scalar2=None,
                                    op0=ALU.mult).then_inc(s["a_y"], 1)
                    dve.wait_ge(s["a_y"], n + 2)

            def sb_head(e, par, k):
                attn_front(e, par, k, "sb")
                neg, keep = [maskd[:, i * 512:(i + 1) * 512] for i in range(2)]
                if k == 3:
                    dve.wait_ge(s["a_z"], e + 1)
                    dve.wait_ge(s["s_l"], e + 1)
                    ch.link(V.tensor_scalar(out=t2[:], in0=aux[1][:, :], scalar1=P ** -0.5, scalar2=0.0, op0=ALU.mult, op1=ALU.max))
                    ch.link(V.tensor_tensor(out=t2[:], in0=t2[:], in1=t1[:], op=ALU.add))
                    V.tensor_tensor(out=t4[:], in0=t2[:], in1=neg, op=ALU.mult).then_inc(s["s_lk"], 1)
                    dve.wait_ge(s["s_lk"], e + 1)
                    ch.link(V.scalar_tensor_tensor(out=t3[:], in0=aux[1][:, :], scalar=P ** -0.5, in1=t2[:], op0=ALU.mult, op1=ALU.subtract))
                if k == 4:
                    dve.wait_ge(s["s_lat"], e + 1)
                    V.tensor_tensor(out=t3[:], in0=t3[:], in1=aux[2][:, :], op=ALU.add).then_inc(s["s_s"], 1)
                if k == 5:
                    dve.wait_ge(s["s_e"], e + 1)
                    V.tensor_tensor(out=aT[:], in0=t3[:], in1=keep, op=ALU.mult).then_inc(s["a_aT"], 1)
                attn_back(e, k, "sb")

            def dil_head(e, par, k):
                attn_front(e, par, k, "dil")
                if k == 2:
                    dve.wait_ge(s["a_z"], 8 + e + 1)
                    bh = bias[:, ds(e, 1), :].rearrange("p a n -> p (a n)")
                    ch.link(V.scalar_tensor_tensor(out=t1[:, 0:256], in0=aux[1][:, 0:256], scalar=P ** -0.5, in1=bh, op0=ALU.mult, op1=ALU.add))
                    bh1 = bias[:, ds(e, 1), 128:256].rearrange("p a n -> p (a n)")
                    ch.link(V.scalar_tensor_tensor(out=t1[:, 256:384], in0=aux[1][:, 256:384], scalar=P ** -0.5, in1=bh1, op0=ALU.mult, op1=ALU.add))
                    ch.link(V.tensor_reduce(out=rmax[:, 0:1], in_=t1[:, 0:256], axis=AX.X, op=ALU.max, negate=True))
                    V.tensor_reduce(out=rmax[:, 1:2], in_=t1[:, 256:384], axis=AX.X, op=ALU.max, negate=True).then_inc(s["d_L"], 1)
                if k == 4:
                    dve.wait_ge(s["d_pT"], e + 1)
                    V.tensor_copy(out=aT[:, 0:384], in_=aux[2][:, 0:384]).then_inc(s["a_aT"], 1)
                    dve.wait_ge(s["d_p"], e + 1)
                    V.reciprocal(out=rsum[:], in_=rsum[:]).then_inc(s["d_r"], 1)
                    dve.wait_ge(s["d_r"], e + 1)
                attn_back(e, k, "dil")

            def plain_out(name, e, par, k):
                if k == 0:
                    dve.wait_ge(eaten, chunk_end(name, e))
                    dve.sem_inc(s["dve_pause"], 1)
                    V.tensor_copy(out=rr[:, 1, ds(e * 512, 512)], in_=main[2 * par + 1][:, :]).then_inc(free_d, 1)

            def residual(n, root_n, row):
                for t in range(2):
                    ch.link(V.scalar_tensor_tensor(out=rr[:, t, :], in0=rr[:, t, :], scalar=rstd[:, t:t + 1], in1=row, op0=ALU.mult, op1=ALU.mult))
                for t in range(2):
                    ch.link(V.tensor_tensor(out=x3[:, t, :], in0=x3[:, t, :], in1=rr[:, t, :], op=ALU.add))
                dve.sem_inc(s["res_x"], 1)

            def ffn_up(e, par, k):
                if k == 0:
                    dve.wait_ge(free_a, done_a["ffn_up"] + e + 1)
                    for t in range(2):
                        ins = V.tensor_tensor(out=ff[:, t, :], in0=fs[:, t, :], in1=main[2 * par + t][:, 256:512], op=ALU.mult)
                    ins.then_inc(free_d, 1)
                if k == 2:
                    dve.wait_ge(s["f_hi"], e + 1)
                    sl = ds(e * 512, 512)
                    V.tensor_tensor(out=f_lo[:, sl], in0=aux[0][:, :], in1=f_hi[:, sl].bitcast(F32), op=ALU.subtract).then_inc(s["f_lo"], 1)
                    dve.wait_ge(s["f_lo"], e + 2)

            def gate(e, par, k):
                if k == 0:
                    dve.wait_ge(free_a, done_a["gate"] + e + 1)
                    for t in range(2):
                        ch.link(V.tensor_tensor(out=sig[:, t, :], in0=sig[:, t, :], in1=rr[:, t, ds(512 * e, 512)], op=ALU.mult))
                    for t in range(2):
                        xt = x3[:, t, ds(512 * e, 512)]
                        ins = V.tensor_tensor(out=xt, in0=xt, in1=sig[:, t, :], op=ALU.add)
                    ins.then_inc(s["gt_x"], 1)
                    dve.wait_ge(s["gt_x"], e + 1)
                    dve.sem_inc(free_d, 1)

            for n in ("md_d", "mg_d", "cv_done", "rt_y", "rt_sT", "a_y", "f_lo"):
                dve.sem_inc(s[n], 1)
            dve.sem_inc(free_d, 1)
            for p in range(LEAD):
                split(p, p)
            dve.wait_ge(s["loads_c"], 32)
            cc = msb[:, 0:32].rearrange("p (k b) -> p k b", b=2)
            ch.link(V.tensor_copy(out=cc[:, :, 0], in_=colv("c", 16)))
            ch.link(V.tensor_copy(out=cc[:, :, 1], in_=colv("cctx", 16)))
            ch.link(V.memset(cvec[:, 2 * KT:2 * KT + P], 0.0))
            dve.sem_inc(s["cx"], 1)
            dve.wait_ge(s["csplit"], 1)
            V.tensor_tensor(out=c_lo[:], in0=cvec[:], in1=c_hi[:].bitcast(F32), op=ALU.subtract).then_inc(s["csplit"], 1)
            ch.link(V.memset(ssq[:], 0.0))
            dve.sem_inc(s["ssq0"], 1)
            dve.wait_ge(s["lgx"], 1)
            V.tensor_scalar(out=lg[:], in0=lg[:], scalar1=-1.0, scalar2=None, op0=ALU.mult).then_inc(s["lgd"], 1)

            norm = 0
            for L in range(2):
                T = tokens[L]
                mL = lambda e, par, k: mod(L, e, par, k)
                phase(f"mod{L}", nothing, mL)
                if L == 1:
                    dve.wait_ge(s["gate_row"], 64)
                    phase("modg1", lambda k: mL(7, 1, k), lambda e, par, k: mod_gate(1, e, par, k))
                    tail(lambda e, par, k: mod_gate(1, e, par, k), 3, 1)
                else:
                    tail(mL, 7, 1)
                dve.wait_ge(s["md_d"], 8 * L + 9)
                for b in range(2):
                    ch.link(V.scalar_tensor_tensor(out=mod_a[:, b, :], in0=modT[:, b, 16:32], scalar=1.0, in1=colv(f"norm{L}", 16), op0=ALU.add, op1=ALU.mult))
                dve.sem_inc(s["consts"], 1)
                dve.wait_ge(s["out_sq"], 4 * L + 4 if L == 0 else 8)
                norm_sum(norm, 4, True)
                phase(f"in{L}_conv", lambda k: [norm_step(norm, 4, msb, act_hi, act_lo, a_layer, b_layer, kg) for kg in norm_groups(k)],
                      lambda e, par, k: conv(L, e, k))

                def ret_start(k):
                    conv(L, 7, k)
                    if k == 7:
                        conv_rstd(L)

                phase(f"in{L}_ret", ret_start, lambda e, par, k: ret(L, e, k))
                Y, W = y_of[L], T * P
                if L == 0:
                    dve.wait_ge(s["gate_row"], 32)
                    dve.wait_ge(s["y_scaled"], 8)
                    phase("modg0", lambda k: ret(0, 7, k), lambda e, par, k: mod_gate(0, e, par, k))
                    tail(lambda e, par, k: mod_gate(0, e, par, k), 3, 1)
                else:
                    for k in range(8):
                        ret(1, 7, k)

                def branch(k, L=L, Y=Y, W=W):
                    if k == 0:
                        dve.wait_ge(s["y_scaled"], 8 * L + 8)
                    split_step(L, act_hi, act_lo, lambda k: Y[:, 2 * k:2 * k + 2, :].rearrange("p a n -> p (a n)"), W, k)

                phase(f"out{L}", branch, lambda e, par, k: out_layer(L, e, par, k))
                out_layer(L, 3, 1, 0)
                norm += 1
            dve.wait_ge(s["out_sq"], 12)
            norm_sum(2, 2, True)
            for t in range(2):
                ch.link(V.scalar_tensor_tensor(out=x3[:, t, :], in0=x3[:, t, :], scalar=rstd[:, t:t + 1], in1=gates[:, 1, :], op0=ALU.mult, op1=ALU.mult))
            dve.sem_inc(s["fin_x1"], 1)
            dve.wait_ge(s["fin_sq"], 1)
            norm_sum(3, 2, False)
            ln = lambda name: (lambda b, kt: col(name, kt))

            def sb_start(k):
                for kg in norm_groups(k):
                    norm_step(3, 2, None, h_hi, h_lo, ln("mixpre"), None, kg)
                if k == 7:
                    dve.wait_ge(s["bT2"], 1)
                    V.tensor_tensor(out=ext[:], in0=aux[0][0:HEADS, 0:384], in1=dadd[:], op=ALU.add).then_inc(s["bT3"], 1)
                    for j in range(4):
                        dve.wait_ge(s["bT2"], j + 2)
                        V.tensor_copy(out=bias[:, 2 * j:2 * j + 2, :].rearrange("p h n -> p (h n)"), in_=aux[j][:, :]).then_inc(s["bT3"], 1)

            phase("sb", sb_start, sb_head)
            phase("dil", lambda k: sb_head(7, 1, k), dil_head)
            tail(dil_head, 7, 1)
            O = y_of[1]
            phase("out2", lambda k: split_step(2, h_hi, h_lo, lambda k: O[:, 2 * k:2 * k + 2, :].rearrange("p a n -> p (a n)"), 256, k),
                  lambda e, par, k: plain_out("out2", e, par, k))
            plain_out("out2", 3, 1, 0)
            dve.wait_ge(s["out_sq"], 16)
            norm_sum(4, 2, True)
            dve.wait_ge(s["mix_in"], 16)
            residual(0, 4, mixrow[:])
            dve.wait_ge(s["ssq0"], 2)
            norm_sum(5, 2, False)
            phase("ffn_up", lambda k: [norm_step(5, 2, None, h_hi, h_lo, ln("ffnpre"), None, kg) for kg in norm_groups(k)], ffn_up)
            phase("ffn_down", lambda k: ffn_up(21, 1, k), lambda e, par, k: plain_out("ffn_down", e, par, k))
            plain_out("ffn_down", 3, 1, 0)
            dve.wait_ge(s["out_sq"], 20)
            norm_sum(6, 2, True)
            dve.wait_ge(s["px_h"], 1)
            V.tensor_tensor(out=p_lo[:], in0=ptok[:], in1=p_hi[:].bitcast(F32), op=ALU.subtract).then_inc(s["p_ready"], 1)
            phase("proj", nothing, None)
            dve.wait_ge(s["fr_in"], 16)
            residual(1, 6, frow[:])
            dve.wait_ge(s["ssq0"], 3)
            norm_sum(7, 2, False)
            dve.wait_ge(eaten, chunk_end("proj", 3))
            for c in range(4):
                ins = V.tensor_copy(out=rr[:, 1, c * 512:(c + 1) * 512], in_=(main if c < 2 else aux)[2 * (c % 2) + 1][:, :])
            ins.then_inc(s["pj_out"], 1)
            dve.wait_ge(s["pj_out"], 2)
            phase("gate", lambda k: [norm_step(7, 2, None, h_hi, h_lo, ln("pli"), None, kg) for kg in norm_groups(k)], gate, last=True)
            gate(3, 1, 0)

        @block.tensor
        def _(pe):
            ch = Chain(pe, s["act_chain"])
            mm = nc.tensor.matmul
            tr = lambda o, i: nc.tensor.transpose(o, i, mat("ident"))

            def piece(name, c, cs, k, parts, tw):
                chunks, per, w = SHAPE[name]
                slot = (BASE[name] + cs * per + k) % SLOTS
                n = w // 2
                if k == 0:
                    back = 1 if paired[name] and not (isinstance(c, int) and c == 0) else 0
                    pe.wait_ge(free_d, done_d[name] + c - back)
                    pe.wait_ge(free_a, (done_a[name] + c - back) if name in by_act else done_a[name])
                pe.wait_ge(lo_split, BASE[name] + c * per + k + 1)
                for bank, c0, c1, stat in parts:
                    for j in range(2):
                        hi, lo = stat(2 * k + j)
                        for i, (x, w_part) in enumerate(((hi, w_hi), (hi, w_lo), (lo, w_hi))):
                            ins = mm(bank[:, c0:c1], x, w_part[:, slot, j * n + c0:j * n + c1],
                                     start=(k == 0 and j == 0 and i == 0), stop=(k == per - 1 and j == 1 and i == 2))
                ins.then_inc(eaten, 1)

            def phase(name, head, epi, parts, tw=512, last=False, ready=None):
                chunks, per, w = SHAPE[name]

                def body(c, cs, step):
                    for k in range(per):
                        step(k)
                        if ready and isinstance(c, int) and c == 0:
                            ready(k)
                        piece(name, c, cs, k, parts(cs if paired[name] else 0), tw)

                body(0, 0, head)
                if epi and last:
                    for c in range(1, chunks):
                        body(c, c % 2, lambda k: epi(c - 1, (c - 1) % 2, k))
                elif epi:
                    over_chunks(pe, ch, "pe_" + name, chunks, paired[name],
                                lambda c, par: body(c, par, lambda k: epi(c - 1, 1 - par, k)))
                else:
                    for c in range(1, chunks):
                        body(c, c % 2, lambda k: None)

            nothing = lambda k: None

            def tail(epi, e, par, per=8):
                for k in range(per):
                    epi(e, par, k)

            def rows(hi, lo, T, blocks):
                def make(t):
                    return lambda kt: tuple(x[:, kt * T * P + t * P:kt * T * P + (t + 1) * P] for x in (hi, lo))
                return [(bank, c0, c1, make(t)) for t, bank, c0, c1 in blocks]

            mod_parts = lambda par: [(main[2 * par], 0, 512, lambda kt: (c_hi[:, 2 * kt:2 * kt + P], c_lo[:, 2 * kt:2 * kt + P]))]

            def mod(L, e, par, k):
                if k == 1:
                    pe.wait_ge(free_d, done_d[f"mod{L}"] + e + 1)
                    pe.wait_ge(s["md_d"], 8 * L + e + 1)
                    pe.sem_inc(s["msb_read"], 1)
                    for kk in range(4):
                        ins = nc.tensor.transpose(aux[0][:, 2 * kk:2 * kk + 2], msb[0:2, kk * P:(kk + 1) * P], mats[0:2, 0:2])
                    ins.then_inc(s["md_T"], 1)

            def mod_gate(L, e, par, k):
                if k == 1:
                    pe.wait_ge(free_d, done_d[f"modg{L}"] + e + 1)
                    pe.wait_ge(s["mg_d"], 4 * L + e + 1)
                    for b in range(2 - L):
                        ins = mm(aux[b][:, :], mats[0:2, b:b + 1].to_broadcast([2, P]), msb[0:2, :], start=True, stop=True)
                    ins.then_inc(s["mg_s"], 1)

            def norm_T(n, T, xs, kg):
                m = 4 * prep_index(n) + kg
                pe.wait_ge(s["xs_ready"], m + 1)
                back = 1 if T == 2 and kg > 0 else 0
                if m - back > 0:
                    pe.wait_ge(s["h_ready"], m - back)
                for kk in range(4):
                    bank, c0 = norm_bank(T, kg, kk)
                    for t in range(T):
                        ins = tr(bank[:, c0 + t * P:c0 + (t + 1) * P], xs[:, t, kk * P:(kk + 1) * P])
                ins.then_inc(s["xT_ready"], 1)

            def norm_head(n, T, xs):
                def step(k):
                    for kg in norm_groups(k):
                        norm_T(n, T, xs, kg)
                    if k % 2 == 0:
                        pe.wait_ge(s["h_ready"], 4 * prep_index(n) + k // 2 + 1)
                return step

            def conv(L, e, k):
                T = tokens[L]
                if k == 1:
                    pe.wait_ge(free_a, done_a[f"in{L}_conv"] + e + 1)
                    pe.wait_ge(free_d, done_d[f"in{L}_conv"] + e + 1)
                    pe.wait_ge(s["cv_done"], 8 * L + e + 1)
                    for sec in range(4):
                        for t in range(T):
                            ins = tr(aux[sec][:, t * P:(t + 1) * P], u[:, t, sec * P:(sec + 1) * P])
                    ins.then_inc(s["cv_T"], 1)

            def ret(L, e, k):
                T = tokens[L]
                n = 8 * L + e
                tok = (2, 3, 0, 1)
                if k == 1:
                    pe.wait_ge(free_a, done_a[f"in{L}_ret"] + e + 1)
                    pe.wait_ge(s["rt_rope"], n + 1)
                    for t in range(T):
                        tr(aux[0][:, t * P:(t + 1) * P], qk[:, t, 0:P] if t < 2 else u[:, t, 0:P])
                    for t in range(4):
                        ins = tr(aux[1][:, t * P:(t + 1) * P], qk[:, t, P:2 * P] if t < 2 else u[:, t, P:2 * P])
                    ins.then_inc(s["rt_T"], 1)
                if k == 3:
                    pe.wait_ge(s["rt_qa"], n + 1)
                    pe.wait_ge(s["rt_kd"], n + 1)
                    for b in range(4):
                        ins = mm(aux[2 + b // 2][:, (b % 2) * 256:(b % 2 + 1) * 256], kT[:, tok[b] * P:(tok[b] + 1) * P], qT[:, 0:256], start=True, stop=True)
                    if L == 0:
                        for b in range(2):
                            ins = mm(aux[0][:, b * 256:(b + 1) * 256], kT[:, tok[b] * P:(tok[b] + 1) * P], qT[:, 256:512], start=True, stop=True)
                    ins.then_inc(s["rt_s"], 1)
                if k == 5:
                    pe.wait_ge(s["rt_sT"], n + 2)
                    for t in range(2):
                        for b in range(4):
                            ins = mm(aux[1][:, t * P:(t + 1) * P], sT[:, b, t * P:(t + 1) * P], u[:, tok[b], 256:384], start=(b == 0), stop=(b == 3))
                    for t in range(2, T):
                        for b in range(2):
                            ins = mm(aux[1][:, t * P:(t + 1) * P], sTc[:, b, (t - 2) * P:(t - 1) * P], u[:, tok[b], 256:384], start=(b == 0), stop=(b == 1))
                    ins.then_inc(s["rt_o"], 1)
                if k == 7:
                    pe.wait_ge(s["rt_n"], n + 1)
                    for t in range(T):
                        ins = tr(aux[2][:, t * P:(t + 1) * P], kT[:, t * P:(t + 1) * P])
                    ins.then_inc(s["rt_yT"], 1)

            def attn(e, par, k, name):
                n = e + (8 if name == "dil" else 0)
                if k == 1:
                    pe.wait_ge(free_a, done_a[name] + e + 1)
                    pe.wait_ge(free_d, done_d[name] + e + 1)
                    pe.wait_ge(s["a_y"], n + 1)
                    for i in range(2):
                        for t in range(2):
                            ins = tr(aux[0][:, (2 * i + t) * P:(2 * i + t + 1) * P], u2[:, t, i * P:(i + 1) * P])
                    ins.then_inc(s["a_T"], 1)
                q, kk = qkT[:, 0:256], qkT[:, 256:512]
                if k == 2:
                    pe.wait_ge(s["a_qk"], n + 1)
                    if name == "sb":
                        for b in range(2):
                            ins = mm(aux[1][:, b * 256:(b + 1) * 256], kk[:, b * P:(b + 1) * P], q, start=True, stop=True)
                    else:
                        mm(aux[1][:, 0:256], q[:, P:2 * P], kk, start=True, stop=True)
                        ins = mm(aux[1][:, 256:384], q[:, 0:P], kk[:, 0:P], start=True, stop=True)
                    ins.then_inc(s["a_z"], 1)
                if k == 4:
                    if name == "sb":
                        pe.wait_ge(s["s_lk"], e + 1)
                        mm(aux[2][:, 0:256], amat("later"), t4[:, 0:256], start=True, stop=False)
                        mm(aux[2][:, 0:256], mat("ones"), t4[:, 256:512], start=False, stop=True)
                        mm(aux[2][:, 256:512], amat("later"), t4[:, 256:512], start=True, stop=True).then_inc(s["s_lat"], 1)
                    else:
                        pe.wait_ge(s["d_p"], e + 1)
                        for b in range(3):
                            ins = tr(aux[2][:, b * P:(b + 1) * P], t2[:, b * P:(b + 1) * P])
                        ins.then_inc(s["d_pT"], 1)
                if k == 6:
                    pe.wait_ge(s["a_aT"], n + 1)
                    of = {"sb": {0: [(0, 0)], 1: [(0, P), (1, 3 * P)]}, "dil": {0: [(0, 2 * P)], 1: [(0, 0), (1, P)]}}[name]
                    for t in range(2):
                        for i, (b, c0) in enumerate(of[t]):
                            ins = mm(aux[3][:, t * P:(t + 1) * P], aT[:, c0:c0 + P], u2[:, b, 256:384], start=(i == 0), stop=(i == len(of[t]) - 1))
                    ins.then_inc(s["a_o"], 1)
                if k == 7:
                    pe.wait_ge(s["a_n"], n + 1)
                    for t in range(2):
                        ins = tr(aux[0][:, t * P:(t + 1) * P], on[:, t, :])
                    ins.then_inc(s["a_yT"], 1)

            def ffn_up(e, par, k):
                if k == 1:
                    pe.wait_ge(free_d, done_d["ffn_up"] + e + 1)
                    pe.wait_ge(s["f_lo"], e + 1)
                    for j in range(2):
                        for t in range(2):
                            ins = tr(aux[0][:, (2 * j + t) * P:(2 * j + t + 1) * P], ff[:, t, j * P:(j + 1) * P])
                    ins.then_inc(s["f_T"], 1)

            pe.sem_inc(s["f_T"], 1)
            pe.wait_ge(s["loads_c"], 32)
            pe.wait_ge(s["csplit"], 2)
            for L in range(2):
                T = tokens[L]
                phase(f"mod{L}", nothing, lambda e, par, k: mod(L, e, par, k), mod_parts)
                if L == 1:
                    phase("modg1", lambda k: mod(L, 7, 1, k), lambda e, par, k: mod_gate(L, e, par, k), mod_parts)
                    tail(lambda e, par, k: mod_gate(L, e, par, k), 3, 1)
                else:
                    tail(lambda e, par, k: mod(L, e, par, k), 7, 1)
                conv_parts = rows(act_hi, act_lo, 4, [(t, main[t], 0, 512) for t in range(T)])
                ret_parts = conv_parts + rows(act_hi, act_lo, 4, [(t, main[t], 128, 384) for t in range(T, 4)])
                phase(f"in{L}_conv", norm_head(L, 4, u), lambda e, par, k: conv(L, e, k), lambda par: conv_parts)

                def ret_start(k):
                    conv(L, 7, k)
                    if k == 7:
                        pe.wait_ge(s["cv_q"], 9 * L + 9)
                        pe.wait_ge(s["cv_done"], 8 * L + 9)
                        mm(aux[0][:, 0:T * P], mat("ones"), acc[:, 0:T * P], start=True, stop=True).then_inc(s["cf_s"], 1)

                def ret_step(e, par, k):
                    if k == 1:
                        pe.wait_ge(s["cf_r"], L + 1)
                    ret(L, e, k)

                phase(f"in{L}_ret", ret_start, ret_step, lambda par: ret_parts)
                if L == 0:
                    phase("modg0", lambda k: ret(0, 7, k), lambda e, par, k: mod_gate(0, e, par, k), mod_parts)
                    tail(lambda e, par, k: mod_gate(0, e, par, k), 3, 1)
                else:
                    for k in range(8):
                        ret(1, 7, k)
                out_parts = (lambda par: rows(act_hi, act_lo, 4, [(t, main[t], 0, 512) for t in range(4)])) if L == 0 else \
                    (lambda par: rows(act_hi, act_lo, 2, [(t, main[2 * par + t], 0, 512) for t in range(2)]))
                phase(f"out{L}", nothing, lambda e, par, k: None, out_parts, ready=lambda k: pe.wait_ge(s["p_lo_ready"], 8 * L + k + 1))
            two = lambda hi, lo: (lambda par: rows(hi, lo, 2, [(t, main[2 * par + t], 0, 512) for t in range(2)]))
            attn_parts = lambda par: rows(h_hi, h_lo, 2, [(t, main[2 * par + t], 0, 384) for t in range(2)])
            sb_norm = norm_head(3, 2, xs2)

            def sb_start(k):
                sb_norm(k)
                if k == 7:
                    pe.wait_ge(s["bT"], 64)
                    mm(aux[0][0:HEADS, 0:384], relb[:], onehot[:], start=True, stop=True).then_inc(s["bT2"], 1)
                    pe.wait_ge(s["bT5"], 16)
                    pe.wait_ge(s["bT3"], 1)
                    for j in range(4):
                        mm(aux[j][:, :], amat("flip"), hankel[:, 2 * j:2 * j + 2, :].rearrange("p h n -> p (h n)"), start=True, stop=True).then_inc(s["bT2"], 1)

            def sb_step(e, par, k):
                if k == 1:
                    pe.wait_ge(s["bT3"], 5)
                attn(e, par, k, "sb")

            phase("sb", sb_start, sb_step, attn_parts)
            phase("dil", lambda k: attn(7, 1, k, "sb"), lambda e, par, k: attn(e, par, k, "dil"), attn_parts)
            tail(lambda e, par, k: attn(e, par, k, "dil"), 7, 1)
            phase("out2", nothing, lambda e, par, k: None, two(h_hi, h_lo), ready=lambda k: pe.wait_ge(s["p_lo_ready"], 16 + k + 1))
            phase("ffn_up", norm_head(5, 2, xs2), ffn_up, two(h_hi, h_lo))

            def down_ready(k):
                if k == 21:
                    pe.wait_ge(s["f_lo"], 23)
                elif k == 0:
                    pe.wait_ge(s["f_lo"], 22)

            phase("ffn_down", lambda k: ffn_up(21, 1, k), lambda e, par, k: None, two(f_hi, f_lo), ready=down_ready)
            pe.wait_ge(s["p_ready"], 1)
            proj = rows(p_hi, p_lo, 2, [(t, None, 0, 512) for t in range(2)])
            pe.wait_ge(free_a, done_a["gate"])
            pe.wait_ge(free_d, done_d["gate"])
            for c in range(4):
                pe.wait_ge(lo_split, BASE["proj"] + c + 1)
                for t in range(2):
                    bank = (main if c < 2 else aux)[2 * (c % 2) + t]
                    for j in range(2):
                        hi, lo = proj[t][3](j)
                        for i, (x, w_part) in enumerate(((hi, w_hi), (hi, w_lo), (lo, w_hi))):
                            ins = mm(bank[:, :], x, w_part[:, (BASE["proj"] + c) % SLOTS, j * 512:(j + 1) * 512], start=(j == 0 and i == 0), stop=(j == 1 and i == 2))
                ins.then_inc(eaten, 1)
            pe.wait_ge(s["pj_out"], 2)
            phase("gate", norm_head(7, 2, xs2), lambda e, par, k: None, two(h_hi, h_lo), last=True)


def kernel(**inputs):
    import concourse.bacc as bacc
    from concourse.bass_utils import run_bass_kernel_spmd

    x = {k: np.asarray(v) for k, v in inputs.items()}

    def pieces(w, groups):
        k, n = w.shape
        parts = w.reshape(k // 256, 2, P, n)
        return np.stack([parts[..., g].transpose(0, 2, 1, 3).reshape(k // 256, P, -1) for g in groups]) \
                 .reshape(-1, P, 2 * len(groups[0]))

    span = lambda a, n: np.arange(a, a + n)
    plain = lambda first, n: [span(first + 512 * c, 512) for c in range(n)]
    arrays = {}
    for L in range(2):
        w = x["w_mod"][L]
        arrays[f"w_mod{L}"] = pieces(w, plain(0, 8))
        arrays[f"w_modg{L}"] = pieces(w, plain(4096, 4))
        w = x["w_in"][L]
        for half, name in ((0, "conv"), (4 * HALF, "ret")):
            arrays[f"w_in{L}_{name}"] = pieces(w, [np.concatenate([span(half + i * HALF + h * P, P) for i in range(4)]) for h in range(8)])
        arrays[f"w_out{L}"] = pieces(x["w_out"][L], plain(0, 4))
    w = x["w_in_2"][0]
    for half, name in ((0, "sb"), (3 * HALF, "dil")):
        arrays[f"w_{name}"] = pieces(w, [np.concatenate([span(half + i * HALF + h * P, P) for i in range(3)]) for h in range(8)])
    arrays["w_out2"] = pieces(x["w_out_2"][0], plain(0, 4))
    arrays["w_ffn_up"] = pieces(x["w_gate_up_2"][0], [np.concatenate([span(256 * c, 256), span(FF + 256 * c, 256)]) for c in range(22)])
    arrays["w_ffn_down"] = pieces(x["w_down_2"][0], plain(0, 4))
    arrays["w_proj"] = pieces(x["w_pli_proj_2"][0], plain(0, 4))
    arrays["w_gate"] = pieces(x["w_pli_gate_2"][0], plain(0, 4))
    column = lambda v: v.reshape(-1, P).T
    vec = []
    for name in COLS:
        L = int(name[-1]) if name[-1] in "01" else 0
        vec.append({
            "norm": lambda: column(x["norm_w"][L]), "bmod": lambda: column(x["b_mod"][L][:4096]),
            "convw": lambda: column(x["conv_w"][L].reshape(-1)), "convn": lambda: column(x["conv_norm_w"][L]),
            "retn": lambda: column(x["ret_norm_w"][L]), "mixpre": lambda: column(x["ln_mix_pre_2"][0]),
            "head": lambda: column(x["ln_head_2"][0]), "ffnpre": lambda: column(x["ln_ffn_pre_2"][0]),
            "pli": lambda: column(x["ln_pli_2"][0]), "c": lambda: column(x["c"][0]), "cctx": lambda: column(x["c_ctx"]),
            "eps": lambda: np.full((P, 1), EPS, np.float32),
        }[name.rstrip("01")]())
    arrays["cols"] = np.concatenate(vec, 1)
    arrays["gate_bias"] = x["b_mod"][:, 4096:]
    arrays["rows"] = np.stack([x["final_norm_w"], x["ln_mix_post_2"][0], x["ln_ffn_post_2"][0]])
    arrays["decays"] = np.stack([x["ret_decay_f"], x["ret_decay_b"]], 1).reshape(32)
    arrays["x"], arrays["ctx"] = x["x"][0], x["ctx"][0]
    arrays["pT"] = x["p_2"][0, 0].T.reshape(2, P, TOK).transpose(1, 0, 2).reshape(P, 2 * TOK)
    arrays["rel_bias"] = x["rel_bias_2"]
    for name, v in zip(("mats", "wide", "maskd", "onehot", "dadd"), shape_constants()):
        arrays[name] = v
    nc = bacc.Bacc("TRN2", target_bir_lowering=False, num_devices=1)
    send, aps = {}, {}
    for name, v in arrays.items():
        send["in_" + name] = np.ascontiguousarray(v)
        aps[name] = nc.dram_tensor("in_" + name, v.shape, mybir.dt.float32, kind="ExternalInput").ap()
    out = nc.dram_tensor("out", (TOK, D), mybir.dt.float32, kind="ExternalOutput").ap()
    build(nc, aps, out)
    r = run_bass_kernel_spmd(nc, [send], core_ids=[0])
    return r.results[0]["out"].reshape(1, TOK, D)
```

```python
import numpy as np
import concourse.bass as bass
import concourse.mybir as mybir
from contextlib import ExitStack, contextmanager

P = 128
D = 2048
KT = D // P
TOK = 256
HALF = 1024
HEADS = 8
FF = 5632
FKT = FF // P
EPS = 1e-6
SLOTS = 4
LEAD = 3
SIDE_SLOTS = 2
SIDE_CHUNKS = 16
PHASES = [
    ("mod0", 8, 8, 1024), ("in0_conv", 8, 8, 1024), ("in0_ret", 8, 8, 1024), 
    ("out0", 4, 8, 1024), ("in1_conv", 8, 8, 1024),
    ("in1_ret", 8, 8, 1024), ("out1", 4, 8, 1024), ("sb", 8, 8, 768), ("dil", 8, 8, 768),
    ("out2", 4, 8, 1024), ("ffn_up", 22, 8, 1024), ("ffn_down", 4, 22, 1024), ("gate", 4, 9, 1024),
]
BASE, SHAPE = {}, {}
_n = 0
for _name, _c, _per, _w in PHASES:
    BASE[_name], SHAPE[_name] = _n, (_c, _per, _w)
    _n += _c * _per
PIECES = _n
LINKS = {'pool_ret': 1, 'act_in0_conv': 0, 'act_in0_ret': 0, 'act_out0': 4, 'act_in1_conv': 0, 'act_in1_ret': 0, 'act_sb': 8, 'act_dil': 8, 'act_ffn_up': 0, 'act_gate': 0, 'dve_mod0': 0, 'dve_in0_conv': 12, 'dve_in0_ret': 14, 'dve_out0': 0, 'dve_mod1': 0, 'dve_in1_conv': 4, 'dve_in1_ret': 6, 'dve_sb': 8, 'dve_dil': 10, 'dve_ffn_up': 0, 'dve_gate': 2, 'pe_mod0': 0, 'pe_in0_conv': 0, 'pe_in0_ret': 0, 'pe_out0': 0, 'pe_mod1': 0, 'pe_in1_conv': 0, 'pe_in1_ret': 0, 'pe_sb': 0, 'pe_dil': 0, 'pe_ffn_up': 0, 'pe_gate': 0}
COLS, _n = {}, 0
for _name, _w in [("norm0", 16), ("norm1", 16), ("bmod0", 32), ("bside", 64), ("convw0", 24),
                  ("convw1", 24), ("convn0", 8), ("convn1", 8), ("retn0", 8), ("retn1", 8),
                  ("mixpre", 16), ("head", 16), ("ffnpre", 16), ("pli", 16), ("c", 16),
                  ("cctx", 16), ("eps", 1)]:
    COLS[_name] = _n
    _n += _w
NCOLS = _n
MATS = ["ident", "ones"]
ATTN_MATS = ["later", "flip"]
WIDE = ["cos", "sin", "dpos", "dneg", "dscale", "dctxf", "dctxb"]


def shape_constants():
    i = np.arange(P)
    mats = {
        "ident": np.eye(P), "later": i[:, None] > i[None, :], "ones": np.ones((P, P)),
        "flip": i[:, None] + i[None, :] == P - 1,
    }
    f = 32
    inv = (np.float32(10000.0) ** (-np.arange(f, dtype=np.float32) / np.float32(f))).astype(np.float32)
    pos = np.arange(TOK)
    ang = np.stack([(pos // 64), (pos % 64)], 1).astype(np.float32)[:, :, None] * inv
    cos = np.cos(ang.astype(np.float32)).astype(np.float32)
    sin = np.sin(ang.astype(np.float32)).astype(np.float32)
    cos = np.stack([cos, cos], 2).reshape(TOK, 128)
    sin = np.stack([-sin, sin], 2).reshape(TOK, 128)
    rows = lambda a: np.concatenate([a, a], 1).reshape(2, P, 256).transpose(1, 0, 2).reshape(P, 512)
    key = (np.arange(2)[None, :, None] * P + i[:, None, None])
    q = np.arange(TOK)[None, None, :]
    d = q - key
    wide = {
        "cos": rows(cos), "sin": rows(sin), "dpos": np.maximum(d, 0), "dneg": np.maximum(-d, 0),
        "dscale": (1 + (d == 0)) * np.float32(P ** -0.5), "dctxf": q + TOK - key, "dctxb": TOK - q + key,
    }
    earlier = (key < q).astype(np.float32)
    n = np.arange(384)
    dist = 255 - n
    dd = np.maximum(dist, 0)
    big = 16 + (np.log(np.maximum(dd, 1).astype(np.float32) / np.float32(16)) / np.float32(np.log(128.0))
                * np.float32(16)).astype(np.int32)
    bucket = np.where(dd < 16, dd, np.minimum(big, 31))
    onehot = (np.arange(32)[:, None] == bucket[None, :]) & (dist >= 0)[None, :]
    times = (dist <= 128).astype(int) + (dist % 4 == 0) + (dist % 16 == 0)
    times = np.where(dist >= 0, times, 0)
    add = np.where(times > 0, np.log(np.maximum(times, 1)), -1e30)
    f32 = lambda a: np.ascontiguousarray(a, np.float32)
    return (f32(np.concatenate([mats[m] for m in MATS], 1)),
            f32(np.concatenate([wide[m].reshape(P, 512) for m in WIDE], 1)),
            f32(np.concatenate([-earlier.reshape(P, 512), earlier.reshape(P, 512)] + [mats[m] for m in ATTN_MATS], 1)),
            f32(onehot), f32(np.repeat(add[None], HEADS, 0)))


class Chain:

    def __init__(self, eng, sem):
        self.eng, self.sem, self.total, self.n, self.at = eng, sem, 0, 0, 0

    def link(self, ins):
        self.n += 1
        ins.then_inc(self.sem, 1)
        self.eng.wait_ge(self.sem, self.at + self.total + self.n)

    @contextmanager
    def turn(self, name, i, turns):
        self.total, self.n = self.total + self.n, 0
        self.at = i * LINKS.get(name, 1)
        yield
        if self.n != LINKS.get(name, 1):
            raise ValueError(f"LINKS {name} {self.n}")
        self.at, self.n, self.total = 0, 0, self.total + turns * LINKS.get(name, 1)


def over_chunks(eng, chain, key, chunks, paired, body):
    if not paired:
        with eng.Fori(0, chunks - 1) as i, chain.turn(key, i, chunks - 1):
            body(i + 1, 1)
        return
    pairs = (chunks - 2) // 2
    if pairs > 1:
        with eng.Fori(0, pairs) as i, chain.turn(key, i, pairs):
            body(2 * i + 1, 1)
            body(2 * i + 2, 0)
    else:
        body(1, 1)
        body(2, 0)
    body(chunks - 1, 1)


def build(nc, a, out):
    F32, F32R = mybir.dt.float32, mybir.dt.float32r
    ALU, ACT, AX = mybir.AluOpType, mybir.ActivationFunctionType, mybir.AxisListType
    ds = bass.ds
    top = ExitStack()
    sb = lambda scope, n, shape, dt=F32: scope.enter_context(nc.sbuf_tensor(n, shape, dt))
    scratch = nc.dram_tensor("bias_by_distance", [HEADS, 384], F32, kind="Internal").ap()

    with top:
        X = sb(top, "X", [P, 4 * D])
        raw = sb(top, "raw", [P, SLOTS, 1024])
        w_hi = sb(top, "w_hi", [P, SLOTS, 1024], F32R)
        w_lo = sb(top, "w_lo", [P, SLOTS, 1024], F32R)
        mats = sb(top, "mats", [P, len(MATS) * P])
        cols = sb(top, "cols", [P, NCOLS])
        ssq = sb(top, "ssq", [P, 4, 4])
        rstd = sb(top, "rstd", [P, 4])
        rstd_root = sb(top, "rstd_root", [P, 4])
        scale_h = sb(top, "scale_h", [P, 4])
        layer = ExitStack()
        act_hi = sb(layer, "act_hi", [P, KT * 512], F32R)
        act_lo = sb(layer, "act_lo", [P, KT * 512], F32R)
        gates = sb(layer, "gates", [P, 2, D])
        wide = sb(layer, "wide", [P, len(WIDE) * 512])
        lg = sb(layer, "lg", [P, 32])
        cvec = sb(layer, "cvec", [P, 2 * KT + P])
        c_hi = sb(layer, "c_hi", [P, 2 * KT + P], F32R)
        c_lo = sb(layer, "c_lo", [P, 2 * KT + P], F32R)
        modT = sb(layer, "modT", [P, 2, 32])
        side_raw = gates[:, 0, :].rearrange("p (s n) -> p s n", s=SIDE_SLOTS)
        side_acc = gates[:, 1, 0:1024].rearrange("p (v n) -> p v n", v=2)
        sideT = sb(layer, "sideT", [P, 2, 64])
        mod_a = sb(layer, "mod_a", [P, 2, KT])
        u = sb(layer, "u", [P, 4, 512])
        qk = sb(layer, "qk", [P, 2, 256])
        qT = sb(layer, "qT", [P, 512])
        kT = sb(layer, "kT", [P, 512])
        sT = sb(layer, "sT", [P, 4, 256])
        rot = sT[:, 2:4, :]
        sTc = qk
        g = sT[:, :, :].rearrange("p b q -> p (b q)")[:, 0:516].rearrange("p (b n) -> p b n", b=2)
        zr = sb(layer, "zr", [P, 4, 128])
        decay = sb(layer, "decay", [P, 4, 256])
        dtmp = sb(layer, "dtmp", [P, 512])
        acc = decay[:, 0:2, :].rearrange("p b q -> p (b q)")
        stats = sb(layer, "stats", [P, 4, 6])
        mv = sb(layer, "mv", [P, 4, 2])
        root = sb(layer, "root", [P, 4])
        msb = sb(layer, "msb", [P, 512])
        layer.close()
        block2 = ExitStack()
        h_hi = sb(block2, "h_hi", [P, KT * 256], F32R)
        h_lo = sb(block2, "h_lo", [P, KT * 256], F32R)
        xs2 = sb(block2, "xs2", [P, 2, 512])
        attn = ExitStack()
        maskd = sb(attn, "maskd", [P, 2 * 512 + len(ATTN_MATS) * P])
        bias = sb(attn, "bias", [P, HEADS, 256])
        hankel = sb(attn, "hankel", [P, HEADS, 256])
        onehot = sb(attn, "onehot", [32, 384])
        relb = sb(attn, "relb", [32, HEADS])
        dadd = sb(attn, "dadd", [HEADS, 384])
        ext = sb(attn, "ext", [HEADS, 384])
        mixrow = sb(attn, "mixrow", [P, D])
        u2 = sb(attn, "u2", [P, 2, 384])
        qkT = sb(attn, "qkT", [P, 512])
        t1 = sb(attn, "t1", [P, 512])
        t2 = sb(attn, "t2", [P, 512])
        t3 = sb(attn, "t3", [P, 512])
        t4 = sb(attn, "t4", [P, 512])
        aT = sb(attn, "aT", [P, 512])
        on = sb(attn, "on", [P, 2, 128])
        rsum = sb(attn, "rsum", [P, 2])
        hsq = sb(attn, "hsq", [P, 2])
        hroot = sb(attn, "hroot", [P, 2])
        hr = sb(attn, "hr", [P, 2])
        rmax = sb(attn, "rmax", [P, 2])
        attn.close()
        ffn = ExitStack()
        f_hi = sb(ffn, "f_hi", [P, FKT * 256], F32R)
        f_lo = sb(ffn, "f_lo", [P, FKT * 256], F32R)
        ffn.close()
        pli = ExitStack()
        sig = sb(pli, "sig", [P, 2, 512])
        ptok = sb(pli, "ptok", [P, 2 * 256])
        p_hi = sb(pli, "p_hi", [P, 2 * 256], F32R)
        p_lo = sb(pli, "p_lo", [P, 2 * 256], F32R)
        pli.close()
        block2.close()
        late = ExitStack()
        frow = sb(late, "frow", [P, D])
        late.close()
        fs = xs2[:, 0, :].rearrange("p (t n) -> p t n", t=2)
        ff = xs2[:, 1, :].rearrange("p (t n) -> p t n", t=2)

        main = [top.enter_context(nc.psum_tensor(f"main{i}", [P, 512], F32)) for i in range(4)]
        aux = [top.enter_context(nc.psum_tensor(f"aux{i}", [P, 512], F32)) for i in range(4)]

        S = {}

        def sem(name):
            if name not in S:
                S[name] = top.enter_context(nc.semaphore(name))
            return S[name]

        raw_in = [sem(f"raw_in{i}") for i in range(SLOTS)]
        side_in = [sem(f"side_in{i}") for i in range(SIDE_SLOTS)]
        hi_split, lo_split = sem("hi_split"), sem("lo_split")
        eaten = sem("eaten")
        free_a, free_d = sem("free_a"), sem("free_d")
        for n in ("side_used side_sum side_T loads_c loads_p act_chain dve_chain pool_chain consts lgx lgd cx csplit md_T md_d "
                  "mg_s mg_d norm_sum norm_root norm_rstd xs_ready xT_ready h_hi_ready h_ready loads_x "
                  "cv_T cv_z cv_y cv_q cv_done cf_s cf_q cf_r y_scaled p_hi_ready p_lo_ready "
                  "rt_dz rt_e rt_ec stats_done msb_read act_pause dve_pause rt_D rt_rope rt_z rt_T rt_qa rt_kd rt_s rt_sT rt_o rt_v rt_sq rt_n rt_yT rt_y "
                  "out_x x_in gate_row x_grp pre_sq mask_in bT bT2 bT3 bT4 bT5 mix_in fr_in pt_in p_ready px_h "
                  "a_T a_qk a_z s_l s_lk s_lat s_s s_e a_aT a_o a_sq a_n a_yT a_y d_L d_p d_pT d_r "
                  "r_copy res_x f_g f_T f_hi f_lo pj_out gt_sig gt_x stored ssq0 out_sq").split():
            sem(n)
        s = S

        mat = lambda n: mats[:, MATS.index(n) * P:(MATS.index(n) + 1) * P]
        amat = lambda n: maskd[:, 1024 + ATTN_MATS.index(n) * P:1024 + (ATTN_MATS.index(n) + 1) * P]
        wd = lambda n: wide[:, WIDE.index(n) * 512:(WIDE.index(n) + 1) * 512]
        wd3 = lambda n: wd(n).rearrange("p (b q) -> p b q", b=2)
        col = lambda n, j=0: cols[:, ds(COLS[n] + j, 1)]
        colv = lambda n, w: cols[:, COLS[n]:COLS[n] + w]
        x3 = X[:, :].rearrange("p (t d) -> p t d", t=4)
        rr = X[:, 2 * D:4 * D].rearrange("p (t d) -> p t d", t=2)
        y_of = [X[:, :].rearrange("p (k n) -> p k n", n=512),
                X[:, 2 * D:4 * D].rearrange("p (k n) -> p k n", n=256)]
        tokens = [4, 2]

        by_act = {"in0_conv", "in0_ret", "in1_conv", "in1_ret", "sb", "dil", "out2", "ffn_up", "ffn_down", "gate"}
        done_a, done_d, na, nd = {}, {}, 1, 1
        for name, c, per, w in PHASES:
            done_a[name], done_d[name] = na, nd
            nd += c
            na += c if name in by_act else 0
        paired = {n: n not in ("in0_conv", "in0_ret", "in1_conv", "in1_ret", "out0") for n, *_ in PHASES}

        def chunk_end(name, c):
            return BASE[name] + (c + 1) * SHAPE[name][1]

        def squares(W):
            return qk[:].rearrange("p t n -> p (t n)")[:, 0:W]

        def act_hi_scratch():
            return act_hi[:, 0:D]

        def prep_index(n):
            return {0: 0, 1: 1, 3: 2, 5: 3, 7: 4}[n]

        def norm_groups(k):
            return {0: (0, 1), 2: (2,), 4: (3,)}.get(k, ())

        def norm_bank(T, kg, kk):
            if T == 4:
                return aux[kk], 0
            return aux[2 * (kg % 2) + kk // 2], 256 * (kk % 2)

        out_head = {0: ["r0", 0, 1, "r1"], 1: ["r2", 2, "r3"], 2: [3, "r4", "r5"], 3: ["r6", "r7"],
                    4: [4, 5, "g0"], 5: ["g1"], 6: [6], 7: [7]}

        def run_out_head(k, ret, split, gate):
            for what in out_head[k]:
                if isinstance(what, int):
                    split(what)
                elif what[0] == "r":
                    ret(int(what[1]))
                else:
                    gate(int(what[1]))

        block = top.enter_context(nc.Block())

        side_first = {"in0_conv": 0, "in0_ret": 64}

        @block.sync
        def _(sp):
            for name, chunks, per, w in PHASES:
                def fetch(group, slot):
                    n = BASE[name] // SLOTS + group
                    if not (isinstance(n, int) and n == 0):
                        sp.wait_ge(lo_split, SLOTS * n + slot - SLOTS + 1)
                    sp.dma_start(raw[:, slot, 0:w], a["w_" + name][SLOTS * group + slot, :, :]).then_inc(raw_in[slot], 16)
                    if name in side_first or (name == "out0" and isinstance(group, int)):
                        g = group + side_first.get(name, 8 * SIDE_CHUNKS) // SLOTS - 1
                        if isinstance(g, int) and (g < 0 or g >= 2 * SIDE_CHUNKS):
                            return
                        side_slot = slot % SIDE_SLOTS
                        if not (isinstance(g, int) and g == 0 and slot < SIDE_SLOTS):
                            sp.wait_ge(s["side_used"], SLOTS * g + slot + 2)
                        sp.dma_start(side_raw[:, side_slot, :], a["w_side"][SLOTS * g + slot, :, :]).then_inc(side_in[side_slot], 16)

                groups = chunks * per // SLOTS
                for slot in range(SLOTS):
                    fetch(0, slot)
                if groups > 1:
                    with sp.Fori(1, groups) as i:
                        for slot in range(SLOTS):
                            fetch(i, slot)

        @block.gpsimd
        def _(pool):
            ch = Chain(pool, s["pool_chain"])
            pool.dma_start(cols[:], a["cols"]).then_inc(s["loads_c"], 16)
            pool.dma_start(mats[:], a["mats"]).then_inc(s["loads_c"], 16)
            pool.dma_start(x3[:, 0:2, :], a["x"].rearrange("(t p) d -> p t d", p=P)).then_inc(s["loads_x"], 16)
            pool.dma_start(x3[:, 2:4, :], a["ctx"].rearrange("(t p) d -> p t d", p=P)).then_inc(s["loads_x"], 16)
            pool.dma_start(wide[:], a["wide"]).then_inc(s["loads_p"], 16)
            pool.dma_start(lg[:], a["decays"].partition_broadcast(P)).then_inc(s["loads_p"], 16)
            for L in range(2):
                T = tokens[L]
                W = T * P
                Y = y_of[L]
                if L == 1:
                    pool.wait_ge(s["rt_y"], 9)
                ch.link(nc.gpsimd.memset(g[:, :, 0:1], 0.0))
                ch.link(nc.gpsimd.memset(g[:, :, 257:258], 0.0))
                nc.gpsimd.memset(acc[:], 0.0).then_inc(s["cv_q"], 1)
                pool.wait_ge(s["cv_q"], 9 * L + 1)
                with pool.Fori(0, 8) as e, ch.turn("pool_conv", e, 8):
                    pool.wait_ge(s["cv_y"], 8 * L + e + 1)
                    ch.link(nc.gpsimd.tensor_tensor(out=squares(W), in0=kT[:, 0:W], in1=kT[:, 0:W], op=ALU.mult))
                    nc.gpsimd.tensor_tensor(out=acc[:, 0:W], in0=acc[:, 0:W], in1=squares(W), op=ALU.add).then_inc(s["cv_q"], 1)
                    pool.wait_ge(s["cv_q"], 9 * L + e + 2)
                pool.wait_ge(s["cf_r"], L + 1)
                for j in range(8):
                    nc.gpsimd.tensor_tensor(out=Y[:, j, :], in0=Y[:, j, :], in1=msb[:, 0:W], op=ALU.mult).then_inc(s["y_scaled"], 1)
                if L == 0:
                    pool.wait_ge(s["loads_p"], 32)
                with pool.Fori(0, 8) as e, ch.turn("pool_ret", e, 8):
                    dflat = decay[:].rearrange("p b q -> p (b q)")
                    pool.wait_ge(s["rt_e"], 8 * L + e + 1)
                    nc.gpsimd.tensor_tensor(out=dflat[:, 512:1024], in0=dflat[:, 512:1024], in1=dtmp[:], op=ALU.mult).then_inc(s["rt_dz"], 1)
                    pool.wait_ge(s["rt_dz"], 8 * L + e + 1)
                    ch.link(nc.gpsimd.tensor_tensor(out=dflat[:, 512:1024], in0=dflat[:, 512:1024], in1=wd("dscale"), op=ALU.mult))
                    pool.wait_ge(s["rt_ec"], 8 * L + e + 1)
                    nc.gpsimd.tensor_tensor(out=dflat[:, 0:512], in0=dflat[:, 0:512], in1=dtmp[:], op=ALU.add).then_inc(s["rt_D"], 1)
                    pool.wait_ge(s["rt_D"], 8 * L + e + 1)
                if L == 0:
                    pool.wait_ge(s["p_lo_ready"], 8)
                    pool.wait_ge(s["p_hi_ready"], 8)
                    pool.dma_start(x3[:, 0:2, :], a["x"].rearrange("(t p) d -> p t d", p=P)).then_inc(s["x_in"], 16)
                    pool.dma_start(x3[:, 2:4, :], a["ctx"].rearrange("(t p) d -> p t d", p=P)).then_inc(s["x_in"], 16)
                    pool.wait_ge(s["out_x"], 4)
                    pool.dma_start(gates[:, 1, :], a["rows"][0, :].partition_broadcast(P)).then_inc(s["gate_row"], 16)
            pool.wait_ge(s["eaten"], chunk_end("out1", 3))
            pool.dma_start(onehot[:], a["onehot"]).then_inc(s["bT"], 16)
            pool.dma_start(relb[:], a["rel_bias"]).then_inc(s["bT"], 16)
            pool.dma_start(dadd[:], a["dadd"]).then_inc(s["bT"], 16)
            pool.dma_start(maskd[:], a["maskd"]).then_inc(s["mask_in"], 16)
            pool.wait_ge(s["x_grp"], 4)
            pool.dma_start(mixrow[:], a["rows"][1, :].partition_broadcast(P)).then_inc(s["mix_in"], 16)
            pool.wait_ge(s["bT3"], 1)
            pool.dma_start(scratch, ext[:]).then_inc(s["bT4"], 16)
            pool.wait_ge(s["bT4"], 16)
            pool.dma_start(hankel[:], bass.AP(tensor=scratch.tensor, offset=0, ap=[[1, P], [384, HEADS], [1, 256]])).then_inc(s["bT5"], 16)
            pool.wait_ge(s["eaten"], chunk_end("ffn_up", 21))
            pool.dma_start(frow[:], a["rows"][2, :].partition_broadcast(P)).then_inc(s["fr_in"], 16)
            pool.wait_ge(s["eaten"], chunk_end("ffn_down", 3))
            pool.dma_start(ptok[:], a["pT"]).then_inc(s["pt_in"], 16)
            for c in range(4):
                pool.wait_ge(s["gt_x"], c + 1)
                pool.dma_start(out.rearrange("(t p) d -> p t d", p=P)[:, :, c * 512:(c + 1) * 512], x3[:, 0:2, c * 512:(c + 1) * 512]).then_inc(s["stored"], 16)
            pool.wait_ge(s["stored"], 64)

        @block.scalar
        def _(act):
            ch = Chain(act, s["act_chain"])
            A = nc.scalar.activation

            def pause():
                act.sem_inc(s["act_pause"], 1)

            def split(p, slot):
                if isinstance(p, int) and p >= PIECES:
                    return
                act.wait_ge(raw_in[slot], 16 * ((p - slot) // SLOTS) + 16 if isinstance(p, int) else 4 * (p - slot) + 16)
                if not (isinstance(p, int) and p < SLOTS):
                    act.wait_ge(eaten, p - SLOTS + 1)
                A(w_hi[:, slot, :], raw[:, slot, :], ACT.Copy).then_inc(hi_split, 1)

            def phase(name, head, epi, last=False):
                chunks, per, _ = SHAPE[name]
                base = BASE[name]

                def body(c, cs, step):
                    for k in range(per):
                        step(k)
                        split(base + c * per + LEAD + k, (base + (c if isinstance(c, int) else cs) * per + LEAD + k) % SLOTS)

                body(0, 0, head)
                if epi and last:
                    for c in range(1, chunks):
                        body(c, c % 2, lambda k: epi(c - 1, (c - 1) % 2, k))
                elif epi:
                    over_chunks(act, ch, "act_" + name, chunks, paired[name],
                                lambda c, par: body(c, par, lambda k: epi(c - 1, 1 - par, k)))
                else:
                    for c in range(1, chunks):
                        body(c, c, lambda k: None)

            nothing = lambda k: None

            def tail(epi, e, par, per=8):
                for k in range(per):
                    epi(e, par, k)

            def norm_root(n, T, scale=1.0 / D):
                act.wait_ge(s["norm_sum"], n + 1)
                A(rstd_root[:, 0:T], rstd[:, 0:T], ACT.Sqrt, bias=col("eps"), scale=scale).then_inc(s["norm_root"], 1)

            def norm_step(n, T, xs, hi, A_cols, B_cols, kg):
                if kg == 0:
                    act.wait_ge(s["norm_rstd"], n + 1)
                m = 4 * prep_index(n) + kg
                if m > 0:
                    act.wait_ge(s["xT_ready"], m)
                for t in range(T):
                    ins = A(xs[:, t, :], x3[:, t, kg * 512:(kg + 1) * 512], ACT.Copy, scale=rstd[:, t:t + 1])
                ins.then_inc(s["xs_ready"], 1)
                act.wait_ge(s["xT_ready"], m + 1)
                for kk in range(4):
                    kt = 4 * kg + kk
                    bank, c0 = norm_bank(T, kg, kk)
                    for b in range(T // 2):
                        ins = A(hi[:, kt * T * P + b * 256:kt * T * P + b * 256 + 256], bank[:, c0 + b * 256:c0 + b * 256 + 256],
                                ACT.Identity, scale=A_cols(b, kt), bias=B_cols(b, kt) if B_cols else 0.0)
                ins.then_inc(s["h_hi_ready"], 1)

            a_layer = lambda b, kt: mod_a[:, b, kt:kt + 1]
            b_layer = lambda b, kt: (modT[:, b, kt:kt + 1] if L == 0 else sideT[:, b, 16 + kt:17 + kt])

            def prepare(n, A_cols, k):
                j = prep_index(n) - 2
                for kg in norm_groups(k):
                    m = 4 * prep_index(n) + kg
                    act.wait_ge(s["xT_ready"], m + 1)
                    for kk in range(4):
                        kt = 4 * kg + kk
                        bank, c0 = norm_bank(2, kg, kk)
                        ins = A(h_hi[:, kt * 256:(kt + 1) * 256], bank[:, c0:c0 + 256], ACT.Copy, scale=A_cols(0, kt))
                    ins.then_inc(s["h_hi_ready"], 1)
                for kg in {1: (0, 1), 3: (2,), 5: (3,)}.get(k, ()):
                    act.wait_ge(s["x_grp"], 4 * j + kg + 1)
                    for t in range(2):
                        ch.link(A(xs2[:, t, :], x3[:, t, kg * 512:(kg + 1) * 512], ACT.Square, accum_out=ssq[:, t, kg:kg + 1]))
                if k == 5:
                    act.sem_inc(s["pre_sq"], 1)
                if k == 6:
                    norm_root(n, 2)

            def conv(L, e, k):
                T = tokens[L]
                if k == 0:
                    act.wait_ge(eaten, chunk_end(f"in{L}_conv", e))
                    act.wait_ge(s["cv_done"], 8 * L + e + 1)
                    for t in range(0, T, 2):
                        ins = A(u[:, t, :], main[t][:, :], ACT.Copy)
                    ins.then_inc(free_a, 1)
                if k == 2:
                    act.wait_ge(s["cv_T"], 8 * L + e + 1)
                    A(zr[:].rearrange("p t n -> p (t n)")[:, 0:T * P], aux[3][:, 0:T * P], ACT.Silu)
                    A(qT[:, 0:T * P], aux[2][:, 0:T * P], ACT.Copy).then_inc(s["cv_z"], 1)

            def conv_root(L):
                act.wait_ge(s["cf_s"], L + 1)
                A(dtmp[:, 0:tokens[L] * P], aux[0][:, 0:tokens[L] * P], ACT.Sqrt, bias=col("eps"), scale=1.0 / HALF).then_inc(s["cf_q"], 1)

            def ret(L, e, k):
                T = tokens[L]
                if k == 0:
                    act.wait_ge(eaten, chunk_end(f"in{L}_ret", e))
                    act.wait_ge(s["rt_y"], 8 * L + e + 1)
                    for t in range(0, 4, 2):
                        lo, n = (128, 256) if t >= T else (0, 512)
                        ins = A(u[:, t, lo:lo + n], main[t][:, lo:lo + n], ACT.Copy)
                    ins.then_inc(free_a, 1)
                if k == 1:
                    act.wait_ge(free_d, done_d[f"in{L}_ret"] + e + 1)
                    act.wait_ge(free_a, done_a[f"in{L}_ret"] + e + 1)
                    A(zr[:, 0:T, :], u[:, 0:T, 384:512], ACT.Silu).then_inc(s["rt_z"], 1)
                    h = 16 * L + e
                    act.wait_ge(s["rt_sT"], 8 * L + e + 1)
                    dflat = decay[:].rearrange("p b q -> p (b q)")
                    pause()
                    A(dflat[:, 512:1024], wd("dpos"), ACT.Exp, scale=lg[:, ds(h, 1)])
                    A(dtmp[:], wd("dneg"), ACT.Exp, scale=lg[:, ds(h + 8, 1)]).then_inc(s["rt_e"], 1)
                    A(dflat[:, 0:512], wd("dctxf"), ACT.Exp, scale=lg[:, ds(h, 1)])
                    act.wait_ge(s["rt_dz"], 8 * L + e + 1)
                    pause()
                    A(dtmp[:], wd("dctxb"), ACT.Exp, scale=lg[:, ds(h + 8, 1)]).then_inc(s["rt_ec"], 1)
                if k == 2:
                    act.wait_ge(s["rt_T"], 8 * L + e + 1)
                    A(qT[:, 0:T * P], aux[0][:, 0:T * P], ACT.Copy).then_inc(s["rt_qa"], 1)
                if k == 6:
                    act.wait_ge(s["rt_v"], 8 * L + e + 1)
                    A(root[:, 0:T], mv[:, 0:T, 1], ACT.Sqrt, bias=col("eps")).then_inc(s["rt_sq"], 1)

            def split_step(n, hi, src, W, k):
                A(hi[:, 2 * k * W:2 * (k + 1) * W], src(k), ACT.Copy).then_inc(s["p_hi_ready"], 1)

            def out_layer(L, e, k):
                T = tokens[L]
                if k == 1:
                    act.wait_ge(s["out_x"], 4 * L + e + 1)
                    for t in range(T):
                        pause()
                        ch.link(A(msb[:], x3[:, t, ds(e * 512, 512)], ACT.Square, accum_out=ssq[:, t, ds(e, 1)]))
                if k == 2:
                    act.sem_inc(s["out_sq"], 1)

            def attn_front(e, par, k, name):
                n = e + (8 if name == "dil" else 0)
                if k == 0:
                    act.wait_ge(eaten, chunk_end(name, e))
                    act.wait_ge(s["a_y"], n + 1)
                    act.wait_ge(s["norm_rstd"], 4)
                    A(u2[:, 0, :], main[2 * par][:, 0:384], ACT.Copy, scale=scale_h[:, 0:1]).then_inc(free_a, 1)
                if k == 1:
                    act.wait_ge(s["a_T"], n + 1)
                    A(qkT[:], aux[0][:, :], ACT.Copy).then_inc(s["a_qk"], 1)

            def attn_back(e, k, name):
                n = e + (8 if name == "dil" else 0)
                if k == 6:
                    act.wait_ge(s["a_o"], n + 1)
                    if name == "dil":
                        act.wait_ge(s["d_r"], e + 1)
                    for t in range(2):
                        sc = rsum[:, t:t + 1] if name == "dil" else 1.0
                        ch.link(A(t4[:, t * P:(t + 1) * P], aux[3][:, t * P:(t + 1) * P], ACT.Square, scale=sc, accum_out=hsq[:, t:t + 1]))
                    A(hroot[:], hsq[:], ACT.Sqrt, bias=col("eps"), scale=1.0 / P).then_inc(s["a_sq"], 1)

            def sb_head(e, par, k):
                attn_front(e, par, k, "sb")
                if k == 2:
                    act.wait_ge(s["a_z"], e + 1)
                    ch.link(A(t1[:], aux[1][:, :], ACT.Abs, scale=P ** -0.5))
                    ch.link(A(t1[:], t1[:], ACT.Exp, scale=-1.0))
                    A(t1[:], t1[:], ACT.Ln, bias=1.0).then_inc(s["s_l"], 1)
                if k == 4:
                    act.wait_ge(s["s_s"], e + 1)
                    A(t3[:], t3[:], ACT.Exp).then_inc(s["s_e"], 1)
                attn_back(e, k, "sb")

            def dil_head(e, par, k):
                attn_front(e, par, k, "dil")
                if k == 3:
                    act.wait_ge(s["d_L"], e + 1)
                    ch.link(A(t2[:, 0:256], t1[:, 0:256], ACT.Exp, bias=rmax[:, 0:1], accum_out=rsum[:, 0:1]))
                    ch.link(A(t2[:, 256:384], t1[:, 256:384], ACT.Exp, bias=rmax[:, 1:2], accum_out=rsum[:, 1:2]))
                    act.sem_inc(s["d_p"], 1)
                attn_back(e, k, "dil")

            def plain_out(name, e, par, k):
                if k == 0:
                    act.wait_ge(free_a, done_a[name] + e)
                    act.wait_ge(eaten, chunk_end(name, e))
                    for t in range(2):
                        pause()
                        ins = A(xs2[:, t, :], main[2 * par + t][:, :], ACT.Square, accum_out=ssq[:, t, ds(e, 1)])
                    ins.then_inc(free_a, 1)

            def ffn_up(e, par, k):
                if k == 0:
                    act.wait_ge(eaten, chunk_end("ffn_up", e))
                    act.wait_ge(s["norm_rstd"], 6)
                    act.wait_ge(s["f_T"], e + 1)
                    for t in range(2):
                        ins = A(fs[:, t, :], main[2 * par + t][:, 0:256], ACT.Silu, scale=scale_h[:, t:t + 1])
                    ins.then_inc(free_a, 1)
                if k == 2:
                    act.wait_ge(s["f_T"], e + 2)
                    pause()
                    A(f_hi[:, ds(e * 512, 512)], aux[0][:, :], ACT.Copy).then_inc(s["f_hi"], 1)

            def gate(e, par, k):
                if k == 0:
                    act.wait_ge(s["norm_rstd"], 8)
                    act.wait_ge(eaten, chunk_end("gate", e))
                    if e > 0:
                        act.wait_ge(s["gt_x"], e)
                    for t in range(2):
                        ins = A(sig[:, t, :], main[2 * par + t][:, :], ACT.Sigmoid, scale=scale_h[:, t:t + 1])
                    ins.then_inc(free_a, 1)

            act.sem_inc(free_a, 1)
            for p in range(LEAD):
                split(p, p)
            act.wait_ge(s["loads_c"], 32)
            act.wait_ge(s["cx"], 1)
            ch.link(A(cvec[:, 0:2 * KT], msb[:, 0:32], ACT.Silu))
            ch.link(A(c_hi[:], cvec[:], ACT.Copy))
            act.sem_inc(s["csplit"], 1)
            act.wait_ge(s["loads_p"], 32)
            A(lg[:], lg[:], ACT.Exp).then_inc(s["lgx"], 1)

            norm = 0
            for L in range(2):
                T = tokens[L]
                xs = u
                if L == 0:
                    phase("mod0", nothing, None)
                    act.wait_ge(s["loads_x"], 32)
                    act.wait_ge(s["ssq0"], 1)
                    for t in range(4):
                        ch.link(A(act_hi_scratch(), x3[:, t, :], ACT.Square, accum_out=ssq[:, t, 0:1]))
                    act.sem_inc(s["out_sq"], 4)
                norm_root(norm, 4)
                act.wait_ge(s["lgd"], 1)
                act.wait_ge(s["consts"], L + 1)
                phase(f"in{L}_conv", lambda k: [norm_step(norm, 4, xs, act_hi, a_layer, b_layer, kg) for kg in norm_groups(k)],
                      lambda e, par, k: conv(L, e, k))

                def ret_start(k):
                    conv(L, 7, k)
                    if k == 7:
                        conv_root(L)

                phase(f"in{L}_ret", ret_start, lambda e, par, k: ret(L, e, k))
                Y, W = y_of[L], T * P

                def branch(k, L=L, Y=Y, W=W):
                    if k == 0:
                        act.wait_ge(s["y_scaled"], 8 * L + 8)
                    if k == 4:
                        act.wait_ge(s["rt_y"], 8 * L + 9)
                    split_step(L, act_hi, lambda k: Y[:, 2 * k:2 * k + 2, :].rearrange("p a n -> p (a n)"), W, k)

                phase(f"out{L}", lambda k: run_out_head(k, lambda j: ret(L, 7, j), branch, nothing), lambda e, par, k: out_layer(L, e, k))
                for k in range(3):
                    out_layer(L, 3, k)
                norm += 1
            norm_root(2, 2)
            ln = lambda name: (lambda b, kt: col(name, kt))
            phase("sb", lambda k: prepare(3, ln("mixpre"), k), sb_head)
            phase("dil", lambda k: sb_head(7, 1, k), dil_head)
            tail(dil_head, 7, 1)
            O = y_of[1]

            def heads(k):
                if k == 0:
                    act.wait_ge(s["a_y"], 17)
                    act.wait_ge(eaten, chunk_end("dil", 7))
                split_step(2, h_hi, lambda k: O[:, 2 * k:2 * k + 2, :].rearrange("p a n -> p (a n)"), 256, k)

            phase("out2", heads, lambda e, par, k: plain_out("out2", e, par, k))
            plain_out("out2", 3, 1, 0)
            norm_root(4, 2)
            phase("ffn_up", lambda k: prepare(5, ln("ffnpre"), k), ffn_up)
            phase("ffn_down", lambda k: ffn_up(21, 1, k), lambda e, par, k: plain_out("ffn_down", e, par, k))
            plain_out("ffn_down", 3, 1, 0)
            norm_root(6, 2)

            def gate_start(k):
                prepare(7, ln("pli"), k)
                if k == 5:
                    act.wait_ge(s["pt_in"], 16)
                    A(p_hi[:], ptok[:], ACT.Copy).then_inc(s["px_h"], 1)

            phase("gate", gate_start, gate, last=True)
            gate(3, 1, 0)

        @block.vector
        def _(dve):
            ch = Chain(dve, s["dve_chain"])
            V = nc.vector

            def split(p, slot):
                if isinstance(p, int) and p >= PIECES:
                    return
                dve.wait_ge(hi_split, p + 1)
                V.tensor_tensor(out=w_lo[:, slot, :], in0=raw[:, slot, :], in1=w_hi[:, slot, :].bitcast(F32), op=ALU.subtract).then_inc(lo_split, 1)

            def phase(name, head, epi, last=False):
                chunks, per, _ = SHAPE[name]
                base = BASE[name]

                def body(c, cs, step):
                    for k in range(per):
                        step(k)
                        if k == 0 and (name == "in0_ret" or name == "in0_conv" and cs > 0):
                            side_end(side_first[name] // 8 + c - 1)
                        split(base + c * per + LEAD + k, (base + (c if isinstance(c, int) else cs) * per + LEAD + k) % SLOTS)
                        if name in side_first:
                            side_piece(side_first[name] // 8 + c, k)

                body(0, 0, head)
                if epi and last:
                    for c in range(1, chunks):
                        body(c, c % 2, lambda k: epi(c - 1, (c - 1) % 2, k))
                elif epi:
                    over_chunks(dve, ch, "dve_" + name, chunks, paired[name],
                                lambda c, par: body(c, par, lambda k: epi(c - 1, 1 - par, k)))
                else:
                    for c in range(1, chunks):
                        body(c, c, lambda k: None)

            nothing = lambda k: None

            def tail(epi, e, par, per=8):
                for k in range(per):
                    epi(e, par, k)

            def mod(L, e, par, k):
                if k == 0:
                    dve.wait_ge(eaten, chunk_end("mod0", e))
                    V.tensor_copy(out=msb[0:2, :], in_=main[2 * par][0:2, :]).then_inc(free_d, 1)
                if k == 2:
                    dve.wait_ge(s["md_T"], 8 * L + e + 1)
                    V.tensor_tensor(out=modT[:, :, ds(4 * e, 4)], in0=aux[0][:, 0:8].rearrange("p (k b) -> p b k", b=2),
                                    in1=cols[:, ds(COLS[f"bmod0"] + 4 * e, 4)].unsqueeze(1).to_broadcast([P, 2, 4]), op=ALU.add).then_inc(s["md_d"], 1)

            def gate_rows(L, b):
                if b < 2 - L:
                    dve.wait_ge(s["mg_s"], 2 * L + b + 1)
                    for c in range(4):
                        ins = V.tensor_copy(out=gates[:, b, 512 * c:512 * (c + 1)], in_=aux[c][:, :])
                    ins.then_inc(s["mg_d"], 1)
                    dve.wait_ge(s["mg_d"], 2 * L + b + 1)

            def side_piece(chunk, k):
                m = 8 * chunk + k
                dve.wait_ge(s["side_used"], m + 3)
                dve.wait_ge(side_in[k % SIDE_SLOTS], 8 * (m - k % SIDE_SLOTS) + 16)
                if k == 0:
                    dve.wait_ge(s["side_sum"], chunk + 1)
                for j in range(2):
                    for v in range(2):
                        w, cs = side_raw[:, k % SIDE_SLOTS, j * 512:(j + 1) * 512], cvec[:, 4 * k + 2 * j + v:4 * k + 2 * j + v + 1]
                        if k == 0 and j == 0:
                            ins = V.tensor_scalar(out=side_acc[:, v, :], in0=w, scalar1=cs, scalar2=None, op0=ALU.mult)
                        else:
                            ins = V.scalar_tensor_tensor(out=side_acc[:, v, :], in0=w, scalar=cs, in1=side_acc[:, v, :], op0=ALU.mult, op1=ALU.add)
                    if j == 0:
                        ch.link(ins)
                ins.then_inc(s["side_used"], 1)

            def side_end(chunk):
                dve.wait_ge(s["side_sum"], chunk + 2)
                V.tensor_tensor(out=sideT[:, :, ds(4 * chunk, 4)], in0=aux[3][:, 0:8].rearrange("p (v k) -> p v k", v=2),
                                in1=cols[:, ds(COLS["bside"] + 4 * chunk, 4)].unsqueeze(1).to_broadcast([P, 2, 4]), op=ALU.add).then_inc(s["side_T"], 1)

            def norm_sum(n, T, to):
                V.tensor_reduce(out=rstd[:, 0:T], in_=ssq[:, 0:T, :], axis=AX.X, op=ALU.add).then_inc(s["norm_sum"], 1)
                dve.wait_ge(s["norm_root"], n + 1)
                V.reciprocal(out=to[:, 0:T], in_=rstd_root[:, 0:T]).then_inc(s["norm_rstd"], 1)
                dve.wait_ge(s["norm_rstd"], n + 1)

            def norm_step(n, T, tmp, hi, lo, A_cols, B_cols, kg):
                m = 4 * prep_index(n) + kg
                dve.wait_ge(s["xT_ready"], m + 1)
                dve.wait_ge(s["h_hi_ready"], m + 1)
                for kk in range(4):
                    kt = 4 * kg + kk
                    bank, c0 = norm_bank(T, kg, kk)
                    for b in range(T // 2):
                        src = bank[:, c0 + b * 256:c0 + b * 256 + 256]
                        sl = slice(kt * T * P + b * 256, kt * T * P + b * 256 + 256)
                        if B_cols:
                            ch.link(V.tensor_scalar(out=tmp[:, b * 256:b * 256 + 256], in0=src, scalar1=A_cols(b, kt), scalar2=B_cols(b, kt), op0=ALU.mult, op1=ALU.add))
                            ins = V.tensor_tensor(out=lo[:, sl], in0=tmp[:, b * 256:b * 256 + 256], in1=hi[:, sl].bitcast(F32), op=ALU.subtract)
                        else:
                            ins = V.scalar_tensor_tensor(out=lo[:, sl], in0=src, scalar=A_cols(b, kt), in1=hi[:, sl].bitcast(F32), op0=ALU.mult, op1=ALU.subtract)
                        if kk < 3 or b < T // 2 - 1:
                            ch.link(ins)
                ins.then_inc(s["h_ready"], 1)
                dve.wait_ge(s["h_ready"], m + 1)

            a_layer = lambda b, kt: mod_a[:, b, kt:kt + 1]
            b_layer = lambda b, kt: (modT[:, b, kt:kt + 1] if L == 0 else sideT[:, b, 16 + kt:17 + kt])

            def prepare(n, A_cols, new_x, k):
                def x_group(kg):
                    new_x(kg).then_inc(s["x_grp"], 1)

                def low(kg):
                    norm_step(n, 2, None, h_hi, h_lo, A_cols, None, kg)

                if k == 0:
                    x_group(0)
                    x_group(1)
                    low(0)
                    x_group(2)
                    low(1)
                    x_group(3)
                if k == 2:
                    low(2)
                if k == 4:
                    low(3)
                if k == 6:
                    dve.wait_ge(s["pre_sq"], prep_index(n) - 1)
                    norm_sum(n, 2, scale_h)

            def conv(L, e, k):
                T = tokens[L]
                S2, W = T // 2, T * P
                seq = lambda ap: ap.rearrange("p (b n) -> p b n", b=S2)
                if k == 0:
                    dve.wait_ge(eaten, chunk_end(f"in{L}_conv", e))
                    for t in range(1, T, 2):
                        ins = V.tensor_copy(out=u[:, t, :], in_=main[t][:, :])
                    ins.then_inc(free_d, 1)
                if k == 3:
                    dve.wait_ge(s["cv_z"], 8 * L + e + 1)
                    dve.wait_ge(s["cv_T"], 8 * L + e + 1)
                    ch.link(V.tensor_tensor(out=g[:, 0:S2, 1:257], in0=seq(qT[:, 0:W]), in1=seq(aux[0][:, 0:W]), op=ALU.mult))
                    dve.wait_ge(s["cv_q"], 9 * L + e + 1)
                    y = seq(kT[:, 0:W])
                    ch.link(V.tensor_scalar(out=y, in0=g[:, 0:S2, 0:256], scalar1=col(f"convw{L}", e), scalar2=None, op0=ALU.mult))
                if k == 4:
                    y = seq(kT[:, 0:W])
                    for tap in (1, 2):
                        ch.link(V.scalar_tensor_tensor(out=y, in0=g[:, 0:S2, tap:tap + 256], scalar=col(f"convw{L}", e + 8 * tap), in1=y, op0=ALU.mult, op1=ALU.add))
                if k == 5:
                    V.tensor_tensor(out=kT[:, 0:W], in0=kT[:, 0:W], in1=aux[1][:, 0:W], op=ALU.mult).then_inc(s["cv_y"], 1)
                    dve.wait_ge(s["cv_y"], 8 * L + e + 1)
                    V.scalar_tensor_tensor(out=y_of[L][:, ds(e, 1), :].rearrange("p a n -> p (a n)"), in0=kT[:, 0:W], scalar=col(f"convn{L}", e),
                                           in1=zr[:].rearrange("p t n -> p (t n)")[:, 0:W], op0=ALU.mult, op1=ALU.mult).then_inc(s["cv_done"], 1)
                    dve.wait_ge(s["cv_done"], 8 * L + e + 2)

            def conv_rstd(L):
                dve.wait_ge(s["cf_q"], L + 1)
                V.reciprocal(out=msb[:, 0:tokens[L] * P], in_=dtmp[:, 0:tokens[L] * P]).then_inc(s["cf_r"], 1)

            def ret(L, e, k):
                T = tokens[L]
                W = T * P
                n = 8 * L + e
                if k == 0:
                    dve.wait_ge(eaten, chunk_end(f"in{L}_ret", e))
                    for t in (1, 3):
                        lo, w = (128, 256) if t >= T else (0, 512)
                        ins = V.tensor_copy(out=u[:, t, lo:lo + w], in_=main[t][:, lo:lo + w])
                    ins.then_inc(free_d, 1)
                    dve.wait_ge(free_d, done_d[f"in{L}_ret"] + e + 1)
                    dve.wait_ge(free_a, done_a[f"in{L}_ret"] + e + 1)
                    ch.link(V.tensor_tensor(out=qk[:], in0=u[:, 0:2, 0:256], in1=wd3("cos"), op=ALU.mult))
                    halves = lambda ap: ap.rearrange("p t (a h f) -> p t a h f", a=4, h=2)
                    src, dst, sn = halves(u[:, 0:2, 0:256]), halves(rot), halves(wd3("sin"))
                    for h in range(2):
                        ch.link(V.tensor_tensor(out=dst[:, :, :, h, :], in0=src[:, :, :, 1 - h, :], in1=sn[:, :, :, h, :], op=ALU.mult))
                    V.tensor_tensor(out=qk[:], in0=qk[:], in1=rot, op=ALU.add).then_inc(s["rt_rope"], 1)
                if k == 2:
                    dve.wait_ge(s["rt_T"], n + 1)
                    V.tensor_copy(out=kT[:], in_=aux[1][:, :]).then_inc(s["rt_kd"], 1)
                if k == 3:
                    dve.wait_ge(s["rt_s"], n + 1)
                    dve.wait_ge(s["rt_D"], n + 1)
                    two = lambda b: aux[b][:, :].rearrange("p (b q) -> p b q", b=2)
                    V.scalar_tensor_tensor(out=sT[:, 0:2, :], in0=two(2), scalar=P ** -0.5, in1=decay[:, 0:2, :], op0=ALU.mult, op1=ALU.mult)
                    if L == 0:
                        V.tensor_tensor(out=sTc[:], in0=two(0), in1=decay[:, 2:4, :], op=ALU.mult)
                    V.tensor_tensor(out=sT[:, 2:4, :], in0=two(3), in1=decay[:, 2:4, :], op=ALU.mult).then_inc(s["rt_sT"], 1)
                if k == 5:
                    dve.wait_ge(s["rt_o"], n + 1)
                    for t in range(T):
                        ins = V.bn_stats(out=stats[:, t, :], in_=aux[1][:, t * P:(t + 1) * P])
                    ch.link(ins)
                    dve.sem_inc(s["stats_done"], 1)
                    for t in range(T):
                        ins = V.bn_aggr(out=mv[:, t, :], in_=stats[:, t, :])
                    ins.then_inc(s["rt_v"], 1)
                if k == 6:
                    dve.wait_ge(s["rt_v"], n + 1)
                    dve.wait_ge(s["rt_sq"], n + 1)
                    ch.link(V.reciprocal(out=root[:, 0:T], in_=root[:, 0:T]))
                    for t in range(T):
                        ins = V.tensor_scalar(out=kT[:, t * P:(t + 1) * P], in0=aux[1][:, t * P:(t + 1) * P], scalar1=mv[:, t, 0:1],
                                              scalar2=root[:, t:t + 1], op0=ALU.subtract, op1=ALU.mult)
                    ch.link(ins)
                    dve.wait_ge(s["rt_z"], n + 1)
                    V.tensor_tensor(out=kT[:, 0:W], in0=kT[:, 0:W], in1=zr[:].rearrange("p t n -> p (t n)")[:, 0:W], op=ALU.mult).then_inc(s["rt_n"], 1)
                if k == 7:
                    dve.wait_ge(s["rt_yT"], n + 1)
                    V.tensor_scalar(out=y_of[L][:, ds(8 + e, 1), :].rearrange("p a n -> p (a n)"), in0=aux[2][:, 0:W], scalar1=col(f"retn{L}", e),
                                    scalar2=None, op0=ALU.mult).then_inc(s["rt_y"], 1)
                    dve.wait_ge(s["rt_y"], n + 2)

            def split_step(n, hi, lo, src, W, k):
                dve.wait_ge(s["p_hi_ready"], 8 * n + k + 1)
                V.tensor_tensor(out=lo[:, 2 * k * W:2 * (k + 1) * W], in0=src(k), in1=hi[:, 2 * k * W:2 * (k + 1) * W].bitcast(F32), op=ALU.subtract).then_inc(s["p_lo_ready"], 1)

            def out_layer(L, e, par, k):
                T = tokens[L]
                if k == 0:
                    dve.wait_ge(eaten, chunk_end(f"out{L}", e))
                    for t in range(T):
                        gt = gates[:, t // 2, ds(512 * e, 512)]
                        ins = V.tensor_tensor(out=u[:, t, :], in0=main[(2 * par if L else 0) + t][:, :], in1=gt, op=ALU.mult)
                    ins.then_inc(free_d, 1)
                    dve.wait_ge(free_d, done_d[f"out{L}"] + e + 1)
                    dve.wait_ge(s["x_in"], 32)
                    for t in range(T):
                        xt = x3[:, t, ds(512 * e, 512)]
                        ins = V.tensor_tensor(out=xt, in0=xt, in1=u[:, t, :], op=ALU.add)
                    ins.then_inc(s["out_x"], 1)
                    dve.wait_ge(s["out_x"], 4 * L + e + 1)

            def attn_front(e, par, k, name):
                n = e + (8 if name == "dil" else 0)
                if k == 0:
                    dve.wait_ge(eaten, chunk_end(name, e))
                    V.tensor_scalar(out=u2[:, 1, :], in0=main[2 * par + 1][:, 0:384], scalar1=scale_h[:, 1:2], scalar2=None, op0=ALU.mult).then_inc(free_d, 1)

            def attn_back(e, k, name):
                n = e + (8 if name == "dil" else 0)
                if k == 6:
                    dve.wait_ge(s["a_sq"], n + 1)
                    ch.link(V.reciprocal(out=hr[:], in_=hroot[:]))
                    if name == "dil":
                        ch.link(V.tensor_tensor(out=hr[:], in0=hr[:], in1=rsum[:], op=ALU.mult))
                    for t in range(2):
                        ins = V.tensor_scalar(out=on[:, t, :], in0=aux[3][:, t * P:(t + 1) * P], scalar1=hr[:, t:t + 1], scalar2=None, op0=ALU.mult)
                    ins.then_inc(s["a_n"], 1)
                if k == 7:
                    dve.wait_ge(s["a_yT"], n + 1)
                    V.tensor_scalar(out=y_of[1][:, ds(n, 1), :].rearrange("p a n -> p (a n)"), in0=aux[0][:, 0:256], scalar1=col("head", n), scalar2=None,
                                    op0=ALU.mult).then_inc(s["a_y"], 1)
                    dve.wait_ge(s["a_y"], n + 2)

            def sb_head(e, par, k):
                attn_front(e, par, k, "sb")
                neg, keep = [maskd[:, i * 512:(i + 1) * 512] for i in range(2)]
                if k == 3:
                    dve.wait_ge(s["a_z"], e + 1)
                    dve.wait_ge(s["s_l"], e + 1)
                    ch.link(V.tensor_scalar(out=t2[:], in0=aux[1][:, :], scalar1=P ** -0.5, scalar2=0.0, op0=ALU.mult, op1=ALU.max))
                    ch.link(V.tensor_tensor(out=t2[:], in0=t2[:], in1=t1[:], op=ALU.add))
                    V.tensor_tensor(out=t4[:], in0=t2[:], in1=neg, op=ALU.mult).then_inc(s["s_lk"], 1)
                    dve.wait_ge(s["s_lk"], e + 1)
                    ch.link(V.scalar_tensor_tensor(out=t3[:], in0=aux[1][:, :], scalar=P ** -0.5, in1=t2[:], op0=ALU.mult, op1=ALU.subtract))
                if k == 4:
                    dve.wait_ge(s["s_lat"], e + 1)
                    V.tensor_tensor(out=t3[:], in0=t3[:], in1=aux[2][:, :], op=ALU.add).then_inc(s["s_s"], 1)
                if k == 5:
                    dve.wait_ge(s["s_e"], e + 1)
                    V.tensor_tensor(out=aT[:], in0=t3[:], in1=keep, op=ALU.mult).then_inc(s["a_aT"], 1)
                attn_back(e, k, "sb")

            def dil_head(e, par, k):
                attn_front(e, par, k, "dil")
                if k == 2:
                    dve.wait_ge(s["a_z"], 8 + e + 1)
                    bh = bias[:, ds(e, 1), :].rearrange("p a n -> p (a n)")
                    ch.link(V.scalar_tensor_tensor(out=t1[:, 0:256], in0=aux[1][:, 0:256], scalar=P ** -0.5, in1=bh, op0=ALU.mult, op1=ALU.add))
                    bh1 = bias[:, ds(e, 1), 128:256].rearrange("p a n -> p (a n)")
                    ch.link(V.scalar_tensor_tensor(out=t1[:, 256:384], in0=aux[1][:, 256:384], scalar=P ** -0.5, in1=bh1, op0=ALU.mult, op1=ALU.add))
                    ch.link(V.tensor_reduce(out=rmax[:, 0:1], in_=t1[:, 0:256], axis=AX.X, op=ALU.max, negate=True))
                    V.tensor_reduce(out=rmax[:, 1:2], in_=t1[:, 256:384], axis=AX.X, op=ALU.max, negate=True).then_inc(s["d_L"], 1)
                if k == 4:
                    dve.wait_ge(s["d_pT"], e + 1)
                    V.tensor_copy(out=aT[:, 0:384], in_=aux[2][:, 0:384]).then_inc(s["a_aT"], 1)
                    dve.wait_ge(s["d_p"], e + 1)
                    V.reciprocal(out=rsum[:], in_=rsum[:]).then_inc(s["d_r"], 1)
                    dve.wait_ge(s["d_r"], e + 1)
                attn_back(e, k, "dil")

            def plain_out(name, row, e, par, k):
                if k == 0:
                    dve.wait_ge(free_a, done_a[name] + e + 1)
                    cs = ds(e * 512, 512)
                    for t in range(2):
                        ins = V.tensor_tensor(out=rr[:, t, cs], in0=main[2 * par + t][:, :], in1=row[:, cs], op=ALU.mult)
                    ins.then_inc(free_d, 1)

            def residual(kg):
                for t in range(2):
                    cs = slice(kg * 512, (kg + 1) * 512)
                    ins = V.scalar_tensor_tensor(out=x3[:, t, cs], in0=rr[:, t, cs], scalar=rstd[:, t:t + 1], in1=x3[:, t, cs], op0=ALU.mult, op1=ALU.add)
                return ins

            def ffn_up(e, par, k):
                if k == 0:
                    dve.wait_ge(free_a, done_a["ffn_up"] + e + 1)
                    for t in range(2):
                        ins = V.scalar_tensor_tensor(out=ff[:, t, :], in0=main[2 * par + t][:, 256:512], scalar=scale_h[:, t:t + 1], in1=fs[:, t, :], op0=ALU.mult, op1=ALU.mult)
                    ins.then_inc(free_d, 1)
                if k == 2:
                    dve.wait_ge(s["f_hi"], e + 1)
                    sl = ds(e * 512, 512)
                    V.tensor_tensor(out=f_lo[:, sl], in0=aux[0][:, :], in1=f_hi[:, sl].bitcast(F32), op=ALU.subtract).then_inc(s["f_lo"], 1)
                    dve.wait_ge(s["f_lo"], e + 2)

            def gate(e, par, k):
                if k == 0:
                    dve.wait_ge(free_a, done_a["gate"] + e + 1)
                    for t in range(2):
                        ch.link(V.tensor_tensor(out=sig[:, t, :], in0=sig[:, t, :], in1=aux[2 * par + t][:, :], op=ALU.mult))
                    for t in range(2):
                        xt = x3[:, t, ds(512 * e, 512)]
                        ins = V.tensor_tensor(out=xt, in0=xt, in1=sig[:, t, :], op=ALU.add)
                    ins.then_inc(s["gt_x"], 1)
                    dve.wait_ge(s["gt_x"], e + 1)
                    dve.sem_inc(free_d, 1)

            for n in ("md_d", "cv_done", "rt_y", "rt_sT", "a_y", "f_lo"):
                dve.sem_inc(s[n], 1)
            dve.sem_inc(free_d, 1)
            dve.sem_inc(s["side_used"], 3)
            for p in range(LEAD):
                split(p, p)
            dve.wait_ge(s["loads_c"], 32)
            cc = msb[:, 0:32].rearrange("p (k b) -> p k b", b=2)
            ch.link(V.tensor_copy(out=cc[:, :, 0], in_=colv("c", 16)))
            ch.link(V.tensor_copy(out=cc[:, :, 1], in_=colv("cctx", 16)))
            ch.link(V.memset(cvec[:, 2 * KT:2 * KT + P], 0.0))
            dve.sem_inc(s["cx"], 1)
            dve.wait_ge(s["csplit"], 1)
            V.tensor_tensor(out=c_lo[:], in0=cvec[:], in1=c_hi[:].bitcast(F32), op=ALU.subtract).then_inc(s["csplit"], 1)
            ch.link(V.memset(ssq[:], 0.0))
            dve.sem_inc(s["ssq0"], 1)
            dve.wait_ge(s["lgx"], 1)
            V.tensor_scalar(out=lg[:], in0=lg[:], scalar1=-1.0, scalar2=None, op0=ALU.mult).then_inc(s["lgd"], 1)

            norm = 0
            for L in range(2):
                T = tokens[L]
                if L == 0:
                    mL = lambda e, par, k: mod(L, e, par, k)
                    phase("mod0", nothing, mL)
                    tail(mL, 7, 1)
                    dve.wait_ge(s["md_d"], 9)
                scale = modT[:, :, 16:32] if L == 0 else sideT[:, :, 32:48]
                for b in range(2):
                    ch.link(V.scalar_tensor_tensor(out=mod_a[:, b, :], in0=scale[:, b, :], scalar=1.0, in1=colv(f"norm{L}", 16), op0=ALU.add, op1=ALU.mult))
                dve.sem_inc(s["consts"], 1)
                dve.wait_ge(s["out_sq"], 4 * L + 4 if L == 0 else 8)
                norm_sum(norm, 4, rstd)
                phase(f"in{L}_conv", lambda k: [norm_step(norm, 4, msb, act_hi, act_lo, a_layer, b_layer, kg) for kg in norm_groups(k)],
                      lambda e, par, k: conv(L, e, k))

                def ret_start(k):
                    conv(L, 7, k)
                    if k == 7:
                        conv_rstd(L)

                phase(f"in{L}_ret", ret_start, lambda e, par, k: ret(L, e, k))
                Y, W = y_of[L], T * P

                def branch(k, L=L, Y=Y, W=W):
                    if k == 0:
                        dve.wait_ge(s["y_scaled"], 8 * L + 8)
                        if L == 0:
                            side_end(SIDE_CHUNKS - 1)
                            dve.wait_ge(s["side_T"], SIDE_CHUNKS)
                    split_step(L, act_hi, act_lo, lambda k: Y[:, 2 * k:2 * k + 2, :].rearrange("p a n -> p (a n)"), W, k)

                phase(f"out{L}", lambda k: run_out_head(k, lambda j: ret(L, 7, j), branch, lambda b: gate_rows(L, b)),
                      lambda e, par, k: out_layer(L, e, par, k))
                out_layer(L, 3, 1, 0)
                norm += 1
            dve.wait_ge(s["gate_row"], 16)
            dve.wait_ge(s["out_sq"], 12)
            norm_sum(2, 2, rstd)
            ln = lambda name: (lambda b, kt: col(name, kt))

            def final_norm(kg):
                for t in range(2):
                    cs = slice(kg * 512, (kg + 1) * 512)
                    ins = V.scalar_tensor_tensor(out=x3[:, t, cs], in0=x3[:, t, cs], scalar=rstd[:, t:t + 1], in1=gates[:, 1, cs], op0=ALU.mult, op1=ALU.mult)
                return ins

            def sb_start(k):
                prepare(3, ln("mixpre"), final_norm, k)
                if k == 1:
                    dve.wait_ge(s["bT2"], 1)
                    V.tensor_tensor(out=ext[:], in0=aux[0][0:HEADS, 0:384], in1=dadd[:], op=ALU.add).then_inc(s["bT3"], 1)
                if k == 7:
                    for j in range(4):
                        dve.wait_ge(s["bT2"], j + 2)
                        V.tensor_copy(out=bias[:, 2 * j:2 * j + 2, :].rearrange("p h n -> p (h n)"), in_=aux[j][:, :]).then_inc(s["bT3"], 1)

            phase("sb", sb_start, sb_head)
            phase("dil", lambda k: sb_head(7, 1, k), dil_head)
            tail(dil_head, 7, 1)
            O = y_of[1]
            dve.wait_ge(s["mix_in"], 16)
            phase("out2", lambda k: split_step(2, h_hi, h_lo, lambda k: O[:, 2 * k:2 * k + 2, :].rearrange("p a n -> p (a n)"), 256, k),
                  lambda e, par, k: plain_out("out2", mixrow, e, par, k))
            plain_out("out2", mixrow, 3, 1, 0)
            norm_sum(4, 2, rstd)
            dve.wait_ge(free_d, done_d["ffn_up"])
            phase("ffn_up", lambda k: prepare(5, ln("ffnpre"), residual, k), ffn_up)

            def down_step(e, par, k):
                if e == 0 and k == 0:
                    dve.wait_ge(s["fr_in"], 16)
                plain_out("ffn_down", frow, e, par, k)

            phase("ffn_down", lambda k: ffn_up(21, 1, k), down_step)
            down_step(3, 1, 0)
            norm_sum(6, 2, rstd)
            dve.wait_ge(free_d, done_d["gate"])

            def gate_start(k):
                prepare(7, ln("pli"), residual, k)
                if k == 5:
                    dve.wait_ge(s["px_h"], 1)
                    V.tensor_tensor(out=p_lo[:], in0=ptok[:], in1=p_hi[:].bitcast(F32), op=ALU.subtract).then_inc(s["p_ready"], 1)

            phase("gate", gate_start, gate, last=True)
            gate(3, 1, 0)

        @block.tensor
        def _(pe):
            ch = Chain(pe, s["act_chain"])
            mm = nc.tensor.matmul
            tr = lambda o, i: nc.tensor.transpose(o, i, mat("ident"))

            def piece(name, c, cs, k, parts, tw):
                chunks, per, w = SHAPE[name]
                slot = (BASE[name] + (c if isinstance(c, int) else cs) * per + k) % SLOTS
                n = w // 2
                if k == 0:
                    back = 1 if paired[name] and not (isinstance(c, int) and c == 0) else 0
                    pe.wait_ge(free_d, done_d[name] + c - back)
                    pe.wait_ge(free_a, (done_a[name] + c - back) if name in by_act else done_a[name])
                pe.wait_ge(lo_split, BASE[name] + c * per + k + 1)
                if name == "gate" and k == 8:
                    for t in range(2):
                        for j in range(2):
                            cs = slice(j * 256 + t * P, j * 256 + (t + 1) * P)
                            for i, (x, w_part) in enumerate(((p_hi, w_hi), (p_hi, w_lo), (p_lo, w_hi))):
                                ins = mm(aux[2 * (c % 2) + t][:, :], x[:, cs], w_part[:, slot, j * n:(j + 1) * n],
                                         start=(j == 0 and i == 0), stop=(j == 1 and i == 2))
                    ins.then_inc(eaten, 1)
                    return
                for bank, c0, c1, stat in parts:
                    for j in range(2):
                        hi, lo = stat(2 * k + j)
                        for i, (x, w_part) in enumerate(((hi, w_hi), (hi, w_lo), (lo, w_hi))):
                            ins = mm(bank[:, c0:c1], x, w_part[:, slot, j * n + c0:j * n + c1],
                                     start=(k == 0 and j == 0 and i == 0), stop=(k == (7 if name == "gate" else per - 1) and j == 1 and i == 2))
                ins.then_inc(eaten, 1)

            def phase(name, head, epi, parts, tw=512, last=False, ready=None):
                chunks, per, w = SHAPE[name]

                def body(c, cs, step):
                    for k in range(per):
                        if k == 0 and name == "in0_conv" and cs > 0:
                            side_total(c - 1, c)
                        if k == 0 and name == "in0_ret":
                            side_total(c + 7, 8 if cs == 0 else 9)
                        if k == 1 and (name == "in0_ret" or name == "in0_conv" and cs > 0):
                            pe.wait_ge(s["side_T"], side_first[name] // 8 + c)
                        step(k)
                        if ready and isinstance(c, int) and c == 0:
                            ready(k)
                        piece(name, c, cs, k, parts(cs if paired[name] else 0), tw)

                body(0, 0, head)
                if epi and last:
                    for c in range(1, chunks):
                        body(c, c % 2, lambda k: epi(c - 1, (c - 1) % 2, k))
                elif epi:
                    over_chunks(pe, ch, "pe_" + name, chunks, paired[name],
                                lambda c, par: body(c, par, lambda k: epi(c - 1, 1 - par, k)))
                else:
                    for c in range(1, chunks):
                        body(c, c % 2, lambda k: None)

            nothing = lambda k: None

            def tail(epi, e, par, per=8):
                for k in range(per):
                    epi(e, par, k)

            def rows(hi, lo, T, blocks):
                def make(t):
                    return lambda kt: tuple(x[:, kt * T * P + t * P:kt * T * P + (t + 1) * P] for x in (hi, lo))
                return [(bank, c0, c1, make(t)) for t, bank, c0, c1 in blocks]

            mod_parts = lambda par: [(main[2 * par], 0, 512, lambda kt: (c_hi[:, 2 * kt:2 * kt + P], c_lo[:, 2 * kt:2 * kt + P]))]

            def mod(L, e, par, k):
                if k == 1:
                    pe.wait_ge(free_d, done_d["mod0"] + e + 1)
                    pe.wait_ge(s["md_d"], 8 * L + e + 1)
                    pe.sem_inc(s["msb_read"], 1)
                    for kk in range(4):
                        ins = nc.tensor.transpose(aux[0][:, 2 * kk:2 * kk + 2], msb[0:2, kk * P:(kk + 1) * P], mats[0:2, 0:2])
                    ins.then_inc(s["md_T"], 1)

            def gate_rows(L, b):
                if b < 2 - L:
                    if b == 0:
                        pe.wait_ge(s["rt_y"], 8 * L + 9)
                        pe.wait_ge(s["side_T"], SIDE_CHUNKS)
                    if b + L > 0:
                        pe.wait_ge(s["mg_d"], 1 + L)
                    for j in range(KT):
                        ins = mm(aux[j // 4][:, (j % 4) * P:(j % 4 + 1) * P], sideT[:, b, 48 * L + j:48 * L + j + 1].to_broadcast([P, P]), mat("ident"), start=True, stop=True)
                    ins.then_inc(s["mg_s"], 1)

            def side_total(chunk, cv):
                pe.wait_ge(s["side_used"], 8 * chunk + 11)
                pe.wait_ge(s["cv_done"], cv)
                for v in range(2):
                    for j in range(4):
                        ins = mm(aux[3][:, 4 * v + j:4 * v + j + 1], side_acc[:, v, j * P:(j + 1) * P], mat("ones")[:, 0:1], start=True, stop=True)
                ins.then_inc(s["side_sum"], 1)

            def norm_T(n, T, xs, kg):
                m = 4 * prep_index(n) + kg
                if T == 4:
                    pe.wait_ge(s["xs_ready"], m + 1)
                else:
                    pe.wait_ge(s["x_grp"], m - 7)
                back = 1 if T == 2 and kg > 0 else 0
                if m - back > 0:
                    pe.wait_ge(s["h_ready"], m - back)
                for kk in range(4):
                    bank, c0 = norm_bank(T, kg, kk)
                    for t in range(T):
                        src = xs[:, t, kk * P:(kk + 1) * P] if T == 4 else x3[:, t, (4 * kg + kk) * P:(4 * kg + kk + 1) * P]
                        ins = tr(bank[:, c0 + t * P:c0 + (t + 1) * P], src)
                ins.then_inc(s["xT_ready"], 1)

            def norm_head(n, T, xs):
                def step(k):
                    for kg in norm_groups(k):
                        norm_T(n, T, xs, kg)
                    if k % 2 == 0:
                        pe.wait_ge(s["h_ready"], 4 * prep_index(n) + k // 2 + 1)
                return step

            def conv(L, e, k):
                T = tokens[L]
                if k == 1:
                    pe.wait_ge(free_a, done_a[f"in{L}_conv"] + e + 1)
                    pe.wait_ge(free_d, done_d[f"in{L}_conv"] + e + 1)
                    pe.wait_ge(s["cv_done"], 8 * L + e + 1)
                    for sec in range(4):
                        for t in range(T):
                            ins = tr(aux[sec][:, t * P:(t + 1) * P], u[:, t, sec * P:(sec + 1) * P])
                    ins.then_inc(s["cv_T"], 1)

            def ret(L, e, k):
                T = tokens[L]
                n = 8 * L + e
                tok = (2, 3, 0, 1)
                if k == 1:
                    pe.wait_ge(free_a, done_a[f"in{L}_ret"] + e + 1)
                    pe.wait_ge(s["rt_rope"], n + 1)
                    for t in range(T):
                        tr(aux[0][:, t * P:(t + 1) * P], qk[:, t, 0:P] if t < 2 else u[:, t, 0:P])
                    for t in range(4):
                        ins = tr(aux[1][:, t * P:(t + 1) * P], qk[:, t, P:2 * P] if t < 2 else u[:, t, P:2 * P])
                    ins.then_inc(s["rt_T"], 1)
                if k == 3:
                    pe.wait_ge(s["rt_qa"], n + 1)
                    pe.wait_ge(s["rt_kd"], n + 1)
                    for b in range(4):
                        ins = mm(aux[2 + b // 2][:, (b % 2) * 256:(b % 2 + 1) * 256], kT[:, tok[b] * P:(tok[b] + 1) * P], qT[:, 0:256], start=True, stop=True)
                    if L == 0:
                        for b in range(2):
                            ins = mm(aux[0][:, b * 256:(b + 1) * 256], kT[:, tok[b] * P:(tok[b] + 1) * P], qT[:, 256:512], start=True, stop=True)
                    ins.then_inc(s["rt_s"], 1)
                if k == 5:
                    pe.wait_ge(s["rt_sT"], n + 2)
                    for t in range(2):
                        for b in range(4):
                            ins = mm(aux[1][:, t * P:(t + 1) * P], sT[:, b, t * P:(t + 1) * P], u[:, tok[b], 256:384], start=(b == 0), stop=(b == 3))
                    for t in range(2, T):
                        for b in range(2):
                            ins = mm(aux[1][:, t * P:(t + 1) * P], sTc[:, b, (t - 2) * P:(t - 1) * P], u[:, tok[b], 256:384], start=(b == 0), stop=(b == 1))
                    ins.then_inc(s["rt_o"], 1)
                if k == 7:
                    pe.wait_ge(s["rt_n"], n + 1)
                    for t in range(T):
                        ins = tr(aux[2][:, t * P:(t + 1) * P], kT[:, t * P:(t + 1) * P])
                    ins.then_inc(s["rt_yT"], 1)

            def attn(e, par, k, name):
                n = e + (8 if name == "dil" else 0)
                if k == 1:
                    pe.wait_ge(free_a, done_a[name] + e + 1)
                    pe.wait_ge(free_d, done_d[name] + e + 1)
                    pe.wait_ge(s["a_y"], n + 1)
                    for i in range(2):
                        for t in range(2):
                            ins = tr(aux[0][:, (2 * i + t) * P:(2 * i + t + 1) * P], u2[:, t, i * P:(i + 1) * P])
                    ins.then_inc(s["a_T"], 1)
                q, kk = qkT[:, 0:256], qkT[:, 256:512]
                if k == 2:
                    pe.wait_ge(s["a_qk"], n + 1)
                    if name == "sb":
                        for b in range(2):
                            ins = mm(aux[1][:, b * 256:(b + 1) * 256], kk[:, b * P:(b + 1) * P], q, start=True, stop=True)
                    else:
                        mm(aux[1][:, 0:256], q[:, P:2 * P], kk, start=True, stop=True)
                        ins = mm(aux[1][:, 256:384], q[:, 0:P], kk[:, 0:P], start=True, stop=True)
                    ins.then_inc(s["a_z"], 1)
                if k == 4:
                    if name == "sb":
                        pe.wait_ge(s["s_lk"], e + 1)
                        mm(aux[2][:, 0:256], amat("later"), t4[:, 0:256], start=True, stop=False)
                        mm(aux[2][:, 0:256], mat("ones"), t4[:, 256:512], start=False, stop=True)
                        mm(aux[2][:, 256:512], amat("later"), t4[:, 256:512], start=True, stop=True).then_inc(s["s_lat"], 1)
                    else:
                        pe.wait_ge(s["d_p"], e + 1)
                        for b in range(3):
                            ins = tr(aux[2][:, b * P:(b + 1) * P], t2[:, b * P:(b + 1) * P])
                        ins.then_inc(s["d_pT"], 1)
                if k == 6:
                    pe.wait_ge(s["a_aT"], n + 1)
                    of = {"sb": {0: [(0, 0)], 1: [(0, P), (1, 3 * P)]}, "dil": {0: [(0, 2 * P)], 1: [(0, 0), (1, P)]}}[name]
                    for t in range(2):
                        for i, (b, c0) in enumerate(of[t]):
                            ins = mm(aux[3][:, t * P:(t + 1) * P], aT[:, c0:c0 + P], u2[:, b, 256:384], start=(i == 0), stop=(i == len(of[t]) - 1))
                    ins.then_inc(s["a_o"], 1)
                if k == 7:
                    pe.wait_ge(s["a_n"], n + 1)
                    for t in range(2):
                        ins = tr(aux[0][:, t * P:(t + 1) * P], on[:, t, :])
                    ins.then_inc(s["a_yT"], 1)

            def ffn_up(e, par, k):
                if k == 1:
                    pe.wait_ge(free_d, done_d["ffn_up"] + e + 1)
                    pe.wait_ge(s["f_lo"], e + 1)
                    for j in range(2):
                        for t in range(2):
                            ins = tr(aux[0][:, (2 * j + t) * P:(2 * j + t + 1) * P], ff[:, t, j * P:(j + 1) * P])
                    ins.then_inc(s["f_T"], 1)

            pe.sem_inc(s["f_T"], 1)
            pe.sem_inc(s["side_sum"], 1)
            pe.wait_ge(s["loads_c"], 32)
            pe.wait_ge(s["csplit"], 2)
            for L in range(2):
                T = tokens[L]
                if L == 1:
                    pe.wait_ge(s["mg_d"], 2)
                if L == 0:
                    phase("mod0", nothing, lambda e, par, k: mod(0, e, par, k), mod_parts)
                    tail(lambda e, par, k: mod(0, e, par, k), 7, 1)
                conv_parts = rows(act_hi, act_lo, 4, [(t, main[t], 0, 512) for t in range(T)])
                ret_parts = conv_parts + rows(act_hi, act_lo, 4, [(t, main[t], 128, 384) for t in range(T, 4)])
                phase(f"in{L}_conv", norm_head(L, 4, u), lambda e, par, k: conv(L, e, k), lambda par: conv_parts)

                def ret_start(k):
                    conv(L, 7, k)
                    if k == 7:
                        pe.wait_ge(s["cv_q"], 9 * L + 9)
                        pe.wait_ge(s["cv_done"], 8 * L + 9)
                        mm(aux[0][:, 0:T * P], mat("ones"), acc[:, 0:T * P], start=True, stop=True).then_inc(s["cf_s"], 1)

                def ret_step(e, par, k):
                    if k == 1:
                        pe.wait_ge(s["cf_r"], L + 1)
                    ret(L, e, k)

                phase(f"in{L}_ret", ret_start, ret_step, lambda par: ret_parts)
                out_parts = (lambda par: rows(act_hi, act_lo, 4, [(t, main[t], 0, 512) for t in range(4)])) if L == 0 else \
                    (lambda par: rows(act_hi, act_lo, 2, [(t, main[2 * par + t], 0, 512) for t in range(2)]))

                def branch(j):
                    if L == 0 and j == 0:
                        side_total(SIDE_CHUNKS - 1, 9)
                    if L == 0 and j == 1:
                        pe.wait_ge(s["side_T"], SIDE_CHUNKS)

                phase(f"out{L}", lambda k: run_out_head(k, lambda j: ret(L, 7, j), branch, lambda b: gate_rows(L, b)), lambda e, par, k: None, out_parts, ready=lambda k: pe.wait_ge(s["p_lo_ready"], 8 * L + k + 1))
            pe.wait_ge(s["mg_d"], 3)
            two = lambda hi, lo: (lambda par: rows(hi, lo, 2, [(t, main[2 * par + t], 0, 512) for t in range(2)]))
            attn_parts = lambda par: rows(h_hi, h_lo, 2, [(t, main[2 * par + t], 0, 384) for t in range(2)])
            sb_norm = norm_head(3, 2, None)

            def sb_start(k):
                if k == 2:
                    pe.wait_ge(s["bT3"], 1)
                sb_norm(k)
                if k == 1:
                    pe.wait_ge(s["bT"], 48)
                    mm(aux[0][0:HEADS, 0:384], relb[:], onehot[:], start=True, stop=True).then_inc(s["bT2"], 1)
                if k == 7:
                    pe.wait_ge(s["mask_in"], 16)
                    pe.wait_ge(s["bT5"], 16)
                    for j in range(4):
                        mm(aux[j][:, :], amat("flip"), hankel[:, 2 * j:2 * j + 2, :].rearrange("p h n -> p (h n)"), start=True, stop=True).then_inc(s["bT2"], 1)

            def sb_step(e, par, k):
                if k == 1:
                    pe.wait_ge(s["bT3"], 5)
                attn(e, par, k, "sb")

            phase("sb", sb_start, sb_step, attn_parts)
            phase("dil", lambda k: attn(7, 1, k, "sb"), lambda e, par, k: attn(e, par, k, "dil"), attn_parts)
            tail(lambda e, par, k: attn(e, par, k, "dil"), 7, 1)
            phase("out2", nothing, lambda e, par, k: None, two(h_hi, h_lo), ready=lambda k: pe.wait_ge(s["p_lo_ready"], 16 + k + 1))
            phase("ffn_up", norm_head(5, 2, None), ffn_up, two(h_hi, h_lo))

            def down_ready(k):
                if k == 21:
                    pe.wait_ge(s["f_lo"], 23)
                elif k == 0:
                    pe.wait_ge(s["f_lo"], 22)

            phase("ffn_down", lambda k: ffn_up(21, 1, k), lambda e, par, k: None, two(f_hi, f_lo), ready=down_ready)
            gate_norm = norm_head(7, 2, None)

            def gate_start(k):
                if k < 8:
                    gate_norm(k)
                else:
                    pe.wait_ge(s["p_ready"], 1)

            phase("gate", gate_start, lambda e, par, k: None, two(h_hi, h_lo), last=True)


def kernel(**inputs):
    import concourse.bacc as bacc
    from concourse.bass_utils import run_bass_kernel_spmd

    x = {k: np.asarray(v) for k, v in inputs.items()}

    def pieces(w, groups):
        k, n = w.shape
        parts = w.reshape(k // 256, 2, P, n)
        return np.stack([parts[..., g].transpose(0, 2, 1, 3).reshape(k // 256, P, -1) for g in groups]) \
                 .reshape(-1, P, 2 * len(groups[0]))

    span = lambda a, n: np.arange(a, a + n)
    plain = lambda first, n: [span(first + 512 * c, 512) for c in range(n)]
    arrays = {}
    arrays["w_mod0"] = pieces(x["w_mod"][0], plain(0, 8))
    arrays["w_side"] = np.concatenate([pieces(x["w_mod"][0], plain(4096, 4)), pieces(x["w_mod"][1], plain(0, 12))])
    for L in range(2):
        w = x["w_in"][L]
        for half, name in ((0, "conv"), (4 * HALF, "ret")):
            arrays[f"w_in{L}_{name}"] = pieces(w, [np.concatenate([span(half + i * HALF + h * P, P) for i in range(4)]) for h in range(8)])
        arrays[f"w_out{L}"] = pieces(x["w_out"][L], plain(0, 4))
    w = x["w_in_2"][0]
    for half, name in ((0, "sb"), (3 * HALF, "dil")):
        arrays[f"w_{name}"] = pieces(w, [np.concatenate([span(half + i * HALF + h * P, P) for i in range(3)]) for h in range(8)])
    arrays["w_out2"] = pieces(x["w_out_2"][0], plain(0, 4))
    arrays["w_ffn_up"] = pieces(x["w_gate_up_2"][0], [np.concatenate([span(256 * c, 256), span(FF + 256 * c, 256)]) for c in range(22)])
    arrays["w_ffn_down"] = pieces(x["w_down_2"][0], plain(0, 4))
    arrays["w_gate"] = np.concatenate([pieces(x[n][0], plain(0, 4)).reshape(4, -1, P, 1024) for n in ("w_pli_gate_2", "w_pli_proj_2")], 1) \
                         .reshape(-1, P, 1024)
    column = lambda v: v.reshape(-1, P).T
    vec = []
    for name in COLS:
        L = int(name[-1]) if name[-1] in "01" else 0
        vec.append({
            "norm": lambda: column(x["norm_w"][L]), "bmod": lambda: column(x["b_mod"][0][:4096]),
            "bside": lambda: column(np.concatenate([x["b_mod"][0][4096:], x["b_mod"][1]])),
            "convw": lambda: column(x["conv_w"][L].reshape(-1)), "convn": lambda: column(x["conv_norm_w"][L]),
            "retn": lambda: column(x["ret_norm_w"][L]), "mixpre": lambda: column(x["ln_mix_pre_2"][0]),
            "head": lambda: column(x["ln_head_2"][0]), "ffnpre": lambda: column(x["ln_ffn_pre_2"][0]),
            "pli": lambda: column(x["ln_pli_2"][0]), "c": lambda: column(x["c"][0]), "cctx": lambda: column(x["c_ctx"]),
            "eps": lambda: np.full((P, 1), EPS, np.float32),
        }[name.rstrip("01")]())
    arrays["cols"] = np.concatenate(vec, 1)
    arrays["rows"] = np.stack([x["final_norm_w"], x["ln_mix_post_2"][0], x["ln_ffn_post_2"][0]])
    arrays["decays"] = np.stack([x["ret_decay_f"], x["ret_decay_b"]], 1).reshape(32)
    arrays["x"], arrays["ctx"] = x["x"][0], x["ctx"][0]
    arrays["pT"] = x["p_2"][0, 0].T.reshape(2, P, TOK).transpose(1, 0, 2).reshape(P, 2 * TOK)
    arrays["rel_bias"] = x["rel_bias_2"]
    for name, v in zip(("mats", "wide", "maskd", "onehot", "dadd"), shape_constants()):
        arrays[name] = v
    nc = bacc.Bacc("TRN2", target_bir_lowering=False, num_devices=1)
    send, aps = {}, {}
    for name, v in arrays.items():
        send["in_" + name] = np.ascontiguousarray(v)
        aps[name] = nc.dram_tensor("in_" + name, v.shape, mybir.dt.float32, kind="ExternalInput").ap()
    out = nc.dram_tensor("out", (TOK, D), mybir.dt.float32, kind="ExternalOutput").ap()
    build(nc, aps, out)
    r = run_bass_kernel_spmd(nc, [send], core_ids=[0])
    return r.results[0]["out"].reshape(1, TOK, D)
```

```python
import numpy as np
import concourse.bass as bass
import concourse.mybir as mybir
from contextlib import ExitStack, contextmanager

P = 128
D = 2048
KT = D // P
TOK = 256
HALF = 1024
HEADS = 8
FF = 5632
FKT = FF // P
EPS = 1e-6
SLOTS = 4
LEAD = 3
SIDE_SLOTS = 2
SIDE_CHUNKS = 16
PHASES = [
    ("mod0", 8, 8, 1024), ("in0_conv", 8, 8, 1024), ("in0_ret", 8, 8, 1024), 
    ("out0", 4, 8, 1024), ("in1_conv", 8, 8, 1024),
    ("in1_ret", 8, 8, 1024), ("out1", 4, 8, 1024), ("sb", 8, 8, 768), ("dil", 8, 8, 768),
    ("out2", 4, 8, 1024), ("ffn_up", 22, 8, 1024), ("ffn_down", 4, 22, 1024), ("gate", 4, 9, 1024),
]
BASE, SHAPE = {}, {}
_n = 0
for _name, _c, _per, _w in PHASES:
    BASE[_name], SHAPE[_name] = _n, (_c, _per, _w)
    _n += _c * _per
PIECES = _n
LINKS = {'pool_ret': 1, 'act_in0_conv': 7, 'act_in0_ret': 7, 'act_out0': 4, 'act_in1_conv': 0, 'act_in1_ret': 0, 'act_sb': 8, 'act_dil': 8, 'act_ffn_up': 0, 'act_gate': 0, 'dve_mod0': 0, 'dve_in0_conv': 11, 'dve_in0_ret': 14, 'dve_out0': 0, 'dve_mod1': 0, 'dve_in1_conv': 6, 'dve_in1_ret': 6, 'dve_sb': 8, 'dve_dil': 10, 'dve_ffn_up': 0, 'dve_gate': 2, 'pe_mod0': 0, 'pe_in0_conv': 0, 'pe_in0_ret': 0, 'pe_out0': 0, 'pe_mod1': 0, 'pe_in1_conv': 0, 'pe_in1_ret': 0, 'pe_sb': 0, 'pe_dil': 0, 'pe_ffn_up': 0, 'pe_gate': 0}
COLS, _n = {}, 0
for _name, _w in [("norm0", 16), ("norm1", 16), ("bmod0", 32), ("bside", 64), ("convw0", 24),
                  ("convw1", 24), ("convn0", 8), ("convn1", 8), ("retn0", 8), ("retn1", 8),
                  ("mixpre", 16), ("head", 16), ("ffnpre", 16), ("pli", 16), ("c", 16),
                  ("cctx", 16), ("eps", 1)]:
    COLS[_name] = _n
    _n += _w
NCOLS = _n
MATS = ["ident", "ones"]
ATTN_MATS = ["later", "flip"]
WIDE = ["cos", "sin", "dpos", "dneg", "dscale", "dctxf", "dctxb"]


def shape_constants():
    i = np.arange(P)
    mats = {
        "ident": np.eye(P), "later": i[:, None] > i[None, :], "ones": np.ones((P, P)),
        "flip": i[:, None] + i[None, :] == P - 1,
    }
    f = 32
    inv = (np.float32(10000.0) ** (-np.arange(f, dtype=np.float32) / np.float32(f))).astype(np.float32)
    pos = np.arange(TOK)
    ang = np.stack([(pos // 64), (pos % 64)], 1).astype(np.float32)[:, :, None] * inv
    cos = np.cos(ang.astype(np.float32)).astype(np.float32)
    sin = np.sin(ang.astype(np.float32)).astype(np.float32)
    cos = np.stack([cos, cos], 2).reshape(TOK, 128)
    sin = np.stack([-sin, sin], 2).reshape(TOK, 128)
    rows = lambda a: np.concatenate([a, a], 1).reshape(2, P, 256).transpose(1, 0, 2).reshape(P, 512)
    key = (np.arange(2)[None, :, None] * P + i[:, None, None])
    q = np.arange(TOK)[None, None, :]
    d = q - key
    wide = {
        "cos": rows(cos), "sin": rows(sin), "dpos": np.maximum(d, 0), "dneg": np.maximum(-d, 0),
        "dscale": (1 + (d == 0)) * np.float32(P ** -0.5), "dctxf": q + TOK - key, "dctxb": TOK - q + key,
    }
    earlier = (key < q).astype(np.float32)
    n = np.arange(384)
    dist = 255 - n
    dd = np.maximum(dist, 0)
    big = 16 + (np.log(np.maximum(dd, 1).astype(np.float32) / np.float32(16)) / np.float32(np.log(128.0))
                * np.float32(16)).astype(np.int32)
    bucket = np.where(dd < 16, dd, np.minimum(big, 31))
    onehot = (np.arange(32)[:, None] == bucket[None, :]) & (dist >= 0)[None, :]
    times = (dist <= 128).astype(int) + (dist % 4 == 0) + (dist % 16 == 0)
    times = np.where(dist >= 0, times, 0)
    add = np.where(times > 0, np.log(np.maximum(times, 1)), -1e30)
    f32 = lambda a: np.ascontiguousarray(a, np.float32)
    return (f32(np.concatenate([mats[m] for m in MATS], 1)),
            f32(np.concatenate([wide[m].reshape(P, 512) for m in WIDE], 1)),
            f32(np.concatenate([-earlier.reshape(P, 512), earlier.reshape(P, 512)] + [mats[m] for m in ATTN_MATS], 1)),
            f32(onehot), f32(np.repeat(add[None], HEADS, 0)))


class Chain:

    def __init__(self, eng, sem):
        self.eng, self.sem, self.total, self.n, self.at = eng, sem, 0, 0, 0

    def link(self, ins):
        self.n += 1
        ins.then_inc(self.sem, 1)
        self.eng.wait_ge(self.sem, self.at + self.total + self.n)

    @contextmanager
    def turn(self, name, i, turns):
        self.total, self.n = self.total + self.n, 0
        self.at = i * LINKS.get(name, 1)
        yield
        if self.n != LINKS.get(name, 1):
            raise ValueError(f"LINKS {name} {self.n}")
        self.at, self.n, self.total = 0, 0, self.total + turns * LINKS.get(name, 1)


def over_chunks(eng, chain, key, chunks, paired, body, lag=1):
    if lag == 2:
        body(1, 1)
        pairs = (chunks - 2) // 2
        with eng.Fori(0, pairs) as i, chain.turn(key, i, pairs):
            body(2 * i + 2, 0)
            body(2 * i + 3, 1)
        return
    if not paired:
        with eng.Fori(0, chunks - 1) as i, chain.turn(key, i, chunks - 1):
            body(i + 1, 1)
        return
    pairs = (chunks - 2) // 2
    if pairs > 1:
        with eng.Fori(0, pairs) as i, chain.turn(key, i, pairs):
            body(2 * i + 1, 1)
            body(2 * i + 2, 0)
    else:
        body(1, 1)
        body(2, 0)
    body(chunks - 1, 1)


def build(nc, a, out):
    F32, F32R = mybir.dt.float32, mybir.dt.float32r
    ALU, ACT, AX = mybir.AluOpType, mybir.ActivationFunctionType, mybir.AxisListType
    ds = bass.ds
    top = ExitStack()
    sb = lambda scope, n, shape, dt=F32: scope.enter_context(nc.sbuf_tensor(n, shape, dt))
    scratch = nc.dram_tensor("bias_by_distance", [HEADS, 384], F32, kind="Internal").ap()

    with top:
        X = sb(top, "X", [P, 4 * D])
        raw = sb(top, "raw", [P, SLOTS, 1024])
        w_hi = sb(top, "w_hi", [P, SLOTS, 1024], F32R)
        w_lo = sb(top, "w_lo", [P, SLOTS, 1024], F32R)
        mats = sb(top, "mats", [P, len(MATS) * P])
        cols = sb(top, "cols", [P, NCOLS])
        ssq = sb(top, "ssq", [P, 4, 4])
        rstd = sb(top, "rstd", [P, 4])
        rstd_root = sb(top, "rstd_root", [P, 4])
        table = sb(top, "table", [P, 1])
        scale_h = sb(top, "scale_h", [P, 4])
        layer = ExitStack()
        act_hi = sb(layer, "act_hi", [P, KT * 512], F32R)
        act_lo = sb(layer, "act_lo", [P, KT * 512], F32R)
        gates = sb(layer, "gates", [P, 2, D])
        wide = sb(layer, "wide", [P, len(WIDE) * 512])
        lg = sb(layer, "lg", [P, 32])
        cvec = sb(layer, "cvec", [P, 2 * KT + P])
        c_hi = sb(layer, "c_hi", [P, 2 * KT + P], F32R)
        c_lo = sb(layer, "c_lo", [P, 2 * KT + P], F32R)
        modT = sb(layer, "modT", [P, 2, 32])
        side_raw = gates[:, 0, :].rearrange("p (s n) -> p s n", s=SIDE_SLOTS)
        side_acc = gates[:, 1, 0:1024].rearrange("p (v n) -> p v n", v=2)
        side_junk = gates[:, 1, 1024:1024 + P]
        side_cols = sb(layer, "side_cols", [P, 2, 4])
        sideT = sb(layer, "sideT", [P, 2, 64])
        mod_a = sb(layer, "mod_a", [P, 2, KT])
        u = sb(layer, "u", [P, 4, 512])
        qk = sb(layer, "qk", [P, 2, 256])
        qT = sb(layer, "qT", [P, 512])
        kT = sb(layer, "kT", [P, 512])
        sT = sb(layer, "sT", [P, 4, 256])
        rot = sT[:, 2:4, :]
        sTc = qk
        g = sT[:, :, :].rearrange("p b q -> p (b q)")[:, 0:516].rearrange("p (b n) -> p b n", b=2)
        zr = sb(layer, "zr", [P, 4, 128])
        decay = sb(layer, "decay", [P, 4, 256])
        dtmp = sb(layer, "dtmp", [P, 512])
        acc = decay[:, 0:2, :].rearrange("p b q -> p (b q)")
        stats = sb(layer, "stats", [P, 4, 6])
        mv = sb(layer, "mv", [P, 4, 2])
        root = sb(layer, "root", [P, 4])
        msb = sb(layer, "msb", [P, 512])
        layer.close()
        block2 = ExitStack()
        h_hi = sb(block2, "h_hi", [P, KT * 256], F32R)
        h_lo = sb(block2, "h_lo", [P, KT * 256], F32R)
        xs2 = sb(block2, "xs2", [P, 2, 512])
        attn = ExitStack()
        maskd = sb(attn, "maskd", [P, 2 * 512 + len(ATTN_MATS) * P])
        bias = sb(attn, "bias", [P, HEADS, 256])
        hankel = sb(attn, "hankel", [P, HEADS, 256])
        onehot = sb(attn, "onehot", [32, 384])
        relb = sb(attn, "relb", [32, HEADS])
        dadd = sb(attn, "dadd", [HEADS, 384])
        ext = sb(attn, "ext", [HEADS, 384])
        mixrow = sb(attn, "mixrow", [P, D])
        u2s = sb(attn, "u2", [P, 2, 2, 384])
        qkT = sb(attn, "qkT", [P, 512])
        t1 = sb(attn, "t1", [P, 512])
        t2 = sb(attn, "t2", [P, 512])
        t3 = sb(attn, "t3", [P, 512])
        t4 = sb(attn, "t4", [P, 512])
        aT = sb(attn, "aT", [P, 512])
        on = sb(attn, "on", [P, 2, 128])
        rsums = sb(attn, "rsum", [P, 2, 2])
        hjunk = sb(attn, "hjunk", [P, P])
        hsq = sb(attn, "hsq", [P, 2])
        hroot = sb(attn, "hroot", [P, 2])
        hr = sb(attn, "hr", [P, 2])
        rmax = sb(attn, "rmax", [P, 2])
        attn.close()
        ffn = ExitStack()
        f_hi = sb(ffn, "f_hi", [P, FKT * 256], F32R)
        f_lo = sb(ffn, "f_lo", [P, FKT * 256], F32R)
        ffn.close()
        pli = ExitStack()
        sig = sb(pli, "sig", [P, 2, 512])
        ptok = sb(pli, "ptok", [P, 2 * 256])
        p_hi = sb(pli, "p_hi", [P, 2 * 256], F32R)
        p_lo = sb(pli, "p_lo", [P, 2 * 256], F32R)
        pli.close()
        block2.close()
        late = ExitStack()
        frow = sb(late, "frow", [P, D])
        late.close()
        fs = xs2[:, 0, :].rearrange("p (t n) -> p t n", t=2)
        ff = xs2[:, 1, :].rearrange("p (t n) -> p t n", t=2)

        main = [top.enter_context(nc.psum_tensor(f"main{i}", [P, 512], F32)) for i in range(4)]
        aux = [top.enter_context(nc.psum_tensor(f"aux{i}", [P, 512], F32)) for i in range(4)]

        S = {}

        def sem(name):
            if name not in S:
                S[name] = top.enter_context(nc.semaphore(name))
            return S[name]

        raw_in = [sem(f"raw_in{i}") for i in range(SLOTS)]
        side_in = [sem(f"side_in{i}") for i in range(SIDE_SLOTS)]
        hi_split, lo_split = sem("hi_split"), sem("lo_split")
        eaten = sem("eaten")
        free_a, free_d = sem("free_a"), sem("free_d")
        for n in ("side_col half_a half_d side_used side_sum side_T loads_c loads_p act_chain dve_chain pool_chain "
                  "consts lgx lgd cx csplit md_T md_d mg_s mg_d norm_sum norm_root norm_rstd xs_a xs_d tmp_a tmp_d "
                  "wide_in xT_ready h_hi_ready h_ready loads_x cv_y cv_q cv_done cf_s cf_q cf_r y_scaled "
                  "p_hi_ready p_lo_ready rt_dz rt_e rt_ec stats_done msb_read act_pause rt_D rt_rope rt_z rt_T "
                  "rt_qa rt_kd rt_s rt_sT rt_o rt_v rt_sq rt_n rt_yT rt_y out_x x_in gate_row x_grp pre_sq mask_in "
                  "bT bT2 bT3 bT4 bT5 mix_in fr_in pt_in p_ready px_h a_T a_qk a_z s_l s_lk s_lat s_s s_e a_aT a_o "
                  "a_sq a_n a_yT a_y d_L d_p d_pT d_r f_T f_hi f_lo gt_x stored ssq0 out_sq").split():
            sem(n)
        s = S

        mat = lambda n: mats[:, MATS.index(n) * P:(MATS.index(n) + 1) * P]
        amat = lambda n: maskd[:, 1024 + ATTN_MATS.index(n) * P:1024 + (ATTN_MATS.index(n) + 1) * P]
        wd = lambda n: wide[:, WIDE.index(n) * 512:(WIDE.index(n) + 1) * 512]
        wd3 = lambda n: wd(n).rearrange("p (b q) -> p b q", b=2)
        col = lambda n, j=0: cols[:, ds(COLS[n] + j, 1)]
        colv = lambda n, w: cols[:, COLS[n]:COLS[n] + w]
        x3 = X[:, :].rearrange("p (t d) -> p t d", t=4)
        rr = X[:, 2 * D:4 * D].rearrange("p (t d) -> p t d", t=2)
        y_of = [X[:, :].rearrange("p (k n) -> p k n", n=512),
                X[:, 2 * D:4 * D].rearrange("p (k n) -> p k n", n=256)]
        tokens = [4, 2]

        by_act = {"in0_conv", "in0_ret", "in1_conv", "in1_ret", "sb", "dil", "out2", "ffn_up", "ffn_down", "gate"}
        done_a, done_d, na, nd = {}, {}, 1, 1
        for name, c, per, w in PHASES:
            done_a[name], done_d[name] = na, nd
            nd += c
            na += c if name in by_act else 0
        bank_by_bank = {"in0_conv": (0, 0), "in0_ret": (8, 8), "out0": (16, 16), "in1_conv": (16, 28), "in1_ret": (24, 36)}
        paired = {n: n not in ("in0_conv", "in0_ret", "in1_ret", "out0") for n, *_ in PHASES}

        def chunk_end(name, c):
            return BASE[name] + (c + 1) * SHAPE[name][1]

        xs4 = [qk[:].rearrange("p t n -> p (t n)"), qT[:], kT[:], dtmp[:]]

        def conv_bank(L, par, i):
            return (main[i], 0) if L == 0 else (main[2 * par + i % 2], 256 * (i // 2))

        def conv_psum(L, par, i):
            bank, c0 = conv_bank(L, par, i)
            return bank[:, c0:c0 + tokens[L] * P]

        def squares(W):
            return qk[:].rearrange("p t n -> p (t n)")[:, 0:W]

        def act_hi_scratch():
            return act_hi[:, 0:D]

        def prep_index(n):
            return {0: 0, 1: 1, 3: 2, 5: 3, 7: 4}[n]

        def norm_groups(k):
            return {0: (0, 1), 2: (2,), 4: (3,)}.get(k, ())

        def norm_bank(T, kg, kk):
            if T == 4:
                return aux[kk], 0
            return aux[2 * (kg % 2) + kk // 2], 256 * (kk % 2)

        out_head = {0: ["r0", 0, 1, "r1"], 1: ["r2", 2, "r3"], 2: [3, "r4", "r5"], 3: ["r6", "r7"],
                    4: [4, 5, "g0"], 5: ["g1"], 6: [6], 7: [7]}

        def run_out_head(k, ret, split, gate):
            for what in out_head[k]:
                if isinstance(what, int):
                    split(what)
                elif what[0] == "r":
                    ret(int(what[1]))
                else:
                    gate(int(what[1]))

        def head_steps(front, back, name, e, par, k):
            front(name, e, par, k)
            if isinstance(e, int) and e == 0:
                if name == "dil":
                    back("sb", 7, 1, k)
            else:
                back(name, e - 1, 1 - par, k)

        def last_head(front, back, split, k):
            todo = {0: ["f0", "s0", "f1", "s1"], 1: ["f2", "s2"], 2: ["f3", "s3"], 3: ["f4", "s4"], 4: ["f5", "f6", "s5"],
                    5: ["f7", "b3", "s6"], 6: ["b4", "b5"], 7: ["b7", "s7"]}[k]
            for what in todo:
                j = int(what[1])
                if what[0] == "f":
                    head_steps(front, back, "dil", 7, 1, j)
                elif what[0] == "b":
                    back("dil", 7, 1, j)
                else:
                    split(j)

        block = top.enter_context(nc.Block())

        side_first = {"in0_conv": 0, "in0_ret": 64}

        @block.sync
        def _(sp):
            for name, chunks, per, w in PHASES:
                def fetch(group, slot):
                    n = BASE[name] // SLOTS + group
                    if not (isinstance(n, int) and n == 0):
                        sp.wait_ge(lo_split, SLOTS * n + slot - SLOTS + 1)
                    sp.dma_start(raw[:, slot, 0:w], a["w_" + name][SLOTS * group + slot, :, :]).then_inc(raw_in[slot], 16)
                    if name in side_first or (name == "out0" and isinstance(group, int)):
                        g = group + side_first.get(name, 8 * SIDE_CHUNKS) // SLOTS - 1
                        if isinstance(g, int) and (g < 0 or g >= 2 * SIDE_CHUNKS):
                            return
                        side_slot = slot % SIDE_SLOTS
                        if not (isinstance(g, int) and g == 0 and slot < SIDE_SLOTS):
                            sp.wait_ge(s["side_used"], SLOTS * g + slot + 2)
                        sp.dma_start(side_raw[:, side_slot, :], a["w_side"][SLOTS * g + slot, :, :]).then_inc(side_in[side_slot], 16)

                groups = chunks * per // SLOTS
                for slot in range(SLOTS):
                    fetch(0, slot)
                if groups > 1:
                    with sp.Fori(1, groups) as i:
                        for slot in range(SLOTS):
                            fetch(i, slot)

            for c in range(4):
                for t in range(2):
                    sp.wait_ge(s["gt_x"], 2 * c + t + 1)
                    sp.dma_start(out[t * P:(t + 1) * P, c * 512:(c + 1) * 512], x3[:, t, c * 512:(c + 1) * 512]).then_inc(s["stored"], 16)
            sp.wait_ge(s["stored"], 128)

        @block.gpsimd
        def _(pool):
            ch = Chain(pool, s["pool_chain"])
            pool.dma_start(cols[:], a["cols"]).then_inc(s["loads_c"], 16)
            pool.dma_start(mats[:], a["mats"]).then_inc(s["loads_c"], 16)
            pool.dma_start(lg[:], a["decays"].partition_broadcast(P)).then_inc(s["loads_p"], 16)
            pool.dma_start(x3[:, 0:2, :], a["x"].rearrange("(t p) d -> p t d", p=P)).then_inc(s["loads_x"], 16)
            pool.dma_start(x3[:, 2:4, :], a["ctx"].rearrange("(t p) d -> p t d", p=P)).then_inc(s["loads_x"], 16)
            for L in range(2):
                T = tokens[L]
                W = T * P
                Y = y_of[L]
                if L == 1:
                    pool.wait_ge(s["rt_y"], 9)
                ch.link(nc.gpsimd.memset(g[:, :, 0:1], 0.0))
                ch.link(nc.gpsimd.memset(g[:, :, 257:258], 0.0))
                nc.gpsimd.memset(acc[:], 0.0).then_inc(s["cv_q"], 1)
                pool.wait_ge(s["cv_q"], 9 * L + 1)
                if L == 0:
                    pool.wait_ge(s["eaten"], 72)
                    pool.dma_start(wide[:], a["wide"]).then_inc(s["wide_in"], 16)
                with pool.Fori(0, 8) as e, ch.turn("pool_conv", e, 8):
                    pool.wait_ge(s["cv_y"], 8 * L + e + 1)
                    ch.link(nc.gpsimd.tensor_tensor(out=squares(W), in0=kT[:, 0:W], in1=kT[:, 0:W], op=ALU.mult))
                    nc.gpsimd.tensor_tensor(out=acc[:, 0:W], in0=acc[:, 0:W], in1=squares(W), op=ALU.add).then_inc(s["cv_q"], 1)
                    pool.wait_ge(s["cv_q"], 9 * L + e + 2)
                pool.wait_ge(s["cf_r"], L + 1)
                for j in range(8):
                    nc.gpsimd.tensor_tensor(out=Y[:, j, :], in0=Y[:, j, :], in1=msb[:, 0:W], op=ALU.mult).then_inc(s["y_scaled"], 1)
                if L == 0:
                    pool.wait_ge(s["wide_in"], 16)
                with pool.Fori(0, 8) as e, ch.turn("pool_ret", e, 8):
                    dflat = decay[:].rearrange("p b q -> p (b q)")
                    pool.wait_ge(s["rt_e"], 8 * L + e + 1)
                    nc.gpsimd.tensor_tensor(out=dflat[:, 512:1024], in0=dflat[:, 512:1024], in1=dtmp[:], op=ALU.mult).then_inc(s["rt_dz"], 1)
                    pool.wait_ge(s["rt_dz"], 8 * L + e + 1)
                    ch.link(nc.gpsimd.tensor_tensor(out=dflat[:, 512:1024], in0=dflat[:, 512:1024], in1=wd("dscale"), op=ALU.mult))
                    pool.wait_ge(s["rt_ec"], 8 * L + e + 1)
                    nc.gpsimd.tensor_tensor(out=dflat[:, 0:512], in0=dflat[:, 0:512], in1=dtmp[:], op=ALU.add).then_inc(s["rt_D"], 1)
                    pool.wait_ge(s["rt_D"], 8 * L + e + 1)
                if L == 0:
                    pool.wait_ge(s["p_lo_ready"], 8)
                    pool.wait_ge(s["p_hi_ready"], 8)
                    pool.dma_start(x3[:, 0:2, :], a["x"].rearrange("(t p) d -> p t d", p=P)).then_inc(s["x_in"], 16)
                    pool.dma_start(x3[:, 2:4, :], a["ctx"].rearrange("(t p) d -> p t d", p=P)).then_inc(s["x_in"], 16)
                    pool.wait_ge(s["out_x"], 16)
                    pool.dma_start(gates[:, 1, :], a["rows"][0, :].partition_broadcast(P)).then_inc(s["gate_row"], 16)
            pool.wait_ge(s["eaten"], chunk_end("out1", 3))
            pool.dma_start(onehot[:], a["onehot"]).then_inc(s["bT"], 16)
            pool.dma_start(relb[:], a["rel_bias"]).then_inc(s["bT"], 16)
            pool.dma_start(dadd[:], a["dadd"]).then_inc(s["bT"], 16)
            pool.dma_start(maskd[:], a["maskd"]).then_inc(s["mask_in"], 16)
            pool.wait_ge(s["x_grp"], 4)
            pool.dma_start(mixrow[:], a["rows"][1, :].partition_broadcast(P)).then_inc(s["mix_in"], 16)
            pool.wait_ge(s["bT3"], 1)
            pool.dma_start(scratch, ext[:]).then_inc(s["bT4"], 16)
            pool.wait_ge(s["bT4"], 16)
            pool.dma_start(hankel[:], bass.AP(tensor=scratch.tensor, offset=0, ap=[[1, P], [384, HEADS], [1, 256]])).then_inc(s["bT5"], 16)
            pool.wait_ge(s["eaten"], chunk_end("ffn_up", 21))
            pool.dma_start(frow[:], a["rows"][2, :].partition_broadcast(P)).then_inc(s["fr_in"], 16)
            pool.wait_ge(s["eaten"], chunk_end("ffn_down", 3))
            pool.dma_start(ptok[:], a["pT"]).then_inc(s["pt_in"], 16)

        @block.scalar
        def _(act):
            ch = Chain(act, s["act_chain"])
            A = nc.scalar.activation

            def pause():
                act.sem_inc(s["act_pause"], 1)

            def split(p, slot):
                if isinstance(p, int) and p >= PIECES:
                    return
                act.wait_ge(raw_in[slot], 16 * ((p - slot) // SLOTS) + 16 if isinstance(p, int) else 4 * (p - slot) + 16)
                if not (isinstance(p, int) and p < SLOTS):
                    act.wait_ge(eaten, p - SLOTS + 1)
                A(w_hi[:, slot, :], raw[:, slot, :], ACT.Copy).then_inc(hi_split, 1)

            def phase(name, head, epi, last=False):
                chunks, per, _ = SHAPE[name]
                base = BASE[name]

                def body(c, cs, step):
                    for k in range(per):
                        step(k)
                        if k == 0 and (name == "in0_ret" or name == "in0_conv" and cs > 0):
                            side_columns(side_first[name] // 8 + c - 1)
                        split(base + c * per + LEAD + k, (base + (c if isinstance(c, int) else cs) * per + LEAD + k) % SLOTS)

                body(0, 0, head)
                if epi and last:
                    for c in range(1, chunks):
                        body(c, c % 2, lambda k: epi(c - 1, (c - 1) % 2, k))
                elif epi:
                    over_chunks(act, ch, "act_" + name, chunks, paired[name],
                                lambda c, par: body(c, par, lambda k: epi(c - 1, 1 - par, k)), lag=2 if name in ("sb", "dil") else 1)
                else:
                    for c in range(1, chunks):
                        body(c, c, first_squares if c == chunks - 1 else nothing)

            def side_columns(chunk):
                act.wait_ge(s["side_sum"], chunk + 2)
                act.wait_ge(s["side_T"], chunk + 1)
                for v in range(2):
                    for j in range(4):
                        ins = A(side_junk, aux[2 + v][:, j * P:(j + 1) * P], ACT.Copy, accum_out=side_cols[:, v, j:j + 1])
                        if v + j < 4:
                            ch.link(ins)
                ins.then_inc(s["side_col"], 1)

            def first_squares(k):
                if k == 0:
                    act.wait_ge(s["loads_x"], 32)
                    act.wait_ge(s["ssq0"], 1)
                if k < 4:
                    ch.link(A(act_hi_scratch(), x3[:, k, :], ACT.Square, accum_out=ssq[:, k, 0:1]))
                    act.sem_inc(s["out_sq"], 1)

            nothing = lambda k: None

            def sqrt_table():
                ch.link(A(table[:], col("eps"), ACT.Sqrt))

            def norm_root(n, T, scale=1.0 / D):
                act.wait_ge(s["norm_sum"], n + 1)
                A(rstd_root[:, 0:T], rstd[:, 0:T], ACT.Sqrt, bias=col("eps"), scale=scale).then_inc(s["norm_root"], 1)

            def norm_xs(m, kg):
                if m > 0:
                    act.wait_ge(s["xT_ready"], m)
                for t in range(2):
                    ins = A(xs4[t], x3[:, t, kg * 512:(kg + 1) * 512], ACT.Copy, scale=rstd[:, t:t + 1])
                ins.then_inc(s["xs_a"], 1)

            def norm_step(n, L, A_cols, B_cols, kg):
                m = 4 * L + kg
                if kg == 0:
                    act.wait_ge(s["norm_rstd"], n + 1)
                    norm_xs(m, 0)
                    act.wait_ge(s["consts"], L + 1)
                act.wait_ge(s["xT_ready"], m + 1)
                if m > 0:
                    act.wait_ge(s["h_ready"], m)
                for kk in range(2):
                    for b in range(2):
                        ins = A(u[:, kk, b * 256:(b + 1) * 256], aux[kk][:, b * 256:(b + 1) * 256], ACT.Identity,
                                scale=A_cols(b, 4 * kg + kk), bias=B_cols(b, 4 * kg + kk))
                ins.then_inc(s["tmp_a"], 1)
                if kg < 3:
                    norm_xs(m + 1, kg + 1)
                act.wait_ge(s["tmp_a"], m + 1)
                act.wait_ge(s["tmp_d"], m + 1)
                A(act_hi[:, kg * 2048:(kg + 1) * 2048], u[:].rearrange("p t n -> p (t n)"), ACT.Copy).then_inc(s["h_hi_ready"], 1)

            a_layer = lambda b, kt: mod_a[:, b, kt:kt + 1]
            b_layer = lambda b, kt: (modT[:, b, kt:kt + 1] if L == 0 else sideT[:, b, 16 + kt:17 + kt])

            def prepare(n, A_cols, k):
                j = prep_index(n) - 2
                for kg in norm_groups(k):
                    m = 4 * prep_index(n) + kg
                    act.wait_ge(s["xT_ready"], m + 1)
                    for kk in range(4):
                        kt = 4 * kg + kk
                        bank, c0 = norm_bank(2, kg, kk)
                        ins = A(h_hi[:, kt * 256:(kt + 1) * 256], bank[:, c0:c0 + 256], ACT.Copy, scale=A_cols(0, kt))
                    ins.then_inc(s["h_hi_ready"], 1)
                for kg in {1: (0, 1), 3: (2,), 5: (3,)}.get(k, ()):
                    act.wait_ge(s["x_grp"], 4 * j + kg + 1)
                    for t in range(2):
                        ch.link(A(xs2[:, t, :], x3[:, t, kg * 512:(kg + 1) * 512], ACT.Square, accum_out=ssq[:, t, kg:kg + 1]))
                if k == 5:
                    act.sem_inc(s["pre_sq"], 1)
                if k == 6:
                    norm_root(n, 2)

            def conv(L, e, par, k):
                W = tokens[L] * P
                if k == 0:
                    act.wait_ge(eaten, chunk_end(f"in{L}_conv", e))
                    act.wait_ge(s["cv_done"], 8 * L + e + 1)
                    A(qT[:, 0:W], conv_psum(L, par, 0), ACT.Copy).then_inc(s["half_a"], 1)
                    A(zr[:].rearrange("p t n -> p (t n)")[:, 0:W], conv_psum(L, par, 2), ACT.Silu).then_inc(free_a, 1)

            def conv_root(L):
                act.wait_ge(s["cf_s"], L + 1)
                A(dtmp[:, 0:tokens[L] * P], aux[0][:, 0:tokens[L] * P], ACT.Sqrt, bias=col("eps"), scale=1.0 / HALF).then_inc(s["cf_q"], 1)

            def ret(L, e, k):
                T = tokens[L]
                if k == 0:
                    act.wait_ge(eaten, chunk_end(f"in{L}_ret", e))
                    act.wait_ge(s["rt_y"], 8 * L + e + 1)
                    for t in range(0, 4, 2):
                        lo, n = (128, 256) if t >= T else (0, 512)
                        ins = A(u[:, t, lo:lo + n], main[t][:, lo:lo + n], ACT.Copy)
                        if t == 0:
                            ins.then_inc(s["half_a"], 1)
                    ins.then_inc(free_a, 1)
                if k == 1:
                    act.wait_ge(free_d, done_d[f"in{L}_ret"] + e + 1)
                    act.wait_ge(free_a, done_a[f"in{L}_ret"] + e + 1)
                    A(zr[:, 0:T, :], u[:, 0:T, 384:512], ACT.Silu).then_inc(s["rt_z"], 1)
                    h = 16 * L + e
                    act.wait_ge(s["rt_sT"], 8 * L + e + 1)
                    dflat = decay[:].rearrange("p b q -> p (b q)")
                    pause()
                    A(dflat[:, 512:1024], wd("dpos"), ACT.Exp, scale=lg[:, ds(h, 1)])
                    A(dtmp[:], wd("dneg"), ACT.Exp, scale=lg[:, ds(h + 8, 1)]).then_inc(s["rt_e"], 1)
                    A(dflat[:, 0:512], wd("dctxf"), ACT.Exp, scale=lg[:, ds(h, 1)])
                    act.wait_ge(s["rt_dz"], 8 * L + e + 1)
                    pause()
                    A(dtmp[:], wd("dctxb"), ACT.Exp, scale=lg[:, ds(h + 8, 1)]).then_inc(s["rt_ec"], 1)
                if k == 2:
                    act.wait_ge(s["rt_T"], 8 * L + e + 1)
                    A(qT[:, 0:T * P], aux[0][:, 0:T * P], ACT.Copy).then_inc(s["rt_qa"], 1)
                if k == 6:
                    act.wait_ge(s["rt_v"], 8 * L + e + 1)
                    A(root[:, 0:T], mv[:, 0:T, 1], ACT.Sqrt, bias=col("eps")).then_inc(s["rt_sq"], 1)

            def split_step(n, hi, src, W, k):
                A(hi[:, 2 * k * W:2 * (k + 1) * W], src(k), ACT.Copy).then_inc(s["p_hi_ready"], 1)

            def out_layer(L, e, k):
                T = tokens[L]
                if k == 1:
                    for t in range(T):
                        act.wait_ge(s["out_x"], 16 * L + T * e + t + 1)
                        pause()
                        ch.link(A(msb[:], x3[:, t, ds(e * 512, 512)], ACT.Square, accum_out=ssq[:, t, ds(e, 1)]))
                if k == 2:
                    act.sem_inc(s["out_sq"], 1)

            def front(name, e, par, k):
                n = e + (8 if name == "dil" else 0)
                if k == 0:
                    act.wait_ge(s["norm_rstd"], 4)
                    if not (isinstance(n, int) and n == 0):
                        act.wait_ge(s["a_y"], n)
                    act.wait_ge(eaten, chunk_end(name, e))
                    A(u2s[:, par, 0, :], main[2 * par][:, 0:384], ACT.Copy, scale=scale_h[:, 0:1]).then_inc(free_a, 1)
                if k == 1:
                    act.wait_ge(s["a_T"], n + 1)
                    A(qkT[:], aux[0][:, :], ACT.Copy).then_inc(s["a_qk"], 1)
                if name == "sb":
                    if k == 2:
                        act.wait_ge(s["a_z"], e + 1)
                        ch.link(A(t1[:], aux[1][:, :], ACT.Abs, scale=P ** -0.5))
                        ch.link(A(t1[:], t1[:], ACT.Exp, scale=-1.0))
                    if k == 3:
                        A(t1[:], t1[:], ACT.Ln, bias=1.0).then_inc(s["s_l"], 1)
                elif k == 4:
                    act.wait_ge(s["d_L"], e + 1)
                    ch.link(A(t2[:, 0:256], t1[:, 0:256], ACT.Exp, bias=rmax[:, 0:1], accum_out=rsums[:, par, 0:1]))
                    ch.link(A(t2[:, 256:384], t1[:, 256:384], ACT.Exp, bias=rmax[:, 1:2], accum_out=rsums[:, par, 1:2]))
                    act.sem_inc(s["d_p"], 1)

            def back(name, e, par, k):
                n = e + (8 if name == "dil" else 0)
                if k == 1 and name == "sb":
                    act.wait_ge(s["s_s"], e + 1)
                    A(t3[:], t3[:], ACT.Exp).then_inc(s["s_e"], 1)
                if k == 4:
                    act.wait_ge(s["a_o"], n + 1)
                    if name == "dil":
                        act.wait_ge(s["d_r"], e + 1)
                    for t in range(2):
                        sc = rsums[:, par, t:t + 1] if name == "dil" else 1.0
                        ch.link(A(hjunk[:], aux[3][:, t * P:(t + 1) * P], ACT.Square, scale=sc, accum_out=hsq[:, t:t + 1]))
                    A(hroot[:], hsq[:], ACT.Sqrt, bias=col("eps"), scale=1.0 / P).then_inc(s["a_sq"], 1)

            def plain_out(name, e, par, k):
                if k == 0:
                    act.wait_ge(free_a, done_a[name] + e)
                    act.wait_ge(eaten, chunk_end(name, e))
                    for t in range(2):
                        pause()
                        ins = A(xs2[:, t, :], main[2 * par + t][:, :], ACT.Square, accum_out=ssq[:, t, ds(e, 1)])
                    ins.then_inc(free_a, 1)

            def ffn_up(e, par, k):
                if k == 0:
                    act.wait_ge(eaten, chunk_end("ffn_up", e))
                    act.wait_ge(s["norm_rstd"], 6)
                    act.wait_ge(s["f_T"], e + 1)
                    for t in range(2):
                        ins = A(fs[:, t, :], main[2 * par + t][:, 0:256], ACT.Silu, scale=scale_h[:, t:t + 1])
                    ins.then_inc(free_a, 1)
                if k == 2:
                    act.wait_ge(s["f_T"], e + 2)
                    pause()
                    A(f_hi[:, ds(e * 512, 512)], aux[0][:, :], ACT.Copy).then_inc(s["f_hi"], 1)

            def gate(e, par, k):
                if k == 0:
                    act.wait_ge(s["norm_rstd"], 8)
                    act.wait_ge(eaten, chunk_end("gate", e))
                    if e > 0:
                        act.wait_ge(s["gt_x"], 2 * e)
                    for t in range(2):
                        ins = A(sig[:, t, :], main[2 * par + t][:, :], ACT.Sigmoid, scale=scale_h[:, t:t + 1])
                    ins.then_inc(free_a, 1)

            act.sem_inc(free_a, 1)
            for p in range(LEAD):
                split(p, p)
            act.wait_ge(s["loads_c"], 32)
            act.wait_ge(s["cx"], 1)
            ch.link(A(cvec[:, 0:2 * KT], msb[:, 0:32], ACT.Silu))
            ch.link(A(c_hi[:], cvec[:], ACT.Copy))
            act.sem_inc(s["csplit"], 1)
            act.wait_ge(s["loads_p"], 16)
            A(lg[:], lg[:], ACT.Exp).then_inc(s["lgx"], 1)

            norm = 0
            for L in range(2):
                T = tokens[L]
                if L == 0:
                    phase("mod0", nothing, None)
                norm_root(norm, 4)
                act.wait_ge(s["lgd"], 1)
                phase(f"in{L}_conv", lambda k: [norm_step(norm, L, a_layer, b_layer, kg) for kg in norm_groups(k)],
                      lambda e, par, k: conv(L, e, par, k))

                def ret_start(k):
                    conv(L, 7, 1, k)
                    if k == 7:
                        conv_root(L)
                        act.wait_ge(s["wide_in"], 16)

                phase(f"in{L}_ret", ret_start, lambda e, par, k: ret(L, e, k))
                Y, W = y_of[L], T * P

                def branch(k, L=L, Y=Y, W=W):
                    if k == 0:
                        if L == 0:
                            side_columns(SIDE_CHUNKS - 1)
                        act.wait_ge(s["y_scaled"], 8 * L + 8)
                    if k == 4:
                        act.wait_ge(s["rt_y"], 8 * L + 9)
                    split_step(L, act_hi, lambda k: Y[:, 2 * k:2 * k + 2, :].rearrange("p a n -> p (a n)"), W, k)

                phase(f"out{L}", lambda k: run_out_head(k, lambda j: ret(L, 7, j), branch, nothing), lambda e, par, k: out_layer(L, e, k))
                sqrt_table()
                for k in range(3):
                    out_layer(L, 3, k)
                norm += 1
            norm_root(2, 2)
            ln = lambda name: (lambda b, kt: col(name, kt))
            phase("sb", lambda k: prepare(3, ln("mixpre"), k), lambda e, par, k: head_steps(front, back, "sb", e, par, k))
            phase("dil", lambda k: head_steps(front, back, "sb", 7, 1, k), lambda e, par, k: head_steps(front, back, "dil", e, par, k))
            O = y_of[1]

            def heads(k):
                act.wait_ge(s["a_y"], 2 * k + 3)
                split_step(2, h_hi, lambda k: O[:, 2 * k:2 * k + 2, :].rearrange("p a n -> p (a n)"), 256, k)

            phase("out2", lambda k: last_head(front, back, heads, k), lambda e, par, k: plain_out("out2", e, par, k))
            sqrt_table()
            plain_out("out2", 3, 1, 0)
            norm_root(4, 2)
            phase("ffn_up", lambda k: prepare(5, ln("ffnpre"), k), ffn_up)
            phase("ffn_down", lambda k: ffn_up(21, 1, k), lambda e, par, k: plain_out("ffn_down", e, par, k))
            sqrt_table()
            plain_out("ffn_down", 3, 1, 0)
            norm_root(6, 2)

            def gate_start(k):
                prepare(7, ln("pli"), k)
                if k == 5:
                    act.wait_ge(s["pt_in"], 16)
                    A(p_hi[:], ptok[:], ACT.Copy).then_inc(s["px_h"], 1)

            phase("gate", gate_start, gate, last=True)
            gate(3, 1, 0)

        @block.vector
        def _(dve):
            ch = Chain(dve, s["dve_chain"])
            V = nc.vector

            def split(p, slot):
                if isinstance(p, int) and p >= PIECES:
                    return
                dve.wait_ge(hi_split, p + 1)
                V.tensor_tensor(out=w_lo[:, slot, :], in0=raw[:, slot, :], in1=w_hi[:, slot, :].bitcast(F32), op=ALU.subtract).then_inc(lo_split, 1)

            def phase(name, head, epi, last=False):
                chunks, per, _ = SHAPE[name]
                base = BASE[name]

                def body(c, cs, step):
                    for k in range(per):
                        step(k)
                        if k == 0 and (name == "in0_ret" or name == "in0_conv" and cs > 0):
                            side_end(side_first[name] // 8 + c - 1)
                        split(base + c * per + LEAD + k, (base + (c if isinstance(c, int) else cs) * per + LEAD + k) % SLOTS)
                        if name in side_first:
                            side_piece(side_first[name] // 8 + c, k)

                body(0, 0, head)
                if epi and last:
                    for c in range(1, chunks):
                        body(c, c % 2, lambda k: epi(c - 1, (c - 1) % 2, k))
                elif epi:
                    over_chunks(dve, ch, "dve_" + name, chunks, paired[name],
                                lambda c, par: body(c, par, lambda k: epi(c - 1, 1 - par, k)), lag=2 if name in ("sb", "dil") else 1)
                else:
                    for c in range(1, chunks):
                        body(c, c, lambda k: None)

            nothing = lambda k: None

            def tail(epi, e, par, per=8):
                for k in range(per):
                    epi(e, par, k)

            def mod(L, e, par, k):
                if k == 0:
                    dve.wait_ge(eaten, chunk_end("mod0", e))
                    V.tensor_copy(out=msb[0:2, :], in_=main[2 * par][0:2, :]).then_inc(free_d, 1)
                if k == 2:
                    dve.wait_ge(s["md_T"], 8 * L + e + 1)
                    V.tensor_tensor(out=modT[:, :, ds(4 * e, 4)], in0=aux[0][:, 0:8].rearrange("p (k b) -> p b k", b=2),
                                    in1=cols[:, ds(COLS[f"bmod0"] + 4 * e, 4)].unsqueeze(1).to_broadcast([P, 2, 4]), op=ALU.add).then_inc(s["md_d"], 1)

            def gate_rows(L, b):
                if b < 2 - L:
                    dve.wait_ge(s["mg_s"], 2 * L + b + 1)
                    for c in range(4):
                        ins = V.tensor_copy(out=gates[:, b, 512 * c:512 * (c + 1)], in_=aux[c][:, :])
                    ins.then_inc(s["mg_d"], 1)
                    dve.wait_ge(s["mg_d"], 2 * L + b + 1)

            def side_piece(chunk, k):
                m = 8 * chunk + k
                dve.wait_ge(s["side_used"], m + 3)
                dve.wait_ge(side_in[k % SIDE_SLOTS], 8 * (m - k % SIDE_SLOTS) + 16)
                if k == 0:
                    dve.wait_ge(s["side_sum"], chunk + 1)
                for j in range(2):
                    for v in range(2):
                        w, cs = side_raw[:, k % SIDE_SLOTS, j * 512:(j + 1) * 512], cvec[:, 4 * k + 2 * j + v:4 * k + 2 * j + v + 1]
                        if k == 0 and j == 0:
                            ins = V.tensor_scalar(out=side_acc[:, v, :], in0=w, scalar1=cs, scalar2=None, op0=ALU.mult)
                        else:
                            ins = V.scalar_tensor_tensor(out=side_acc[:, v, :], in0=w, scalar=cs, in1=side_acc[:, v, :], op0=ALU.mult, op1=ALU.add)
                    if j == 0:
                        ch.link(ins)
                ins.then_inc(s["side_used"], 1)

            def side_end(chunk):
                dve.wait_ge(s["side_col"], chunk + 1)
                V.tensor_tensor(out=sideT[:, :, ds(4 * chunk, 4)], in0=side_cols[:],
                                in1=cols[:, ds(COLS["bside"] + 4 * chunk, 4)].unsqueeze(1).to_broadcast([P, 2, 4]), op=ALU.add).then_inc(s["side_T"], 1)

            def norm_sum(n, T, to):
                V.tensor_reduce(out=rstd[:, 0:T], in_=ssq[:, 0:T, :], axis=AX.X, op=ALU.add).then_inc(s["norm_sum"], 1)
                dve.wait_ge(s["norm_root"], n + 1)
                V.reciprocal(out=to[:, 0:T], in_=rstd_root[:, 0:T]).then_inc(s["norm_rstd"], 1)
                dve.wait_ge(s["norm_rstd"], n + 1)

            def layer_xs(kg):
                for t in range(2, 4):
                    ins = V.tensor_scalar(out=xs4[t], in0=x3[:, t, kg * 512:(kg + 1) * 512], scalar1=rstd[:, t:t + 1], scalar2=None, op0=ALU.mult)
                ins.then_inc(s["xs_d"], 1)

            def layer_step(L, A_cols, B_cols, kg):
                m = 4 * L + kg
                if kg == 0:
                    layer_xs(0)
                dve.wait_ge(s["xT_ready"], m + 1)
                for kk in range(2, 4):
                    for b in range(2):
                        ins = V.tensor_scalar(out=u[:, kk, b * 256:(b + 1) * 256], in0=aux[kk][:, b * 256:(b + 1) * 256],
                                              scalar1=A_cols(b, 4 * kg + kk), scalar2=B_cols(b, 4 * kg + kk), op0=ALU.mult, op1=ALU.add)
                ins.then_inc(s["tmp_d"], 1)
                if kg < 3:
                    layer_xs(kg + 1)
                dve.wait_ge(s["tmp_d"], m + 1)
                dve.wait_ge(s["h_hi_ready"], m + 1)
                cs = slice(kg * 2048, (kg + 1) * 2048)
                V.tensor_tensor(out=act_lo[:, cs], in0=u[:].rearrange("p t n -> p (t n)"), in1=act_hi[:, cs].bitcast(F32), op=ALU.subtract).then_inc(s["h_ready"], 1)
                dve.wait_ge(s["h_ready"], m + 1)

            def norm_step(n, T, tmp, hi, lo, A_cols, B_cols, kg):
                m = 4 * prep_index(n) + kg
                dve.wait_ge(s["xT_ready"], m + 1)
                dve.wait_ge(s["h_hi_ready"], m + 1)
                for kk in range(4):
                    kt = 4 * kg + kk
                    bank, c0 = norm_bank(T, kg, kk)
                    for b in range(T // 2):
                        src = bank[:, c0 + b * 256:c0 + b * 256 + 256]
                        sl = slice(kt * T * P + b * 256, kt * T * P + b * 256 + 256)
                        if B_cols:
                            ch.link(V.tensor_scalar(out=tmp[:, b * 256:b * 256 + 256], in0=src, scalar1=A_cols(b, kt), scalar2=B_cols(b, kt), op0=ALU.mult, op1=ALU.add))
                            ins = V.tensor_tensor(out=lo[:, sl], in0=tmp[:, b * 256:b * 256 + 256], in1=hi[:, sl].bitcast(F32), op=ALU.subtract)
                        else:
                            ins = V.scalar_tensor_tensor(out=lo[:, sl], in0=src, scalar=A_cols(b, kt), in1=hi[:, sl].bitcast(F32), op0=ALU.mult, op1=ALU.subtract)
                        if kk < 3 or b < T // 2 - 1:
                            ch.link(ins)
                ins.then_inc(s["h_ready"], 1)
                dve.wait_ge(s["h_ready"], m + 1)

            a_layer = lambda b, kt: mod_a[:, b, kt:kt + 1]
            b_layer = lambda b, kt: (modT[:, b, kt:kt + 1] if L == 0 else sideT[:, b, 16 + kt:17 + kt])

            def prepare(n, A_cols, new_x, k):
                def x_group(kg):
                    new_x(kg).then_inc(s["x_grp"], 1)

                def low(kg):
                    norm_step(n, 2, None, h_hi, h_lo, A_cols, None, kg)

                if k == 0:
                    x_group(0)
                    x_group(1)
                    low(0)
                    x_group(2)
                    low(1)
                    x_group(3)
                if k == 2:
                    low(2)
                if k == 4:
                    low(3)
                if k == 6:
                    dve.wait_ge(s["pre_sq"], prep_index(n) - 1)
                    norm_sum(n, 2, scale_h)

            def conv(L, e, par, k):
                T = tokens[L]
                S2, W = T // 2, T * P
                seq = lambda ap: ap.rearrange("p (b n) -> p b n", b=S2)
                y = seq(kT[:, 0:W])
                if k == 0:
                    dve.wait_ge(eaten, chunk_end(f"in{L}_conv", e))
                    V.tensor_copy(out=u[:, 1, 0:W], in_=conv_psum(L, par, 1)).then_inc(s["half_d"], 1)
                    dve.wait_ge(s["half_a"], bank_by_bank[f"in{L}_conv"][0] + e + 1)
                    dve.wait_ge(s["cv_q"], 9 * L + e + 1)
                    V.tensor_tensor(out=g[:, 0:S2, 1:257], in0=seq(qT[:, 0:W]), in1=seq(conv_psum(L, par, 3)), op=ALU.mult).then_inc(free_d, 1)
                if k == 2:
                    dve.wait_ge(free_d, done_d[f"in{L}_conv"] + e + 1)
                    ch.link(V.tensor_scalar(out=y, in0=g[:, 0:S2, 0:256], scalar1=col(f"convw{L}", e), scalar2=None, op0=ALU.mult))
                if k == 3:
                    for tap in (1, 2):
                        ch.link(V.scalar_tensor_tensor(out=y, in0=g[:, 0:S2, tap:tap + 256], scalar=col(f"convw{L}", e + 8 * tap), in1=y, op0=ALU.mult, op1=ALU.add))
                if k == 4:
                    dve.wait_ge(s["half_d"], bank_by_bank[f"in{L}_conv"][1] + e + 1)
                    V.tensor_tensor(out=kT[:, 0:W], in0=kT[:, 0:W], in1=u[:, 1, 0:W], op=ALU.mult).then_inc(s["cv_y"], 1)
                    dve.wait_ge(s["cv_y"], 8 * L + e + 1)
                    dve.wait_ge(free_a, done_a[f"in{L}_conv"] + e + 1)
                    V.scalar_tensor_tensor(out=y_of[L][:, ds(e, 1), :].rearrange("p a n -> p (a n)"), in0=kT[:, 0:W], scalar=col(f"convn{L}", e),
                                           in1=zr[:].rearrange("p t n -> p (t n)")[:, 0:W], op0=ALU.mult, op1=ALU.mult).then_inc(s["cv_done"], 1)
                    dve.wait_ge(s["cv_done"], 8 * L + e + 2)

            def conv_rstd(L):
                dve.wait_ge(s["cf_q"], L + 1)
                V.reciprocal(out=msb[:, 0:tokens[L] * P], in_=dtmp[:, 0:tokens[L] * P]).then_inc(s["cf_r"], 1)

            def ret(L, e, k):
                T = tokens[L]
                W = T * P
                n = 8 * L + e
                if k == 0:
                    dve.wait_ge(eaten, chunk_end(f"in{L}_ret", e))
                    for t in (1, 3):
                        lo, w = (128, 256) if t >= T else (0, 512)
                        ins = V.tensor_copy(out=u[:, t, lo:lo + w], in_=main[t][:, lo:lo + w])
                        if t == 1:
                            ins.then_inc(s["half_d"], 1)
                    ins.then_inc(free_d, 1)
                    dve.wait_ge(free_d, done_d[f"in{L}_ret"] + e + 1)
                    dve.wait_ge(free_a, done_a[f"in{L}_ret"] + e + 1)
                    ch.link(V.tensor_tensor(out=qk[:], in0=u[:, 0:2, 0:256], in1=wd3("cos"), op=ALU.mult))
                    halves = lambda ap: ap.rearrange("p t (a h f) -> p t a h f", a=4, h=2)
                    src, dst, sn = halves(u[:, 0:2, 0:256]), halves(rot), halves(wd3("sin"))
                    for h in range(2):
                        ch.link(V.tensor_tensor(out=dst[:, :, :, h, :], in0=src[:, :, :, 1 - h, :], in1=sn[:, :, :, h, :], op=ALU.mult))
                    V.tensor_tensor(out=qk[:], in0=qk[:], in1=rot, op=ALU.add).then_inc(s["rt_rope"], 1)
                if k == 2:
                    dve.wait_ge(s["rt_T"], n + 1)
                    V.tensor_copy(out=kT[:], in_=aux[1][:, :]).then_inc(s["rt_kd"], 1)
                if k == 3:
                    dve.wait_ge(s["rt_s"], n + 1)
                    dve.wait_ge(s["rt_D"], n + 1)
                    two = lambda b: aux[b][:, :].rearrange("p (b q) -> p b q", b=2)
                    V.scalar_tensor_tensor(out=sT[:, 0:2, :], in0=two(2), scalar=P ** -0.5, in1=decay[:, 0:2, :], op0=ALU.mult, op1=ALU.mult)
                    if L == 0:
                        V.tensor_tensor(out=sTc[:], in0=two(0), in1=decay[:, 2:4, :], op=ALU.mult)
                    V.tensor_tensor(out=sT[:, 2:4, :], in0=two(3), in1=decay[:, 2:4, :], op=ALU.mult).then_inc(s["rt_sT"], 1)
                if k == 5:
                    dve.wait_ge(s["rt_o"], n + 1)
                    for t in range(T):
                        ins = V.bn_stats(out=stats[:, t, :], in_=aux[1][:, t * P:(t + 1) * P])
                    ch.link(ins)
                    dve.sem_inc(s["stats_done"], 1)
                    for t in range(T):
                        ins = V.bn_aggr(out=mv[:, t, :], in_=stats[:, t, :])
                    ins.then_inc(s["rt_v"], 1)
                if k == 6:
                    dve.wait_ge(s["rt_v"], n + 1)
                    dve.wait_ge(s["rt_sq"], n + 1)
                    ch.link(V.reciprocal(out=root[:, 0:T], in_=root[:, 0:T]))
                    for t in range(T):
                        ins = V.tensor_scalar(out=kT[:, t * P:(t + 1) * P], in0=aux[1][:, t * P:(t + 1) * P], scalar1=mv[:, t, 0:1],
                                              scalar2=root[:, t:t + 1], op0=ALU.subtract, op1=ALU.mult)
                    ch.link(ins)
                    dve.wait_ge(s["rt_z"], n + 1)
                    V.tensor_tensor(out=kT[:, 0:W], in0=kT[:, 0:W], in1=zr[:].rearrange("p t n -> p (t n)")[:, 0:W], op=ALU.mult).then_inc(s["rt_n"], 1)
                if k == 7:
                    dve.wait_ge(s["rt_yT"], n + 1)
                    V.tensor_scalar(out=y_of[L][:, ds(8 + e, 1), :].rearrange("p a n -> p (a n)"), in0=aux[2][:, 0:W], scalar1=col(f"retn{L}", e),
                                    scalar2=None, op0=ALU.mult).then_inc(s["rt_y"], 1)
                    dve.wait_ge(s["rt_y"], n + 2)

            def split_step(n, hi, lo, src, W, k):
                dve.wait_ge(s["p_hi_ready"], 8 * n + k + 1)
                V.tensor_tensor(out=lo[:, 2 * k * W:2 * (k + 1) * W], in0=src(k), in1=hi[:, 2 * k * W:2 * (k + 1) * W].bitcast(F32), op=ALU.subtract).then_inc(s["p_lo_ready"], 1)

            def out_layer(L, e, par, k):
                T = tokens[L]
                if k == 0:
                    dve.wait_ge(eaten, chunk_end(f"out{L}", e))
                    for t in range(T):
                        gt = gates[:, t // 2, ds(512 * e, 512)]
                        ins = V.tensor_tensor(out=u[:, t, :], in0=main[(2 * par if L else 0) + t][:, :], in1=gt, op=ALU.mult)
                        if L == 0 and t < 3:
                            ins.then_inc(s["half_d"], 1)
                    ins.then_inc(free_d, 1)
                    dve.wait_ge(free_d, done_d[f"out{L}"] + e + 1)
                    dve.wait_ge(s["x_in"], 32)
                    for t in range(T):
                        xt = x3[:, t, ds(512 * e, 512)]
                        V.tensor_tensor(out=xt, in0=xt, in1=u[:, t, :], op=ALU.add).then_inc(s["out_x"], 1)
                    dve.wait_ge(s["out_x"], 16 * L + T * (e + 1))

            def front(name, e, par, k):
                n = e + (8 if name == "dil" else 0)
                if k == 0:
                    dve.wait_ge(eaten, chunk_end(name, e))
                    V.tensor_scalar(out=u2s[:, par, 1, :], in0=main[2 * par + 1][:, 0:384], scalar1=scale_h[:, 1:2], scalar2=None, op0=ALU.mult).then_inc(free_d, 1)
                if name == "sb":
                    neg = maskd[:, 0:512]
                    if k == 4:
                        dve.wait_ge(s["a_z"], e + 1)
                        dve.wait_ge(s["s_l"], e + 1)
                        ch.link(V.tensor_scalar(out=t2[:], in0=aux[1][:, :], scalar1=P ** -0.5, scalar2=0.0, op0=ALU.mult, op1=ALU.max))
                        ch.link(V.tensor_tensor(out=t2[:], in0=t2[:], in1=t1[:], op=ALU.add))
                        V.tensor_tensor(out=t4[:], in0=t2[:], in1=neg, op=ALU.mult).then_inc(s["s_lk"], 1)
                        dve.wait_ge(s["s_lk"], e + 1)
                        ch.link(V.scalar_tensor_tensor(out=t3[:], in0=aux[1][:, :], scalar=P ** -0.5, in1=t2[:], op0=ALU.mult, op1=ALU.subtract))
                else:
                    if k == 3:
                        dve.wait_ge(s["a_z"], 8 + e + 1)
                        bh = bias[:, ds(e, 1), :].rearrange("p a n -> p (a n)")
                        ch.link(V.scalar_tensor_tensor(out=t1[:, 0:256], in0=aux[1][:, 0:256], scalar=P ** -0.5, in1=bh, op0=ALU.mult, op1=ALU.add))
                        bh1 = bias[:, ds(e, 1), 128:256].rearrange("p a n -> p (a n)")
                        ch.link(V.scalar_tensor_tensor(out=t1[:, 256:384], in0=aux[1][:, 256:384], scalar=P ** -0.5, in1=bh1, op0=ALU.mult, op1=ALU.add))
                        ch.link(V.tensor_reduce(out=rmax[:, 0:1], in_=t1[:, 0:256], axis=AX.X, op=ALU.max, negate=True))
                        V.tensor_reduce(out=rmax[:, 1:2], in_=t1[:, 256:384], axis=AX.X, op=ALU.max, negate=True).then_inc(s["d_L"], 1)
                    if k == 6:
                        dve.wait_ge(s["d_pT"], e + 1)
                        V.tensor_copy(out=aT[:, 0:384], in_=aux[2][:, 0:384]).then_inc(s["a_aT"], 1)
                        dve.wait_ge(s["d_p"], e + 1)
                        V.reciprocal(out=rsums[:, par, :], in_=rsums[:, par, :]).then_inc(s["d_r"], 1)
                        dve.wait_ge(s["d_r"], e + 1)

            def back(name, e, par, k):
                n = e + (8 if name == "dil" else 0)
                if k == 0 and name == "sb":
                    dve.wait_ge(s["s_lat"], e + 1)
                    V.tensor_tensor(out=t3[:], in0=t3[:], in1=aux[2][:, :], op=ALU.add).then_inc(s["s_s"], 1)
                if k == 2 and name == "sb":
                    dve.wait_ge(s["s_e"], e + 1)
                    V.tensor_tensor(out=aT[:], in0=t3[:], in1=maskd[:, 512:1024], op=ALU.mult).then_inc(s["a_aT"], 1)
                if k == 5:
                    dve.wait_ge(s["a_sq"], n + 1)
                    ch.link(V.reciprocal(out=hr[:], in_=hroot[:]))
                    if name == "dil":
                        ch.link(V.tensor_tensor(out=hr[:], in0=hr[:], in1=rsums[:, par, :], op=ALU.mult))
                    for t in range(2):
                        ins = V.tensor_scalar(out=on[:, t, :], in0=aux[3][:, t * P:(t + 1) * P], scalar1=hr[:, t:t + 1], scalar2=None, op0=ALU.mult)
                    ins.then_inc(s["a_n"], 1)
                if k == 7:
                    dve.wait_ge(s["a_yT"], n + 1)
                    V.tensor_scalar(out=y_of[1][:, ds(n, 1), :].rearrange("p a n -> p (a n)"), in0=aux[0][:, 0:256], scalar1=col("head", n), scalar2=None,
                                    op0=ALU.mult).then_inc(s["a_y"], 1)
                    dve.wait_ge(s["a_y"], n + 2)

            def plain_out(name, row, e, par, k):
                if k == 0:
                    dve.wait_ge(free_a, done_a[name] + e + 1)
                    cs = ds(e * 512, 512)
                    for t in range(2):
                        ins = V.tensor_tensor(out=rr[:, t, cs], in0=main[2 * par + t][:, :], in1=row[:, cs], op=ALU.mult)
                    ins.then_inc(free_d, 1)

            def residual(kg):
                for t in range(2):
                    cs = slice(kg * 512, (kg + 1) * 512)
                    ins = V.scalar_tensor_tensor(out=x3[:, t, cs], in0=rr[:, t, cs], scalar=rstd[:, t:t + 1], in1=x3[:, t, cs], op0=ALU.mult, op1=ALU.add)
                return ins

            def ffn_up(e, par, k):
                if k == 0:
                    dve.wait_ge(free_a, done_a["ffn_up"] + e + 1)
                    for t in range(2):
                        ins = V.scalar_tensor_tensor(out=ff[:, t, :], in0=main[2 * par + t][:, 256:512], scalar=scale_h[:, t:t + 1], in1=fs[:, t, :], op0=ALU.mult, op1=ALU.mult)
                    ins.then_inc(free_d, 1)
                if k == 2:
                    dve.wait_ge(s["f_hi"], e + 1)
                    sl = ds(e * 512, 512)
                    V.tensor_tensor(out=f_lo[:, sl], in0=aux[0][:, :], in1=f_hi[:, sl].bitcast(F32), op=ALU.subtract).then_inc(s["f_lo"], 1)
                    dve.wait_ge(s["f_lo"], e + 2)

            def gate(e, par, k):
                if k == 0:
                    dve.wait_ge(free_a, done_a["gate"] + e + 1)
                    for t in range(2):
                        ch.link(V.tensor_tensor(out=sig[:, t, :], in0=sig[:, t, :], in1=aux[2 * par + t][:, :], op=ALU.mult))
                    for t in range(2):
                        xt = x3[:, t, ds(512 * e, 512)]
                        V.tensor_tensor(out=xt, in0=xt, in1=sig[:, t, :], op=ALU.add).then_inc(s["gt_x"], 1)
                    dve.wait_ge(s["gt_x"], 2 * e + 2)
                    dve.sem_inc(free_d, 1)

            for n in ("md_d", "side_T", "cv_done", "rt_y", "rt_sT", "a_y", "f_lo"):
                dve.sem_inc(s[n], 1)
            dve.sem_inc(free_d, 1)
            dve.sem_inc(s["side_used"], 3)
            for p in range(LEAD):
                split(p, p)
            dve.wait_ge(s["loads_c"], 32)
            cc = msb[:, 0:32].rearrange("p (k b) -> p k b", b=2)
            ch.link(V.tensor_copy(out=cc[:, :, 0], in_=colv("c", 16)))
            ch.link(V.tensor_copy(out=cc[:, :, 1], in_=colv("cctx", 16)))
            ch.link(V.memset(cvec[:, 2 * KT:2 * KT + P], 0.0))
            dve.sem_inc(s["cx"], 1)
            dve.wait_ge(s["csplit"], 1)
            V.tensor_tensor(out=c_lo[:], in0=cvec[:], in1=c_hi[:].bitcast(F32), op=ALU.subtract).then_inc(s["csplit"], 1)
            ch.link(V.memset(ssq[:], 0.0))
            dve.sem_inc(s["ssq0"], 1)
            dve.wait_ge(s["lgx"], 1)
            V.tensor_scalar(out=lg[:], in0=lg[:], scalar1=-1.0, scalar2=None, op0=ALU.mult).then_inc(s["lgd"], 1)

            norm = 0
            for L in range(2):
                T = tokens[L]
                if L == 0:
                    mL = lambda e, par, k: mod(L, e, par, k)
                    phase("mod0", nothing, mL)
                    dve.wait_ge(s["out_sq"], 4)
                    norm_sum(0, 4, rstd)
                    tail(mL, 7, 1)
                    dve.wait_ge(s["md_d"], 9)
                scale = modT[:, :, 16:32] if L == 0 else sideT[:, :, 32:48]
                for b in range(2):
                    ch.link(V.scalar_tensor_tensor(out=mod_a[:, b, :], in0=scale[:, b, :], scalar=1.0, in1=colv(f"norm{L}", 16), op0=ALU.add, op1=ALU.mult))
                dve.sem_inc(s["consts"], 1)
                if L == 1:
                    dve.wait_ge(s["out_sq"], 8)
                    norm_sum(1, 4, rstd)
                phase(f"in{L}_conv", lambda k: [layer_step(L, a_layer, b_layer, kg) for kg in norm_groups(k)],
                      lambda e, par, k: conv(L, e, par, k))

                def ret_start(k):
                    conv(L, 7, 1, k)
                    if k == 7:
                        conv_rstd(L)
                        dve.wait_ge(s["wide_in"], 16)

                phase(f"in{L}_ret", ret_start, lambda e, par, k: ret(L, e, k))
                Y, W = y_of[L], T * P

                def branch(k, L=L, Y=Y, W=W):
                    if k == 0:
                        dve.wait_ge(s["y_scaled"], 8 * L + 8)
                        if L == 0:
                            side_end(SIDE_CHUNKS - 1)
                            dve.wait_ge(s["side_T"], SIDE_CHUNKS + 1)
                    split_step(L, act_hi, act_lo, lambda k: Y[:, 2 * k:2 * k + 2, :].rearrange("p a n -> p (a n)"), W, k)

                phase(f"out{L}", lambda k: run_out_head(k, lambda j: ret(L, 7, j), branch, lambda b: gate_rows(L, b)),
                      lambda e, par, k: out_layer(L, e, par, k))
                out_layer(L, 3, 1, 0)
                norm += 1
            dve.wait_ge(s["gate_row"], 16)
            dve.wait_ge(s["out_sq"], 12)
            norm_sum(2, 2, rstd)
            ln = lambda name: (lambda b, kt: col(name, kt))

            def final_norm(kg):
                for t in range(2):
                    cs = slice(kg * 512, (kg + 1) * 512)
                    ins = V.scalar_tensor_tensor(out=x3[:, t, cs], in0=x3[:, t, cs], scalar=rstd[:, t:t + 1], in1=gates[:, 1, cs], op0=ALU.mult, op1=ALU.mult)
                return ins

            def sb_start(k):
                prepare(3, ln("mixpre"), final_norm, k)
                if k == 1:
                    dve.wait_ge(s["bT2"], 1)
                    V.tensor_tensor(out=ext[:], in0=aux[0][0:HEADS, 0:384], in1=dadd[:], op=ALU.add).then_inc(s["bT3"], 1)
                if k == 7:
                    for j in range(4):
                        dve.wait_ge(s["bT2"], j + 2)
                        V.tensor_copy(out=bias[:, 2 * j:2 * j + 2, :].rearrange("p h n -> p (h n)"), in_=aux[j][:, :]).then_inc(s["bT3"], 1)

            phase("sb", sb_start, lambda e, par, k: head_steps(front, back, "sb", e, par, k))
            phase("dil", lambda k: head_steps(front, back, "sb", 7, 1, k), lambda e, par, k: head_steps(front, back, "dil", e, par, k))
            O = y_of[1]
            dve.wait_ge(s["mix_in"], 16)
            heads = lambda k: split_step(2, h_hi, h_lo, lambda k: O[:, 2 * k:2 * k + 2, :].rearrange("p a n -> p (a n)"), 256, k)
            phase("out2", lambda k: last_head(front, back, heads, k),
                  lambda e, par, k: plain_out("out2", mixrow, e, par, k))
            plain_out("out2", mixrow, 3, 1, 0)
            norm_sum(4, 2, rstd)
            dve.wait_ge(free_d, done_d["ffn_up"])
            phase("ffn_up", lambda k: prepare(5, ln("ffnpre"), residual, k), ffn_up)

            def down_step(e, par, k):
                if e == 0 and k == 0:
                    dve.wait_ge(s["fr_in"], 16)
                plain_out("ffn_down", frow, e, par, k)

            phase("ffn_down", lambda k: ffn_up(21, 1, k), down_step)
            down_step(3, 1, 0)
            norm_sum(6, 2, rstd)
            dve.wait_ge(free_d, done_d["gate"])

            def gate_start(k):
                prepare(7, ln("pli"), residual, k)
                if k == 5:
                    dve.wait_ge(s["px_h"], 1)
                    V.tensor_tensor(out=p_lo[:], in0=ptok[:], in1=p_hi[:].bitcast(F32), op=ALU.subtract).then_inc(s["p_ready"], 1)

            phase("gate", gate_start, gate, last=True)
            gate(3, 1, 0)

        @block.tensor
        def _(pe):
            ch = Chain(pe, s["act_chain"])
            mm = nc.tensor.matmul
            tr = lambda o, i: nc.tensor.transpose(o, i, mat("ident"))

            def piece(name, c, cs, k, parts, tw):
                chunks, per, w = SHAPE[name]
                slot = (BASE[name] + (c if isinstance(c, int) else cs) * per + k) % SLOTS
                n = w // 2
                by_bank = name in bank_by_bank and not paired[name] and not (isinstance(c, int) and c == 0)
                if k == 0 and not by_bank:
                    back = 1 if paired[name] and not (isinstance(c, int) and c == 0) else 0
                    pe.wait_ge(free_d, done_d[name] + c - back)
                    pe.wait_ge(free_a, (done_a[name] + c - back) if name in by_act else done_a[name])
                pe.wait_ge(lo_split, BASE[name] + c * per + k + 1)
                if name == "gate" and k == 8:
                    for t in range(2):
                        for j in range(2):
                            cs = slice(j * 256 + t * P, j * 256 + (t + 1) * P)
                            for i, (x, w_part) in enumerate(((p_hi, w_hi), (p_hi, w_lo), (p_lo, w_hi))):
                                ins = mm(aux[2 * (c % 2) + t][:, :], x[:, cs], w_part[:, slot, j * n:(j + 1) * n],
                                         start=(j == 0 and i == 0), stop=(j == 1 and i == 2))
                    ins.then_inc(eaten, 1)
                    return
                for t, (bank, c0, c1, stat) in enumerate(parts):
                    if k == 0 and by_bank:
                        a0, d0 = bank_by_bank[name]
                        if name == "out0":
                            pe.wait_ge(s["half_d"] if t < 3 else free_d, d0 + 3 * c - 2 + t if t < 3 else done_d[name] + c)
                        elif t % 2 == 0:
                            pe.wait_ge(s["half_a"] if t == 0 else free_a, a0 + c if t == 0 else done_a[name] + c)
                        else:
                            pe.wait_ge(s["half_d"] if t == 1 else free_d, d0 + c if t == 1 else done_d[name] + c)
                    if isinstance(stat, int):
                        for j in range(2):
                            kt, w0 = 2 * k + j, j * n + c0
                            for i, (x, w_part) in enumerate(((act_hi, w_hi), (act_hi, w_lo), (act_lo, w_hi))):
                                ins = mm(bank[:, stat:stat + c1], w_part[:, slot, w0:w0 + P], x[:, kt * 512:kt * 512 + c1],
                                         start=(k == 0 and j == 0 and i == 0 and stat == 0),
                                         stop=(k == per - 1 and j == 1 and i == 2 and (stat > 0 or c1 == 512)))
                        continue
                    for j in range(2):
                        hi, lo = stat(2 * k + j)
                        for i, (x, w_part) in enumerate(((hi, w_hi), (hi, w_lo), (lo, w_hi))):
                            ins = mm(bank[:, c0:c1], x, w_part[:, slot, j * n + c0:j * n + c1],
                                     start=(k == 0 and j == 0 and i == 0), stop=(k == (7 if name == "gate" else per - 1) and j == 1 and i == 2))
                ins.then_inc(eaten, 1)

            def phase(name, head, epi, parts, tw=512, last=False, ready=None):
                chunks, per, w = SHAPE[name]

                def body(c, cs, step):
                    for k in range(per):
                        if k == 0 and name == "in0_conv" and cs > 0:
                            side_total(c - 1)
                        if k == 0 and name == "in0_ret":
                            side_total(c + 7)
                        if k == 1 and (name == "in0_ret" or name == "in0_conv" and cs > 0):
                            pe.wait_ge(s["side_T"], side_first[name] // 8 + c + 1)
                        step(k)
                        if ready and isinstance(c, int) and c == 0:
                            ready(k)
                        piece(name, c, cs, k, parts(cs if paired[name] else 0), tw)

                body(0, 0, head)
                if epi and last:
                    for c in range(1, chunks):
                        body(c, c % 2, lambda k: epi(c - 1, (c - 1) % 2, k))
                elif epi:
                    over_chunks(pe, ch, "pe_" + name, chunks, paired[name],
                                lambda c, par: body(c, par, lambda k: epi(c - 1, 1 - par, k)), lag=2 if name in ("sb", "dil") else 1)
                else:
                    for c in range(1, chunks):
                        body(c, c % 2, lambda k: None)

            nothing = lambda k: None

            def tail(epi, e, par, per=8):
                for k in range(per):
                    epi(e, par, k)

            def rows(hi, lo, T, blocks):
                def make(t):
                    return lambda kt: tuple(x[:, kt * T * P + t * P:kt * T * P + (t + 1) * P] for x in (hi, lo))
                return [(bank, c0, c1, make(t)) for t, bank, c0, c1 in blocks]

            mod_parts = lambda par: [(main[2 * par], 0, 512, lambda kt: (c_hi[:, 2 * kt:2 * kt + P], c_lo[:, 2 * kt:2 * kt + P]))]

            def mod(L, e, par, k):
                if k == 1:
                    pe.wait_ge(free_d, done_d["mod0"] + e + 1)
                    pe.wait_ge(s["md_d"], 8 * L + e + 1)
                    pe.sem_inc(s["msb_read"], 1)
                    for kk in range(4):
                        ins = nc.tensor.transpose(aux[0][:, 2 * kk:2 * kk + 2], msb[0:2, kk * P:(kk + 1) * P], mats[0:2, 0:2])
                    ins.then_inc(s["md_T"], 1)

            def gate_rows(L, b):
                if b < 2 - L:
                    if b == 0:
                        pe.wait_ge(s["rt_y"], 8 * L + 9)
                        pe.wait_ge(s["side_T"], SIDE_CHUNKS + 1)
                    if b + L > 0:
                        pe.wait_ge(s["mg_d"], 1 + L)
                    for j in range(KT):
                        ins = mm(aux[j // 4][:, (j % 4) * P:(j % 4 + 1) * P], sideT[:, b, 48 * L + j:48 * L + j + 1].to_broadcast([P, P]), mat("ident"), start=True, stop=True)
                    ins.then_inc(s["mg_s"], 1)

            def side_total(chunk):
                pe.wait_ge(s["side_used"], 8 * chunk + 11)
                for v in range(2):
                    for j in range(4):
                        ins = tr(aux[2 + v][:, j * P:(j + 1) * P], side_acc[:, v, j * P:(j + 1) * P])
                ins.then_inc(s["side_sum"], 1)

            def stay_warm(bank, n):
                for _ in range(n):
                    mm(bank[:, 0:P], mat("ident"), mat("ones"), start=True, stop=True)

            def norm_T(n, T, xs, kg):
                m = 4 * prep_index(n) + kg
                if T == 4:
                    pe.wait_ge(s["xs_a"], m + 1)
                    pe.wait_ge(s["xs_d"], m + 1)
                    if m > 0:
                        pe.wait_ge(s["tmp_a"], m)
                        pe.wait_ge(s["tmp_d"], m)
                else:
                    pe.wait_ge(s["x_grp"], m - 7)
                    pe.wait_ge(s["h_ready"], m - 1 if kg > 0 else m)
                for kk in range(4):
                    bank, c0 = norm_bank(T, kg, kk)
                    for t in range(T):
                        src = xs[t][:, kk * P:(kk + 1) * P] if T == 4 else x3[:, t, (4 * kg + kk) * P:(4 * kg + kk + 1) * P]
                        ins = tr(bank[:, c0 + t * P:c0 + (t + 1) * P], src)
                ins.then_inc(s["xT_ready"], 1)

            def norm_head(n, T, xs, before, warm):
                def step(k):
                    for kg in norm_groups(k):
                        if kg == 0:
                            if T == 2:
                                pe.wait_ge(free_a, done_a[before] - (1 if before in ("ffn_up", "gate") else 0))
                                pe.wait_ge(free_d, done_d[before] - 1)
                            stay_warm(main[0] if T == 2 else aux[3], warm[0])
                        norm_T(n, T, xs, kg)
                    if k == 0:
                        if T == 4:
                            pe.wait_ge(free_d, done_d[before])
                        stay_warm(main[0], warm[1])
                    if k % 2 == 0:
                        pe.wait_ge(s["h_ready"], 4 * prep_index(n) + k // 2 + 1)
                return step

            def ret(L, e, k):
                T = tokens[L]
                n = 8 * L + e
                tok = (2, 3, 0, 1)
                if k == 1:
                    pe.wait_ge(free_a, done_a[f"in{L}_ret"] + e + 1)
                    pe.wait_ge(s["rt_rope"], n + 1)
                    for t in range(T):
                        tr(aux[0][:, t * P:(t + 1) * P], qk[:, t, 0:P] if t < 2 else u[:, t, 0:P])
                    for t in range(4):
                        ins = tr(aux[1][:, t * P:(t + 1) * P], qk[:, t, P:2 * P] if t < 2 else u[:, t, P:2 * P])
                    ins.then_inc(s["rt_T"], 1)
                if k == 3:
                    pe.wait_ge(s["rt_qa"], n + 1)
                    pe.wait_ge(s["rt_kd"], n + 1)
                    for b in range(4):
                        ins = mm(aux[2 + b // 2][:, (b % 2) * 256:(b % 2 + 1) * 256], kT[:, tok[b] * P:(tok[b] + 1) * P], qT[:, 0:256], start=True, stop=True)
                    if L == 0:
                        for b in range(2):
                            ins = mm(aux[0][:, b * 256:(b + 1) * 256], kT[:, tok[b] * P:(tok[b] + 1) * P], qT[:, 256:512], start=True, stop=True)
                    ins.then_inc(s["rt_s"], 1)
                if k == 5:
                    pe.wait_ge(s["rt_sT"], n + 2)
                    for t in range(2):
                        for b in range(4):
                            ins = mm(aux[1][:, t * P:(t + 1) * P], sT[:, b, t * P:(t + 1) * P], u[:, tok[b], 256:384], start=(b == 0), stop=(b == 3))
                    for t in range(2, T):
                        for b in range(2):
                            ins = mm(aux[1][:, t * P:(t + 1) * P], sTc[:, b, (t - 2) * P:(t - 1) * P], u[:, tok[b], 256:384], start=(b == 0), stop=(b == 1))
                    ins.then_inc(s["rt_o"], 1)
                if k == 7:
                    pe.wait_ge(s["rt_n"], n + 1)
                    for t in range(T):
                        ins = tr(aux[2][:, t * P:(t + 1) * P], kT[:, t * P:(t + 1) * P])
                    ins.then_inc(s["rt_yT"], 1)

            def front(name, e, par, k):
                n = e + (8 if name == "dil" else 0)
                if k == 1:
                    pe.wait_ge(free_a, done_a[name] + e + 1)
                    pe.wait_ge(free_d, done_d[name] + e + 1)
                    if not (isinstance(n, int) and n == 0):
                        pe.wait_ge(s["a_y"], n)
                    for i in range(2):
                        for t in range(2):
                            ins = tr(aux[0][:, (2 * i + t) * P:(2 * i + t + 1) * P], u2s[:, par, t, i * P:(i + 1) * P])
                    ins.then_inc(s["a_T"], 1)
                q, kk = qkT[:, 0:256], qkT[:, 256:512]
                if k == 2:
                    pe.wait_ge(s["a_qk"], n + 1)
                    if name == "sb":
                        for b in range(2):
                            ins = mm(aux[1][:, b * 256:(b + 1) * 256], kk[:, b * P:(b + 1) * P], q, start=True, stop=True)
                    else:
                        mm(aux[1][:, 0:256], q[:, P:2 * P], kk, start=True, stop=True)
                        ins = mm(aux[1][:, 256:384], q[:, 0:P], kk[:, 0:P], start=True, stop=True)
                    ins.then_inc(s["a_z"], 1)
                if k == 7 and name == "sb":
                    pe.wait_ge(s["s_lk"], e + 1)
                    mm(aux[2][:, 0:256], amat("later"), t4[:, 0:256], start=True, stop=False)
                    mm(aux[2][:, 0:256], mat("ones"), t4[:, 256:512], start=False, stop=True)
                    mm(aux[2][:, 256:512], amat("later"), t4[:, 256:512], start=True, stop=True).then_inc(s["s_lat"], 1)
                if k == 6 and name == "dil":
                    pe.wait_ge(s["d_p"], e + 1)
                    for b in range(3):
                        ins = tr(aux[2][:, b * P:(b + 1) * P], t2[:, b * P:(b + 1) * P])
                    ins.then_inc(s["d_pT"], 1)

            def back(name, e, par, k):
                n = e + (8 if name == "dil" else 0)
                if k == 3:
                    pe.wait_ge(s["a_aT"], n + 1)
                    of = {"sb": {0: [(0, 0)], 1: [(0, P), (1, 3 * P)]}, "dil": {0: [(0, 2 * P)], 1: [(0, 0), (1, P)]}}[name]
                    for t in range(2):
                        for i, (b, c0) in enumerate(of[t]):
                            ins = mm(aux[3][:, t * P:(t + 1) * P], aT[:, c0:c0 + P], u2s[:, par, b, 256:384], start=(i == 0), stop=(i == len(of[t]) - 1))
                    ins.then_inc(s["a_o"], 1)
                if k == 7:
                    pe.wait_ge(s["a_n"], n + 1)
                    for t in range(2):
                        ins = tr(aux[0][:, t * P:(t + 1) * P], on[:, t, :])
                    ins.then_inc(s["a_yT"], 1)

            def ffn_up(e, par, k):
                if k == 1:
                    pe.wait_ge(free_d, done_d["ffn_up"] + e + 1)
                    pe.wait_ge(s["f_lo"], e + 1)
                    for j in range(2):
                        for t in range(2):
                            ins = tr(aux[0][:, (2 * j + t) * P:(2 * j + t + 1) * P], ff[:, t, j * P:(j + 1) * P])
                    ins.then_inc(s["f_T"], 1)

            pe.sem_inc(s["f_T"], 1)
            pe.sem_inc(s["side_sum"], 1)
            pe.wait_ge(s["loads_c"], 32)
            pe.wait_ge(s["csplit"], 2)
            for L in range(2):
                T = tokens[L]
                if L == 1:
                    pe.wait_ge(s["mg_d"], 2)
                if L == 0:
                    phase("mod0", nothing, lambda e, par, k: mod(0, e, par, k), mod_parts)
                    tail(lambda e, par, k: mod(0, e, par, k), 7, 1)
                conv_parts = rows(act_hi, act_lo, 4, [(t, main[t], 0, 512) for t in range(T)])
                ret_parts = conv_parts + rows(act_hi, act_lo, 4, [(t, main[t], 128, 384) for t in range(T, 4)])
                W = T * P
                channels = lambda par: [(conv_bank(L, par, i)[0], sec * P, W, conv_bank(L, par, i)[1]) for i, sec in enumerate((2, 1, 3, 0))]
                phase(f"in{L}_conv", norm_head(L, 4, xs4, f"in{L}_conv", ((0, 26)[L], (0, 8)[L])), lambda e, par, k: None, channels)

                def ret_start(k):
                    if k == 7:
                        pe.wait_ge(s["cv_q"], 9 * L + 9)
                        pe.wait_ge(s["cv_done"], 8 * L + 9)
                        mm(aux[0][:, 0:T * P], mat("ones"), acc[:, 0:T * P], start=True, stop=True).then_inc(s["cf_s"], 1)

                def ret_step(e, par, k):
                    if k == 1:
                        pe.wait_ge(s["cf_r"], L + 1)
                    ret(L, e, k)

                phase(f"in{L}_ret", ret_start, ret_step, lambda par: ret_parts)
                out_parts = (lambda par: rows(act_hi, act_lo, 4, [(t, main[t], 0, 512) for t in range(4)])) if L == 0 else \
                    (lambda par: rows(act_hi, act_lo, 2, [(t, main[2 * par + t], 0, 512) for t in range(2)]))

                def branch(j):
                    if j == 0:
                        stay_warm(aux[0], (8, 14)[L])
                    if L == 0 and j == 0:
                        side_total(SIDE_CHUNKS - 1)
                    if L == 0 and j == 1:
                        pe.wait_ge(s["side_T"], SIDE_CHUNKS + 1)

                def split_ready(k):
                    if k == 0:
                        pe.wait_ge(free_a, done_a[f"out{L}"])
                        pe.wait_ge(free_d, done_d[f"out{L}"])
                        stay_warm(main[0], (4, 16)[L])
                    pe.wait_ge(s["p_lo_ready"], 8 * L + k + 1)

                phase(f"out{L}", lambda k: run_out_head(k, lambda j: ret(L, 7, j), branch, lambda b: gate_rows(L, b)), lambda e, par, k: None, out_parts, ready=split_ready)
            pe.wait_ge(s["mg_d"], 3)
            two = lambda hi, lo: (lambda par: rows(hi, lo, 2, [(t, main[2 * par + t], 0, 512) for t in range(2)]))
            attn_parts = lambda par: rows(h_hi, h_lo, 2, [(t, main[2 * par + t], 0, 384) for t in range(2)])
            sb_norm = norm_head(3, 2, None, "sb", (26, 10))

            def sb_start(k):
                if k == 2:
                    pe.wait_ge(s["bT3"], 1)
                sb_norm(k)
                if k == 1:
                    pe.wait_ge(s["bT"], 48)
                    mm(aux[0][0:HEADS, 0:384], relb[:], onehot[:], start=True, stop=True).then_inc(s["bT2"], 1)
                if k == 7:
                    pe.wait_ge(s["mask_in"], 16)
                    pe.wait_ge(s["bT5"], 16)
                    for j in range(4):
                        mm(aux[j][:, :], amat("flip"), hankel[:, 2 * j:2 * j + 2, :].rearrange("p h n -> p (h n)"), start=True, stop=True).then_inc(s["bT2"], 1)

            def sb_step(e, par, k):
                if k == 1:
                    pe.wait_ge(s["bT3"], 5)
                head_steps(front, back, "sb", e, par, k)

            phase("sb", sb_start, sb_step, attn_parts)
            phase("dil", lambda k: head_steps(front, back, "sb", 7, 1, k), lambda e, par, k: head_steps(front, back, "dil", e, par, k), attn_parts)
            def out2_split(j):
                if j == 0:
                    pe.wait_ge(free_a, done_a["out2"] - 1)
                    pe.wait_ge(free_d, done_d["out2"] - 1)
                    stay_warm(main[0], 14)

            phase("out2", lambda k: last_head(front, back, out2_split, k), lambda e, par, k: None, two(h_hi, h_lo), ready=lambda k: pe.wait_ge(s["p_lo_ready"], 16 + k + 1))
            phase("ffn_up", norm_head(5, 2, None, "ffn_up", (18, 6)), ffn_up, two(h_hi, h_lo))

            def down_ready(k):
                if k == 21:
                    pe.wait_ge(s["f_lo"], 23)
                elif k == 0:
                    pe.wait_ge(s["f_lo"], 22)

            phase("ffn_down", lambda k: ffn_up(21, 1, k), lambda e, par, k: None, two(f_hi, f_lo), ready=down_ready)
            gate_norm = norm_head(7, 2, None, "gate", (18, 6))

            def gate_start(k):
                if k < 8:
                    gate_norm(k)
                else:
                    pe.wait_ge(s["p_ready"], 1)

            phase("gate", gate_start, lambda e, par, k: None, two(h_hi, h_lo), last=True)


def kernel(**inputs):
    import concourse.bacc as bacc
    from concourse.bass_utils import run_bass_kernel_spmd

    x = {k: np.asarray(v) for k, v in inputs.items()}

    def pieces(w, groups):
        k, n = w.shape
        parts = w.reshape(k // 256, 2, P, n)
        return np.stack([parts[..., g].transpose(0, 2, 1, 3).reshape(k // 256, P, -1) for g in groups]) \
                 .reshape(-1, P, 2 * len(groups[0]))

    span = lambda a, n: np.arange(a, a + n)
    plain = lambda first, n: [span(first + 512 * c, 512) for c in range(n)]
    arrays = {}
    arrays["w_mod0"] = pieces(x["w_mod"][0], plain(0, 8))
    arrays["w_side"] = np.concatenate([pieces(x["w_mod"][0], plain(4096, 4)), pieces(x["w_mod"][1], plain(0, 12))])
    for L in range(2):
        w = x["w_in"][L]
        for half, name in ((0, "conv"), (4 * HALF, "ret")):
            arrays[f"w_in{L}_{name}"] = pieces(w, [np.concatenate([span(half + i * HALF + h * P, P) for i in range(4)]) for h in range(8)])
        arrays[f"w_out{L}"] = pieces(x["w_out"][L], plain(0, 4))
    w = x["w_in_2"][0]
    for half, name in ((0, "sb"), (3 * HALF, "dil")):
        arrays[f"w_{name}"] = pieces(w, [np.concatenate([span(half + i * HALF + h * P, P) for i in range(3)]) for h in range(8)])
    arrays["w_out2"] = pieces(x["w_out_2"][0], plain(0, 4))
    arrays["w_ffn_up"] = pieces(x["w_gate_up_2"][0], [np.concatenate([span(256 * c, 256), span(FF + 256 * c, 256)]) for c in range(22)])
    arrays["w_ffn_down"] = pieces(x["w_down_2"][0], plain(0, 4))
    arrays["w_gate"] = np.concatenate([pieces(x[n][0], plain(0, 4)).reshape(4, -1, P, 1024) for n in ("w_pli_gate_2", "w_pli_proj_2")], 1) \
                         .reshape(-1, P, 1024)
    column = lambda v: v.reshape(-1, P).T
    vec = []
    for name in COLS:
        L = int(name[-1]) if name[-1] in "01" else 0
        vec.append({
            "norm": lambda: column(x["norm_w"][L]), "bmod": lambda: column(x["b_mod"][0][:4096]),
            "bside": lambda: column(np.concatenate([x["b_mod"][0][4096:], x["b_mod"][1]])),
            "convw": lambda: column(x["conv_w"][L].reshape(-1)), "convn": lambda: column(x["conv_norm_w"][L]),
            "retn": lambda: column(x["ret_norm_w"][L]), "mixpre": lambda: column(x["ln_mix_pre_2"][0]),
            "head": lambda: column(x["ln_head_2"][0]), "ffnpre": lambda: column(x["ln_ffn_pre_2"][0]),
            "pli": lambda: column(x["ln_pli_2"][0]), "c": lambda: column(x["c"][0]), "cctx": lambda: column(x["c_ctx"]),
            "eps": lambda: np.full((P, 1), EPS, np.float32),
        }[name.rstrip("01")]())
    arrays["cols"] = np.concatenate(vec, 1)
    arrays["rows"] = np.stack([x["final_norm_w"], x["ln_mix_post_2"][0], x["ln_ffn_post_2"][0]])
    arrays["decays"] = np.stack([x["ret_decay_f"], x["ret_decay_b"]], 1).reshape(32)
    arrays["x"], arrays["ctx"] = x["x"][0], x["ctx"][0]
    arrays["pT"] = x["p_2"][0, 0].T.reshape(2, P, TOK).transpose(1, 0, 2).reshape(P, 2 * TOK)
    arrays["rel_bias"] = x["rel_bias_2"]
    for name, v in zip(("mats", "wide", "maskd", "onehot", "dadd"), shape_constants()):
        arrays[name] = v
    nc = bacc.Bacc("TRN2", target_bir_lowering=False, num_devices=1)
    send, aps = {}, {}
    for name, v in arrays.items():
        send["in_" + name] = np.ascontiguousarray(v)
        aps[name] = nc.dram_tensor("in_" + name, v.shape, mybir.dt.float32, kind="ExternalInput").ap()
    out = nc.dram_tensor("out", (TOK, D), mybir.dt.float32, kind="ExternalOutput").ap()
    build(nc, aps, out)
    r = run_bass_kernel_spmd(nc, [send], core_ids=[0])
    return r.results[0]["out"].reshape(1, TOK, D)
```
